# Optimizing a Trainium2 kernel written in Bass

```python
import math
import jax, jax.numpy as jnp
from jax import lax
import numpy as np

D_MODEL = 1024
BATCH = 1
SEQ = 256
DEPTH = 1

GDN_HEADS = 4
GDN_HEAD_DIM = 128
GDN_WIDTH = GDN_HEADS * GDN_HEAD_DIM
CONV_WIDTH = 4
CHUNK = 64
SWA_HEADS = 8
SWA_HEAD_DIM = 64
SWA_WIDTH = SWA_HEADS * SWA_HEAD_DIM
DILATED_CONFIGS = ((128, 1), (512, 4), (2048, 16))
BAND_BLOCK = 128
MIX_WIDTH = GDN_WIDTH + SWA_WIDTH
IN_SIZES = (3 * GDN_WIDTH, GDN_WIDTH, GDN_HEADS, GDN_HEADS, SWA_WIDTH, SWA_WIDTH, SWA_WIDTH)
IN_COLS = sum(IN_SIZES)
IN_SPLITS = tuple(int(c) for c in np.cumsum(IN_SIZES)[:-1])
D_FF = 2816
FFN_CONV_WIDTH = 3
RMS_EPS = 1e-6
L2_EPS = 1e-6


def rmsnorm(x, gain):
    xf = x.astype(jnp.float32)
    y = xf * lax.rsqrt(jnp.mean(xf * xf, axis=-1, keepdims=True) + RMS_EPS)
    return (y * gain.astype(jnp.float32)).astype(x.dtype)

def l2norm(x):
    xf = x.astype(jnp.float32)
    return xf * lax.rsqrt(jnp.sum(xf * xf, axis=-1, keepdims=True) + L2_EPS)

def causal_dwconv(x, w):
    k_width = w.shape[0]
    s = x.shape[1]
    xp = jnp.pad(x, ((0, 0), (k_width - 1, 0), (0, 0)))
    return sum(xp[:, j:j + s] * w[j] for j in range(k_width))

def alibi_slopes(n_heads):
    return jnp.asarray(2.0 ** (-8.0 * np.arange(1, n_heads + 1) / n_heads), dtype=jnp.float32)

def chunk_gated_delta_rule(q, k, v, g, beta):
    bn, h, s, dk = q.shape
    dv = v.shape[-1]
    n = s // CHUNK
    q = q * dk ** -0.5
    q = q.reshape(bn, h, n, CHUNK, dk)
    k = k.reshape(bn, h, n, CHUNK, dk)
    v = v.reshape(bn, h, n, CHUNK, dv)
    beta = beta.reshape(bn, h, n, CHUNK, 1)
    g = jnp.cumsum(g.reshape(bn, h, n, CHUNK), axis=-1)
    idx = jnp.arange(CHUNK)
    causal = idx[:, None] >= idx[None, :]
    strict = idx[:, None] > idx[None, :]
    decay = jnp.exp(jnp.where(causal, g[..., :, None] - g[..., None, :], -jnp.inf))
    k_beta = k * beta
    a = jnp.where(strict, jnp.einsum('bhnik,bhnjk->bhnij', k_beta, k) * decay, 0.0)
    rhs = jnp.concatenate([v * beta, k_beta * jnp.exp(g)[..., None]], axis=-1)
    sol = lax.linalg.triangular_solve(a, rhs, left_side=True, lower=True, unit_diagonal=True)
    u, w = sol[..., :dv], sol[..., dv:]
    a_qk = jnp.where(causal, jnp.einsum('bhnik,bhnjk->bhnij', q, k) * decay, 0.0)
    q_dec = q * jnp.exp(g)[..., None]
    g_last = g[..., -1:]
    k_dec = k * jnp.exp(g_last - g)[..., None]
    decay_last = jnp.exp(g_last[..., 0])

    def step(state, inp):
        qd, wc, uc, kd, aqk, dl = inp
        v_new = uc - jnp.einsum('bhik,bhkv->bhiv', wc, state)
        o = jnp.einsum('bhik,bhkv->bhiv', qd, state) + jnp.einsum('bhij,bhjv->bhiv', aqk, v_new)
        state = state * dl[..., None, None] + jnp.einsum('bhik,bhiv->bhkv', kd, v_new)
        return state, o

    xs = tuple(jnp.moveaxis(t, 2, 0) for t in (q_dec, w, u, k_dec, a_qk, decay_last))
    state0 = jnp.zeros((bn, h, dk, dv), jnp.float32)
    _, o = lax.scan(step, state0, xs)
    return jnp.moveaxis(o, 0, 2).reshape(bn, h, s, dv)

def gated_deltanet(qkv, z, b_logit, a_logit, conv_w, a_log, dt_bias, norm_gain):
    bn, s, _ = qkv.shape
    out_dtype = z.dtype
    qkv = jax.nn.silu(causal_dwconv(qkv, conv_w))
    q, k, v = jnp.split(qkv, 3, axis=-1)
    heads = lambda t: t.reshape(bn, s, GDN_HEADS, GDN_HEAD_DIM).transpose(0, 2, 1, 3)
    q = l2norm(heads(q))
    k = l2norm(heads(k))
    v = heads(v).astype(jnp.float32)
    beta = jax.nn.sigmoid(b_logit.astype(jnp.float32)).transpose(0, 2, 1)
    g = (-jnp.exp(a_log.astype(jnp.float32))
         * jax.nn.softplus(a_logit.astype(jnp.float32) + dt_bias.astype(jnp.float32))).transpose(0, 2, 1)
    o = chunk_gated_delta_rule(q, k, v, g, beta).transpose(0, 2, 1, 3)
    zf = z.reshape(bn, s, GDN_HEADS, GDN_HEAD_DIM).astype(jnp.float32)
    y = (o * lax.rsqrt(jnp.mean(o * o, axis=-1, keepdims=True) + RMS_EPS)
         * norm_gain.astype(jnp.float32) * jax.nn.silu(zf))
    return y.reshape(bn, s, GDN_WIDTH).astype(out_dtype)

def banded_causal_attention(q, k, v, n_back, step, slopes):
    nb, h, l, dh = q.shape
    nblk = -(-l // BAND_BLOCK)
    lp = nblk * BAND_BLOCK
    qb = jnp.pad(q, ((0, 0), (0, 0), (0, lp - l), (0, 0))).reshape(nb, h, nblk, BAND_BLOCK, dh)

    def band(t):
        tp = jnp.pad(t, ((0, 0), (0, 0), (BAND_BLOCK, lp - l), (0, 0)))
        prev = tp[:, :, :lp].reshape(nb, h, nblk, BAND_BLOCK, dh)
        cur = tp[:, :, BAND_BLOCK:].reshape(nb, h, nblk, BAND_BLOCK, dh)
        return jnp.concatenate([prev, cur], axis=3)

    kb, vb = band(k), band(v)
    s = jnp.einsum('nhbqd,nhbkd->nhbqk', qb, kb).astype(jnp.float32) * dh ** -0.5
    qi = jnp.arange(BAND_BLOCK)[:, None]
    kj = jnp.arange(2 * BAND_BLOCK)[None, :]
    dist = qi + BAND_BLOCK - kj
    key_pos = (jnp.arange(nblk) * BAND_BLOCK - BAND_BLOCK)[:, None, None] + kj
    valid = (dist >= 0) & (dist <= n_back) & (key_pos >= 0)
    alibi = -slopes[:, None, None, None] * (dist * step).astype(jnp.float32)
    s = jnp.where(valid, s + alibi, -jnp.inf)
    m = jnp.max(s, axis=-1, keepdims=True)
    p = jnp.exp(s - m)
    den = jnp.sum(p, axis=-1, keepdims=True)
    o = jnp.einsum('nhbqk,nhbkd->nhbqd', p, vb.astype(jnp.float32)) / den
    lse = (m + jnp.log(den))[..., 0]
    return o.reshape(nb, h, lp, dh)[:, :, :l], lse.reshape(nb, h, lp)[:, :, :l]

def dilated_attention(q, k, v, slopes):
    bn, s, h, dh = q.shape
    outs, lses = [], []
    for window, dilation in DILATED_CONFIGS:
        l = s // dilation
        sub = lambda t: t.reshape(bn, l, dilation, h, dh).transpose(0, 2, 3, 1, 4).reshape(bn * dilation, h, l, dh)
        o, lse = banded_causal_attention(sub(q), sub(k), sub(v), window // dilation, dilation, slopes)
        outs.append(o.reshape(bn, dilation, h, l, dh).transpose(0, 3, 1, 2, 4).reshape(bn, s, h, dh))
        lses.append(lse.reshape(bn, dilation, h, l).transpose(0, 3, 1, 2).reshape(bn, s, h))
    weights = jax.nn.softmax(jnp.stack(lses), axis=0)
    return jnp.einsum('gbsh,gbshd->bshd', weights, jnp.stack(outs))

def first_inputs(seed: int = 0) -> dict:
    key = jax.random.key(seed)
    ks = jax.random.split(key, 16)
    nrm = lambda kk, shape, fan_in: jax.random.normal(kk, shape, jnp.float32) * fan_in ** -0.5
    x = jax.random.normal(ks[0], (BATCH, SEQ, D_MODEL), jnp.float32)
    ln1 = 1.0 + 0.02 * jax.random.normal(ks[1], (DEPTH, D_MODEL), jnp.float32)
    w_in = nrm(ks[2], (DEPTH, D_MODEL, IN_COLS), D_MODEL)
    conv_qkv = nrm(ks[3], (DEPTH, CONV_WIDTH, 3 * GDN_WIDTH), CONV_WIDTH)
    a_log = jnp.log(jax.random.uniform(ks[4], (DEPTH, GDN_HEADS), jnp.float32, minval=1.0, maxval=16.0))
    dt = jnp.exp(jax.random.uniform(ks[5], (DEPTH, GDN_HEADS), jnp.float32,
                                    minval=math.log(1e-3), maxval=math.log(1e-1)))
    dt_bias = jnp.log(jnp.expm1(dt))
    gdn_norm = 1.0 + 0.02 * jax.random.normal(ks[6], (DEPTH, GDN_HEAD_DIM), jnp.float32)
    w_out = nrm(ks[7], (DEPTH, MIX_WIDTH, D_MODEL), MIX_WIDTH)
    ln2 = 1.0 + 0.02 * jax.random.normal(ks[8], (DEPTH, D_MODEL), jnp.float32)
    w_gate = nrm(ks[9], (DEPTH, D_MODEL, D_FF), D_MODEL)
    w_up = nrm(ks[10], (DEPTH, D_MODEL, D_FF), D_MODEL)
    ffn_conv = nrm(ks[11], (DEPTH, FFN_CONV_WIDTH, D_FF), FFN_CONV_WIDTH)
    w_down = nrm(ks[12], (DEPTH, D_FF, D_MODEL), D_FF)
    ln_f = 1.0 + 0.02 * jax.random.normal(ks[13], (D_MODEL,), jnp.float32)
    return {'x': x, 'ln1': ln1, 'w_in': w_in, 'conv_qkv': conv_qkv, 'a_log': a_log, 'dt_bias': dt_bias,
            'gdn_norm': gdn_norm, 'w_out': w_out, 'ln2': ln2, 'w_gate': w_gate, 'w_up': w_up,
            'ffn_conv': ffn_conv, 'w_down': w_down, 'ln_f': ln_f}

def first_block(x, ln1, w_in, conv_qkv, a_log, dt_bias, gdn_norm, w_out, ln2, w_gate, w_up, ffn_conv, w_down, ln_f):
    bn, s, _ = x.shape
    slopes = alibi_slopes(SWA_HEADS)
    heads_b = lambda t: t.reshape(bn, s, SWA_HEADS, SWA_HEAD_DIM)
    for l in range(DEPTH):
        h = rmsnorm(x, ln1[l])
        proj = h @ w_in[l]
        qkv_a, z_a, b_a, a_a, q_b, k_b, v_b = jnp.split(proj, IN_SPLITS, axis=-1)
        y_a = gated_deltanet(qkv_a, z_a, b_a, a_a, conv_qkv[l], a_log[l], dt_bias[l], gdn_norm[l])
        y_b = dilated_attention(heads_b(q_b), heads_b(k_b), heads_b(v_b), slopes)
        y_b = y_b.reshape(bn, s, SWA_WIDTH).astype(x.dtype)
        x = x + jnp.concatenate([y_a, y_b], axis=-1) @ w_out[l]
        h = rmsnorm(x, ln2[l])
        gate = causal_dwconv(h @ w_gate[l], ffn_conv[l])
        x = x + (jax.nn.silu(gate) * (h @ w_up[l])) @ w_down[l]
    return rmsnorm(x, ln_f)


DEPTH_2 = 2

N_MIXERS = 2
N_LAYERS_A = (DEPTH_2 + 1) // 2
N_LAYERS_B = DEPTH_2 // 2

A_HEADS = 8
A_HEAD_DIM = 64
A_V_DIM = 2 * A_HEAD_DIM
Q_BLOCK = 128
T5_BUCKETS = 32
T5_MAX_DIST = 1024

B_HEADS = 16
B_HEAD_DIM = D_MODEL // B_HEADS
LEFT_CHUNKS = 8
BAND = (LEFT_CHUNKS + 1) * CHUNK
MAX_REL = 256

N_EXPERTS = 16
N_GROUPS = 4
E_PER_GROUP = N_EXPERTS // N_GROUPS
TOPK_GROUPS = 1
TOP_K = 2
D_FF_EXPERT = 512

NORM_EPS = 1e-6
NEG_INF = -1e30


def rms_norm(x, g):
    xf = x.astype(jnp.float32)
    y = xf * lax.rsqrt(jnp.mean(xf * xf, axis=-1, keepdims=True) + NORM_EPS)
    return (y * g.astype(jnp.float32)).astype(x.dtype)

def t5_bucket(rel):
    nb = T5_BUCKETS // 2
    ret = jnp.where(rel > 0, nb, 0)
    n = jnp.abs(rel)
    max_exact = nb // 2
    nf = jnp.maximum(n, 1).astype(jnp.float32)
    large = max_exact + (jnp.log(nf / max_exact) / math.log(T5_MAX_DIST / max_exact)
                         * (nb - max_exact)).astype(jnp.int32)
    large = jnp.minimum(large, nb - 1)
    return ret + jnp.where(n < max_exact, n, large)

def diff_attention(h, w_qkv, q_gain, k_gain, lam, subln_g, w_o, t5_bias, lambda_init):
    B, S, D = h.shape
    qkv = h @ w_qkv
    q, k, v = jnp.split(qkv, 3, axis=-1)
    q = q.reshape(B, S, A_HEADS, 2, A_HEAD_DIM)
    k = k.reshape(B, S, A_HEADS, 2, A_HEAD_DIM)
    v = v.reshape(B, S, A_HEADS, A_V_DIM)
    q = rms_norm(q, q_gain) * (A_HEAD_DIM ** -0.5)
    k = rms_norm(k, k_gain)
    lamf = lam.astype(jnp.float32)
    lam_full = (jnp.exp(jnp.sum(lamf[0] * lamf[1])) - jnp.exp(jnp.sum(lamf[2] * lamf[3]))
                + lambda_init)
    n_blocks = S // Q_BLOCK
    q_blocks = q.reshape(B, n_blocks, Q_BLOCK, A_HEADS, 2, A_HEAD_DIM).transpose(1, 0, 2, 3, 4, 5)
    k_pos = jnp.arange(S, dtype=jnp.int32)

    def one_block(args):
        qb, blk = args
        q_pos = blk * Q_BLOCK + jnp.arange(Q_BLOCK, dtype=jnp.int32)
        rel = k_pos[None, :] - q_pos[:, None]
        bias = t5_bias.astype(jnp.float32)[t5_bucket(rel)].transpose(2, 0, 1)
        allowed = (k_pos[None, :] // CHUNK) <= (q_pos[:, None] // CHUNK)
        s = jnp.einsum('bqhmd,bkhmd->bmhqk', qb, k).astype(jnp.float32) + bias[None, None]
        s = jnp.where(allowed[None, None, None], s, NEG_INF)
        p = jax.nn.softmax(s, axis=-1)
        a = p[:, 0] - lam_full * p[:, 1]
        return jnp.einsum('bhqk,bkhe->bqhe', a.astype(v.dtype), v)

    o = lax.map(one_block, (q_blocks, jnp.arange(n_blocks, dtype=jnp.int32)))
    o = o.transpose(1, 0, 2, 3, 4).reshape(B, S, A_HEADS, A_V_DIM)
    o = rms_norm(o, subln_g) * (1.0 - lambda_init)
    return o.reshape(B, S, D) @ w_o

def chunked_attention(h, w_qkv, q_gain, k_gain, rel_bias, w_o):
    B, S, D = h.shape
    NC = S // CHUNK
    qkv = h @ w_qkv
    q, k, v = jnp.split(qkv, 3, axis=-1)
    q = rms_norm(q.reshape(B, S, B_HEADS, B_HEAD_DIM), q_gain) * (B_HEAD_DIM ** -0.5)
    k = rms_norm(k.reshape(B, S, B_HEADS, B_HEAD_DIM), k_gain)
    v = v.reshape(B, S, B_HEADS, B_HEAD_DIM)
    pad = ((0, 0), (LEFT_CHUNKS * CHUNK, 0), (0, 0), (0, 0))
    kp = jnp.pad(k, pad)
    vp = jnp.pad(v, pad)
    qi = jnp.arange(CHUNK, dtype=jnp.int32)
    kb = jnp.arange(BAND, dtype=jnp.int32)
    rel = kb[None, :] - LEFT_CHUNKS * CHUNK - qi[:, None]
    idx = jnp.clip(rel, -MAX_REL, MAX_REL) + MAX_REL
    bias = rel_bias.astype(jnp.float32)[:, idx]
    band_chunk = kb // CHUNK
    q_chunks = q.reshape(B, NC, CHUNK, B_HEADS, B_HEAD_DIM).transpose(1, 0, 2, 3, 4)

    def one_chunk(args):
        qc, ci = args
        kband = lax.dynamic_slice_in_dim(kp, ci * CHUNK, BAND, axis=1)
        vband = lax.dynamic_slice_in_dim(vp, ci * CHUNK, BAND, axis=1)
        valid = (ci - LEFT_CHUNKS + band_chunk) >= 0
        s = jnp.einsum('bqhd,bkhd->bhqk', qc, kband).astype(jnp.float32) + bias[None]
        s = jnp.where(valid[None, None, None, :], s, NEG_INF)
        p = jax.nn.softmax(s, axis=-1)
        return jnp.einsum('bhqk,bkhd->bqhd', p.astype(vband.dtype), vband)

    o = lax.map(one_chunk, (q_chunks, jnp.arange(NC, dtype=jnp.int32)))
    o = o.transpose(1, 0, 2, 3, 4).reshape(B, S, D)
    return o @ w_o

def grouped_moe(h, router_w, router_bias, w_gate, w_up, w_down):
    B, S, D = h.shape
    t = h.reshape(B * S, D)
    scores = jax.nn.sigmoid((t @ router_w).astype(jnp.float32))
    sel = scores + router_bias.astype(jnp.float32)
    grp = sel.reshape(-1, N_GROUPS, E_PER_GROUP)
    group_score = lax.top_k(grp, TOP_K)[0].sum(-1)
    _, g_idx = lax.top_k(group_score, TOPK_GROUPS)
    group_mask = jax.nn.one_hot(g_idx, N_GROUPS, dtype=jnp.float32).sum(1) > 0
    expert_mask = jnp.repeat(group_mask, E_PER_GROUP, axis=1)
    masked = jnp.where(expert_mask, sel, NEG_INF)
    _, e_idx = lax.top_k(masked, TOP_K)
    w = jnp.take_along_axis(scores, e_idx, axis=1)
    w = w / jnp.sum(w, axis=-1, keepdims=True)
    gates = jnp.sum(jax.nn.one_hot(e_idx, N_EXPERTS, dtype=jnp.float32) * w[..., None], axis=1)
    gates = gates.astype(t.dtype)
    out = jnp.zeros_like(t)
    for e in range(N_EXPERTS):
        he = jax.nn.silu(t @ w_gate[e]) * (t @ w_up[e])
        out = out + gates[:, e:e + 1] * (he @ w_down[e])
    return out.reshape(B, S, D)

def second_inputs(seed: int = 0) -> dict:
    key = jax.random.key(seed)
    ks = jax.random.split(key, 24)
    D, F, E = D_MODEL, D_FF_EXPERT, N_EXPERTS
    nrm = lambda k, shape, s: jax.random.normal(k, shape, jnp.float32) * s
    gain = lambda k, shape: 1.0 + 0.02 * jax.random.normal(k, shape, jnp.float32)
    return {
        "x": nrm(ks[0], (BATCH, SEQ, D), 1.0),
        "c": nrm(ks[1], (BATCH, D), 1.0),
        "ada_w": nrm(ks[2], (DEPTH_2, D, 6 * D), 0.5 * D ** -0.5),
        "ada_b": nrm(ks[3], (DEPTH_2, 6 * D), 0.01),
        "norm_mix_g": gain(ks[4], (DEPTH_2, D)),
        "norm_ffn_g": gain(ks[5], (DEPTH_2, D)),
        "t5_bias": nrm(ks[6], (T5_BUCKETS, A_HEADS), 0.2),
        "a_w_qkv": nrm(ks[7], (N_LAYERS_A, D, 3 * D), D ** -0.5),
        "a_q_gain": gain(ks[8], (N_LAYERS_A, A_HEAD_DIM)),
        "a_k_gain": gain(ks[9], (N_LAYERS_A, A_HEAD_DIM)),
        "a_lambda": nrm(ks[10], (N_LAYERS_A, 4, A_HEAD_DIM), 0.1),
        "a_subln_g": gain(ks[11], (N_LAYERS_A, A_V_DIM)),
        "a_w_o": nrm(ks[12], (N_LAYERS_A, D, D), D ** -0.5),
        "b_w_qkv": nrm(ks[13], (N_LAYERS_B, D, 3 * D), D ** -0.5),
        "b_q_gain": gain(ks[14], (N_LAYERS_B, B_HEAD_DIM)),
        "b_k_gain": gain(ks[15], (N_LAYERS_B, B_HEAD_DIM)),
        "b_rel_bias": nrm(ks[16], (N_LAYERS_B, B_HEADS, 2 * MAX_REL + 1), 0.2),
        "b_w_o": nrm(ks[17], (N_LAYERS_B, D, D), D ** -0.5),
        "router_w": nrm(ks[18], (D, E), D ** -0.5),
        "router_bias": nrm(ks[19], (E,), 0.01),
        "moe_w_gate": nrm(ks[20], (DEPTH_2, E, D, F), D ** -0.5),
        "moe_w_up": nrm(ks[21], (DEPTH_2, E, D, F), D ** -0.5),
        "moe_w_down": nrm(ks[22], (DEPTH_2, E, F, D), F ** -0.5),
    }

def second_block(x, c, ada_w, ada_b, norm_mix_g, norm_ffn_g, t5_bias,
              a_w_qkv, a_q_gain, a_k_gain, a_lambda, a_subln_g, a_w_o,
              b_w_qkv, b_q_gain, b_k_gain, b_rel_bias, b_w_o,
              router_w, router_bias, moe_w_gate, moe_w_up, moe_w_down):
    silu_c = jax.nn.silu(c)
    for i in range(DEPTH_2):
        mod = silu_c @ ada_w[i] + ada_b[i]
        sh1, sc1, g1, sh2, sc2, g2 = [m[:, None, :] for m in jnp.split(mod, 6, axis=-1)]
        h = rms_norm(x, norm_mix_g[i]) * (1.0 + sc1) + sh1
        if i % N_MIXERS == 0:
            j = i // N_MIXERS
            lambda_init = 0.8 - 0.6 * math.exp(-0.3 * i)
            y = diff_attention(h, a_w_qkv[j], a_q_gain[j], a_k_gain[j], a_lambda[j],
                               a_subln_g[j], a_w_o[j], t5_bias, lambda_init)
        else:
            j = i // N_MIXERS
            y = chunked_attention(h, b_w_qkv[j], b_q_gain[j], b_k_gain[j], b_rel_bias[j], b_w_o[j])
        x = x + g1 * y
        h = rms_norm(x, norm_ffn_g[i]) * (1.0 + sc2) + sh2
        x = x + g2 * grouped_moe(h, router_w, router_bias, moe_w_gate[i], moe_w_up[i], moe_w_down[i])
    return x


def setup_inputs(seed=0):
    out = dict(first_inputs(seed))
    for name, value in second_inputs(seed + 1).items():
        if name != "x":
            out[name + "_2"] = value
    return out


def reference(
    x, ln1, w_in, conv_qkv, a_log, dt_bias, gdn_norm, w_out, ln2, w_gate, w_up, ffn_conv,
    w_down, ln_f, c_2, ada_w_2, ada_b_2, norm_mix_g_2, norm_ffn_g_2, t5_bias_2, a_w_qkv_2,
    a_q_gain_2, a_k_gain_2, a_lambda_2, a_subln_g_2, a_w_o_2, b_w_qkv_2, b_q_gain_2, b_k_gain_2,
    b_rel_bias_2, b_w_o_2, router_w_2, router_bias_2, moe_w_gate_2, moe_w_up_2, moe_w_down_2,
):
    x = first_block(
        x, ln1, w_in, conv_qkv, a_log, dt_bias, gdn_norm, w_out, ln2, w_gate, w_up, ffn_conv,
        w_down, ln_f,
    )
    return second_block(
        x, c_2, ada_w_2, ada_b_2, norm_mix_g_2, norm_ffn_g_2, t5_bias_2, a_w_qkv_2, a_q_gain_2,
        a_k_gain_2, a_lambda_2, a_subln_g_2, a_w_o_2, b_w_qkv_2, b_q_gain_2, b_k_gain_2,
        b_rel_bias_2, b_w_o_2, router_w_2, router_bias_2, moe_w_gate_2, moe_w_up_2,
        moe_w_down_2,
    )


_drawn_inputs = setup_inputs


def setup_inputs(seed=0):
    import zlib

    import numpy as np

    out = dict(_drawn_inputs(seed))
    spreads = {}
    factors = {'norm_mix_g_2': 5.085,
     'a_q_gain_2': 3.217,
     'a_k_gain_2': 3.998,
     'a_subln_g_2': 3.554,
     'b_q_gain_2': 8.0,
     'b_k_gain_2': 8.0,
     'b_rel_bias_2': 4.99}
    for name, (base, spread) in spreads.items():
        noise = np.random.default_rng([zlib.crc32(name.encode()), seed]).standard_normal(out[name].shape)
        drawn = base * np.exp(spread * noise) if base else spread * noise
        out[name] = __import__('jax').numpy.asarray(drawn.astype(out[name].dtype))
    for name, factor in factors.items():
        out[name] = (out[name] * factor).astype(out[name].dtype)
    return out
```

```python
import math
from collections import deque

import numpy as np
import concourse.bass as bass
from concourse import mybir

F32 = mybir.dt.float32
F32R = mybir.dt.float32r
I32 = mybir.dt.int32
ACT = mybir.ActivationFunctionType
ALU = mybir.AluOpType
AX = mybir.AxisListType

EPS = 1e-6
LAMBDA_INIT = 0.8 - 0.6 * math.exp(-0.3 * 0)
FAR = 1e30
LOCAL0 = 16512
LIMIT = 229344
PIECES = 14 + 4 + 33 + 48 + 2 * (16 + 96)




def _swa_tables():
    dist = np.zeros((128, 384), np.float32)
    count = np.zeros((128, 384), np.float32)
    for col in range(384):
        tile, key = (0, col) if col < 128 else (1, col - 128)
        for p in range(128):
            d = tile * 128 + p - key
            n = 0
            for window, dilation in ((128, 1), (512, 4), (2048, 16)):
                if d >= 0 and d % dilation == 0 and d // dilation <= window // dilation:
                    n += 1
            count[p, col] = n
            dist[p, col] = d if n else FAR
    return dist, count


def _t5_onehot():
    hot = np.zeros((128, 512), np.float32)
    for i in range(511):
        rel = 255 - i
        n = abs(rel)
        if n < 8:
            b = n
        else:
            b = 8
            while b < 15 and n ** 8 >= 8 ** 8 * 128 ** (b - 8 + 1):
                b += 1
        hot[b + (16 if rel > 0 else 0), i] = 1.0
    return hot


def constants():
    i = np.arange(128)
    out = {}
    out["ident"] = np.eye(128)
    out["tri"] = (i[:, None] <= i[None, :])
    out["stri"] = (i[:, None] < i[None, :])
    out["ones"] = np.ones((128, 128))
    out["iota"] = np.broadcast_to(np.arange(64), (128, 64))
    out["mhalf"] = np.full((128, 32), -0.5)
    out["eps"] = np.full((128, 1), EPS)
    strict = np.where(i[:, None] < i[None, :], 0.0, -FAR)
    causal = np.where(i[:, None] <= i[None, :], 0.0, -FAR)
    out["gmask"] = np.concatenate([strict, causal], 1)
    levels = []
    for l in range(7):
        b = 1 << l
        row, colm = i[None, :], i[:, None]
        levels.append(((row // (2 * b)) == (colm // (2 * b))) & ((row // b) % 2 == 1) & ((colm // b) % 2 == 0))
    out["level"] = np.concatenate(levels, 1)
    out["dist"], out["count"] = _swa_tables()
    corner = np.zeros((128, 256))
    corner[:64, 192:] = FAR
    out["corner"] = corner
    out["hot"] = _t5_onehot()
    k = np.arange(128)
    e, c = k % 16, k // 16 + 1
    use = k < 48
    out["cut"] = np.where(use, 64.0 * c, 0.0)[:, None]
    out["unit"] = np.concatenate([(e[:, None] == np.arange(16)) & use[:, None], np.where(use, 64.0 * c, 0.0)[:, None]], 1)
    out["where"] = np.where(use, 12 * (e // 2) + e % 2, 0)[:, None]
    out["w4"] = np.broadcast_to(np.tile(np.arange(4, 0, -1), 2), (128, 8))
    out["w16"] = np.broadcast_to(np.tile(np.arange(16, 0, -1), 2), (128, 32))
    return {k: np.ascontiguousarray(v, dtype=np.float32) for k, v in out.items()}


CONST = {k: v.shape[1] for k, v in constants().items()}
PARAM = dict(ln1=8, ln2=8, conv=48, fconv=66, alog=4, dtb=4, gain=128, wba=64, nmix=16, nffn=16, qk=4, subln=1,
             lam=256, rw=128, rbias=16, c=8, adab=64, t5=8)
PLACE = {}
for _k, _n in list(CONST.items()) + list(PARAM.items()):
    PLACE[_k] = (sum(n for _, n in PLACE.values()), _n)
NCST = sum(n for _, n in PLACE.values())




class Count:

    def __init__(self, nc, name):
        self.sem, self.n = nc.alloc_semaphore(name), 0

    def step(self, k):
        self.n += k
        return (self, self.n)


class Lane:

    def __init__(self, nc, name):
        self.count, self.items, self.met = Count(nc, "done_" + name), [], {}

    def wait(self, *marks):
        for m in marks:
            if m is None:
                continue
            if isinstance(m, list):
                self.wait(*m)
                continue
            count, value = m
            if self.met.get(count, 0) < value:
                self.met[count] = value
                self.items.append((None, count.sem, value))

    def do(self, op, *marks, signal=True):
        self.wait(*marks)
        if not signal:
            self.items.append((op, None, 0))
            return None
        self.items.append((op, self.count.sem, 1))
        return self.count.step(1)

    def dma(self, op, count, *marks):
        self.wait(*marks)
        self.items.append((op, count.sem, 16))
        return count.step(16)

    def open(self, count):
        self.kept = (self.items, self.met, self.count)
        self.items, self.met, self.count = [], dict(self.met), count

    def close(self):
        inner = self.items
        self.items, self.met, self.count = self.kept
        return inner

    def branch(self, number, lists):
        self.items.append((number, "branch", lists))

    def emit(self, e, items=None):
        for op, sem, n in self.items if items is None else items:
            if sem == "branch":
                self.nest(e, e.value_load(op, min_val=0, max_val=len(n)), n, 0)
            elif op is None:
                e.wait_ge(sem, n)
            elif sem is None:
                op(e)
            else:
                op(e).then_inc(sem, n)

    def nest(self, e, value, lists, i):
        if i < len(lists):
            with e.If(value > i):
                self.emit(e, lists[i])
                self.nest(e, value, lists, i + 1)


class Turns:

    def __init__(self, things):
        self.free = deque((t, []) for t in things)

    def take(self):
        return self.free.popleft()

    def give(self, thing, *marks):
        self.free.append((thing, list(marks)))


def blocks(ap, b):
    return ap.rearrange("p (a b) -> p a b", b=b)


def spread(ap, n, k):
    return ap.unsqueeze(2).to_broadcast([128, n, k])


def again(ap, n, k):
    return ap.unsqueeze(1).to_broadcast([128, n, k])




class Core:
    def __init__(self, nc):
        self.nc = nc
        self.pe, self.act, self.dve, self.pool, self.sp = (Lane(nc, n) for n in ("pe", "act", "dve", "pool", "sp"))
        self.psum = Turns([nc.alloc_psum_tensor(f"bank{i}", [128, 512], F32) for i in range(8)])
        self.names = 0
        self.order = []
        self.slots = deque()
        self.live = []
        self.outs = []

    def sb(self, shape, offset, dt=F32):
        self.names += 1
        size = int(np.prod(shape[1:])) * 4
        assert offset % 32 == 0 and offset + size <= LIMIT, (offset, size)
        return self.nc.alloc_sbuf_tensor_at(f"t{self.names}", shape, dt, offset=offset)


    def add_slot(self, offset, *marks):
        n = self.names
        self.slots.append(((self.sb([128, 2048], offset), Count(self.nc, f"slot{n}")), list(marks)))

    def piece(self, key):
        (t, count), marks = self.slots.popleft()
        src = self.weights[len(self.order)]
        self.order.append(key)
        mark = self.sp.dma(lambda e: e.dma_start(t[:, :], src), count, marks)
        return t, mark, (t, count)

    def piece_done(self, slot, *marks):
        self.slots.append((slot, list(marks)))


    def mm(self, out, l, r, first, last, *marks, signal=False):
        return self.pe.do(lambda e: e.matmul(out, l, r, start=first, stop=last, skip_group_check=True),
                          *marks, signal=signal)

    def mm3(self, out, l, r, first, last, *marks, signal=False):
        self.mm(out, l[0], r[0], first, False, *marks)
        self.mm(out, l[0], r[1], False, False)
        return self.mm(out, l[1], r[0], False, last, signal=signal)

    def tr(self, out, in_, *marks, signal=False, rows=128):
        ident = self.ident[0:rows, 0:rows]
        return self.pe.do(lambda e: e.transpose(out, in_, ident), *marks, signal=signal)

    def fn(self, out, in_, f, *marks, bias=None, scale=None, accum=None):
        kw = {}
        if bias is not None:
            kw["bias"] = bias
        if scale is not None:
            kw["scale"] = scale
        if accum is not None:
            kw["accum_out"] = accum
        return self.act.do(lambda e: e.activation(out, in_, f, **kw), *marks)

    def acp(self, out, in_, *marks, scale=None):
        return self.fn(out, in_, ACT.Copy, *marks, scale=scale)

    def tt(self, out, a, b, op, *marks, lane=None):
        return (lane or self.dve).do(lambda e: e.tensor_tensor(out, a, b, op), *marks)

    def ts(self, out, a, s1, op0, *marks, s2=None, op1=None, lane=None):
        if op1 is None:
            return (lane or self.dve).do(lambda e: e.tensor_scalar(out, a, s1, None, op0), *marks)
        return (lane or self.dve).do(lambda e: e.tensor_scalar(out, a, s1, s2, op0, op1), *marks)

    def stt(self, out, a, s, b, op0, op1, *marks):
        return self.dve.do(lambda e: e.scalar_tensor_tensor(out, a, s, b, op0, op1), *marks)

    def ttr(self, out, a, b, op0, op1, start, accum, *marks):
        return self.dve.do(lambda e: e.tensor_tensor_reduce(out=out, in0=a, in1=b, scale=1.0, scalar=start, op0=op0,
                                                            op1=op1, accum_out=accum), *marks)

    def cp(self, out, in_, *marks, lane=None):
        return (lane or self.dve).do(lambda e: e.tensor_copy(out, in_), *marks)

    def red(self, out, in_, op, *marks):
        return self.dve.do(lambda e: e.tensor_reduce(out, in_, AX.X, op), *marks)

    def rec(self, out, in_, *marks):
        return self.dve.do(lambda e: e.reciprocal(out, in_), *marks)


    def col(self, n):
        a = self.colat
        self.colat += n
        assert self.colat <= self.cols.shape[1], "columns"
        return self.cols[:, a:a + n]

    def cst(self, name):
        a, n = PLACE[name]
        return self.cstt[:, a:a + n]

    def rstd(self, ss, n, scale, *marks):
        v, r0, a, b, r = (self.col(n) for _ in range(5))
        m = self.ts(v, ss, scale, ALU.mult, *marks, s2=EPS, op1=ALU.add, lane=self.pool)
        m = self.tt(r0, v, self.cst("mhalf")[:, 0:n], ALU.pow, m, lane=self.pool)
        m = self.tt(a, r0, r0, ALU.mult, m)
        m = self.stt(b, a, -0.5, v, ALU.mult, ALU.mult, m)
        m = self.stt(r, b, 1.5, r0, ALU.add, ALU.mult, m)
        return r, m


    def start(self, gen):
        self.live.append(gen)

    def tick(self):
        for g in list(self.live):
            if next(g, self) is self:
                self.live.remove(g)

    def marks(self):
        return [lane.count.step(0) for lane in (self.pe, self.act, self.dve, self.pool)]

    def drain(self):
        while self.live:
            self.tick()

    def run(self, gen):
        for _ in gen:
            self.tick()


    def feed(self, halves):
        self.todo, self.ready, self.open = deque(halves), deque(), {}
        self.top()

    def top(self):
        while self.todo and self.stages.free:
            key, half = self.todo.popleft()
            if half == 0:
                self.open[key] = self.piece(key)
            w, load, slot = self.open[key]
            (hi, lo), free = self.stages.take()
            src = w[:, half * 1024:half * 1024 + 1024]
            m = self.acp(hi[:, :], src, load, free)
            m = self.tt(lo[:, :], src, hi[:, :].bitcast(F32), ALU.subtract, m, load)
            if half == 1:
                self.piece_done(slot, m)
            self.ready.append((key, half, hi, lo, m))

    def staged(self, key, half):
        k, h, hi, lo, m = self.ready.popleft()
        assert (k, h) == (key, half), (k, h, key, half)
        return hi, lo, m

    def unstage(self, hi, lo, mark):
        self.stages.give((hi, lo), mark)
        self.top()

    def feature_major(self, key, then, hmark):
        bank, free = self.psum.take()
        for c in (0, 1):
            hi, lo, m = self.staged(key, c)
            for kt in range(8):
                s = slice(kt * 128, kt * 128 + 128)
                d = self.mm3(bank[:, c * 256:c * 256 + 256], (hi[:, s], lo[:, s]),
                             (self.hh[:, kt, :], self.hl[:, kt, :]), kt == 0, kt == 7, m, free, hmark,
                             signal=kt == 7)
            self.unstage(hi, lo, d)
            if c == 1:
                self.start(then(bank, d))
            yield
        self.hread = d

    def token_major(self, key, then, hmark):
        bank, free = self.psum.take()
        for half in (0, 1):
            hi, lo, m = self.staged(key, half)
            for t in (0, 1):
                for kk in range(4):
                    kt = half * 4 + kk
                    s = slice(kk * 256, kk * 256 + 256)
                    q = slice(t * 128, t * 128 + 128)
                    d = self.mm3(bank[:, t * 256:t * 256 + 256], (self.hh[:, kt, q], self.hl[:, kt, q]),
                                 (hi[:, s], lo[:, s]), kt == 0 and t == 0, kt == 7, m, free, hmark,
                                 signal=kk == 3 and t == 1)
            self.unstage(hi, lo, d)
            if half == 1:
                self.start(then(bank, d))
            yield
        self.hread = d

    def project(self, name, order, src, marks):
        yh, yl = src
        banks = [self.psum.take() for _ in range(4)]
        for n, j in enumerate(order):
            for half in (0, 1):
                kt = 2 * j + half
                hi, lo, m = self.staged((*name, j), half)
                for t in (0, 1):
                    for nh in (0, 1):
                        s = slice(nh * 512, nh * 512 + 512)
                        q = slice(t * 128, t * 128 + 128)
                        bank, free = banks[t * 2 + nh]
                        d = self.mm3(bank[:, :], (yh[:, kt, q], yl[:, kt, q]), (hi[:, s], lo[:, s]),
                                     n == 0 and half == 0, n == len(order) - 1 and half == 1, m, free, marks(kt),
                                     signal=t == 1 and nh == 1)
                self.unstage(hi, lo, d)
                yield
        self.yread = d
        self.sums = [b for b, _ in banks]
        self.sumsmark = d

    def add_sums(self, gate=None, tmp=None):
        for t in (0, 1):
            for nh in (0, 1):
                bank = self.sums[t * 2 + nh]
                s = slice(nh * 512, nh * 512 + 512)
                xs = self.x[:, t, s]
                if gate is None:
                    m = self.tt(xs, bank[:, :], xs, ALU.add, self.sumsmark, self.xmarks[t])
                    self.psum.give(bank, m)
                else:
                    f, free = tmp.take()
                    m = self.tt(f[:, :], bank[:, :], gate[0][:, s], ALU.mult, self.sumsmark, gate[1], free)
                    self.psum.give(bank, m)
                    m = self.tt(xs, f[:, :], xs, ALU.add, m, self.xmarks[t])
                    tmp.give(f, m)
                self.xnew = self.xnew + [(t, m)]
        self.settle()

    def settle(self):
        for t in (0, 1):
            self.xmarks[t] = [m for u, m in self.xnew if u == t]
        self.xnew = []

    def norm_x(self, xn, free):
        ss = self.col(2)
        ms = [self.fn(xn[:, t, :], self.x[:, t, :], ACT.Square, self.xmarks[t], free, accum=ss[:, t:t + 1])
              for t in (0, 1)]
        r, m = self.rstd(ss, 2, 1.0 / 1024, ms)
        return [self.acp(xn[:, t, :], self.x[:, t, :], m, ms, scale=r[:, t:t + 1]) for t in (0, 1)]

    def front(self, gain, shift, xn, xnfree, tmp, hfree):
        xm = self.norm_x(xn, xnfree)
        for j in range(4):
            bank, free = self.psum.take()
            for kk in (0, 1):
                for t in (0, 1):
                    o = (kk * 2 + t) * 128
                    k = (2 * j + kk) * 128
                    d = self.tr(bank[:, o:o + 128], xn[:, t, k:k + 128], free, xm, signal=kk == 1 and t == 1)
            f, ffree = tmp.take()
            for kk in (0, 1):
                kt = 2 * j + kk
                s = slice(kk * 256, kk * 256 + 256)
                if shift is None:
                    m = self.ts(f[:, s], bank[:, s], gain[0][:, kt:kt + 1], ALU.mult, d, ffree, gain[1])
                else:
                    m = self.ts(f[:, s], bank[:, s], gain[0][:, kt:kt + 1], ALU.mult, d, ffree, gain[1], shift[1],
                                s2=shift[0][:, kt:kt + 1], op1=ALU.add)
            self.psum.give(bank, m)
            a = self.acp(self.hh[:, 2 * j:2 * j + 2, :], blocks(f[:, :], 256), m, hfree)
            m = self.tt(self.hl[:, 2 * j:2 * j + 2, :], blocks(f[:, :], 256),
                        self.hh[:, 2 * j:2 * j + 2, :].bitcast(F32), ALU.subtract, a, m, hfree)
            tmp.give(f, m)
        self.xnread = d
        return m


def conv_taps(k, out, bank, at, taps, width, mark, free):
    m = k.ts(out, bank[:, at:at + 256], taps[:, width - 1:width], ALU.mult, mark, free)
    for j in range(1, width):
        m = k.stt(out[:, j:256], bank[:, at:at + 256 - j], taps[:, width - 1 - j:width - j], out[:, j:256],
                  ALU.mult, ALU.add, m)
    return m


def first_mixer(k, at):
    base = at

    def room(*shape):
        nonlocal at
        t = k.sb([128, *shape], at)
        at += int(np.prod(shape)) * 4
        return t

    kq = room(4, 2, 256)
    zg = room(2, 512)
    qb, kb = room(4, 256), room(4, 256)
    vb = room(2, 512)
    aqat = at
    AQ = room(8, 256)
    tat = at
    T = room(8, 128)
    TT = room(8, 128)
    amat = at
    AM = [room(4, 128) for _ in range(2)]
    X = [room(4, 128) for _ in range(2)]
    vT = room(4, 256)
    vB = room(8, 128)
    scrat = at
    ys = Turns([room(256) for _ in range(3)])
    sqs = Turns([room(256) for _ in range(2)])
    diags = Turns([room(256) for _ in range(2)])
    biases = Turns([room(384) for _ in range(2)])
    Ss = Turns([room(384) for _ in range(3)])
    PTs = Turns([room(384) for _ in range(3)])
    assert at <= k.f1end, (at, k.f1end)
    kd, S1 = k.sb([128, 4, 128], tat), k.sb([128, 4, 128], tat + 2048)
    r1, qs = k.sb([128, 4, 128], amat), k.sb([128, 4, 128], amat + 2048)
    o = k.sb([128, 8, 128], amat + 4096)
    vT0 = scrat - 4096 - 4096
    vn = [k.sb([128, 4, 128], vT0), k.sb([128, 4, 128], vT0 + 2048)]
    xn = k.sb([128, 2, 1024], aqat)
    tmp = Turns([k.sb([128, 512], scrat), k.sb([128, 512], scrat + 2048)])

    cst, col, mul, add, sub = k.cst, k.col, ALU.mult, ALU.add, ALU.subtract
    hm = k.front((cst("ln1"), k.cmark), None, xn, [], tmp, [])
    tmpm = [m for _, m in tmp.free]

    wba = cst("wba")
    bbank, free = k.psum.take()
    for t in (0, 1):
        q = slice(t * 128, t * 128 + 128)
        for part in (k.hh, k.hl):
            for kt in range(8):
                ba = k.mm(bbank[:, t * 8:t * 8 + 8], part[:, kt, q].bitcast(F32), wba[:, kt * 8:kt * 8 + 8],
                          part is k.hh and kt == 0, part is k.hl and kt == 7, free, hm,
                          signal=t == 1 and part is k.hl and kt == 7)
    y2 = col(16)
    b3 = blocks(bbank[:, 0:16], 8)
    k.ts(blocks(y2[:, 0:8], 4), b3[:, :, 0:4], -1.0, mul, ba)
    bam = k.tt(blocks(y2[:, 8:16], 4), b3[:, :, 4:8], again(cst("dtb"), 2, 4), add, ba)
    k.psum.give(bbank, bam)

    sbank, sfree = k.psum.take()
    kqm, vm, zm, ssm = {}, {}, {}, []
    taps = cst("conv")

    def conv_piece(kind, pair):
        def then(bank, d):
            made = []
            for c in (0, 1):
                h = pair * 2 + c
                chunk = {"q": 0, "k": 4, "v": 8}[kind] + h
                y, yfree = ys.take()
                m = conv_taps(k, y[:, :], bank, c * 256, taps[:, chunk * 4:chunk * 4 + 4], 4, d, [yfree, tmpm])
                dest = vT[:, h, :] if kind == "v" else kq[:, h, int(kind == "q"), :]
                a = k.fn(dest, y[:, :], ACT.Silu, m)
                ys.give(y, a)
                if kind == "v":
                    vm[h] = a
                    continue
                kqm[kind, h] = a
                sq, sqfree = sqs.take()
                made.append((h, sq, k.fn(sq[:, :], dest, ACT.Square, a, sqfree, tmpm)))
            k.psum.give(bank, m)
            yield
            for h, sq, a in made:
                for t in (0, 1):
                    i = (kind == "q") * 8 + t * 4 + h
                    s = k.mm(sbank[:, i:i + 1], sq[:, t * 128:t * 128 + 128], cst("ones")[:, 0:1], True, True, a, sfree,
                             signal=t == 1)
                sqs.give(sq, s)
                ssm.append(s)
        return then

    def z_piece(pair):
        def then(bank, d):
            s = slice(pair * 256, pair * 256 + 256)
            a = k.fn(zg[:, :, s], blocks(bank[:, :], 256), ACT.Silu, d)
            k.psum.give(bank, a)
            for t in (0, 1):
                zm[pair, t] = k.tt(blocks(zg[:, t, s], 128), blocks(zg[:, t, s], 128), again(cst("gain"), 2, 128),
                                   mul, a)
            yield
        return then

    qbm, kbm, vbm = {}, {}, {}

    def swa_qk(dest, marks, pair, scale):
        def then(bank, d):
            a = k.acp(dest[:, 2 * pair:2 * pair + 2, :], blocks(bank[:, :], 256), d, scale=scale)
            k.psum.give(bank, a)
            marks[pair] = a
            yield
        return then

    def swa_v(pair):
        def then(bank, d):
            a = k.acp(vb[:, :, pair * 256:pair * 256 + 256], blocks(bank[:, :], 256), d)
            k.psum.give(bank, a)
            vbm[pair] = a
            yield
        return then

    ym = {}

    def swa(heads):
        state = {}

        def scores(h):
            ch, r = h // 2, slice(64 * (h % 2), 64 * (h % 2) + 64)
            pair = ch // 2
            bank, free = k.psum.take()
            k.mm(bank[:, 0:128], qb[r, ch, 0:128], kb[r, ch, 0:128], True, True, qbm[pair], kbm[pair], free)
            d = k.mm(bank[:, 128:384], qb[r, ch, 128:256], kb[r, ch, :], True, True, signal=True)
            bt, bfree = biases.take()
            b = k.acp(bt[:, :], cst("dist"), bfree, scale=float(2.0 ** -(h + 1)))
            S, f = Ss.take()
            nm, den, inv = col(2), col(2), col(2)
            parts = (slice(0, 128), slice(128, 384))
            ms = [k.ttr(S[:, p], bank[:, p], bt[:, p], add, ALU.min, FAR * 4, nm[:, i:i + 1], d, b, f)
                  for i, p in enumerate(parts)]
            k.psum.give(bank, ms[1])
            biases.give(bt, ms[1])
            es = [k.fn(S[:, p], S[:, p], ACT.Exp, ms[i], bias=nm[:, i:i + 1], scale=-1.0) for i, p in enumerate(parts)]
            cs = [k.ttr(S[:, p], S[:, p], cst("count")[:, p], mul, add, 0.0, den[:, i:i + 1], es[i])
                  for i, p in enumerate(parts)]
            rv = k.rec(inv, den, cs)
            for i, p in enumerate(parts):
                m = k.ts(S[:, p], S[:, p], inv[:, i:i + 1], mul, rv)
            state[h] = (S, m)

        def turn(h):
            S, m = state[h]
            bank, free = k.psum.take()
            for j in range(3):
                d = k.tr(bank[:, j * 128:j * 128 + 128], S[:, j * 128:j * 128 + 128], m, free, signal=j == 2)
            Ss.give(S, d)
            PT, f = PTs.take()
            a = k.acp(PT[:, :], bank[:, 0:384], d, f)
            k.psum.give(bank, a)
            state[h] = (PT, a)

        def values(h):
            PT, a = state.pop(h)
            r = slice(64 * (h % 2), 64 * (h % 2) + 64)
            if h % 2 == 0:
                state["out"] = k.psum.take()
            bank, free = state["out"]
            v = slice(h * 64, h * 64 + 64)
            k.mm(bank[r, 0:256], vb[:, 0, v], PT[:, 0:256], True, False, a, vbm[h // 4], free)
            d = k.mm(bank[r, 128:256], vb[:, 1, v], PT[:, 256:384], False, True, signal=True)
            PTs.give(PT, d)
            if h % 2 == 1:
                kt = 4 + h // 2
                a = k.acp(k.yh[:, kt, :], bank[:, 0:256], d)
                m = k.tt(k.yl[:, kt, :], bank[:, 0:256], k.yh[:, kt, :].bitcast(F32), sub, a)
                k.psum.give(bank, m)
                ym[kt] = m

        n = len(heads)
        for i in range(n + 2):
            if i < n:
                scores(heads[i])
            if 1 <= i <= n:
                turn(heads[i - 1])
            if i >= 2:
                values(heads[i - 2])
            yield

    def delta():
        eps = cst("eps")
        ones, ident = cst("ones"), cst("ident")
        ab, u, w, lw, den, sp, ea, lns, lnr = (col(16) for _ in range(9))
        m = k.stt(ab, y2, -1.0, y2, mul, ALU.max, bam)
        uu = k.fn(u, ab, ACT.Exp, m, scale=-1.0)
        em = k.fn(ea[:, 0:4], cst("alog"), ACT.Exp, k.cmark)
        wm = k.ts(w, u, 1.0, add, uu)
        lm = k.fn(lw, w, ACT.Ln, wm)
        lsm = k.fn(lns, sbank[:, 0:16], ACT.Ln, ssm, bias=eps)
        k.psum.give(sbank, lsm)
        dm = k.ts(den, w, -1.0, add, wm, s2=1e-30, op1=add)
        dm = k.rec(den, den, dm)
        m = k.stt(lw, lw, 1e-30, u, add, mul, lm)
        m = k.tt(lw, lw, den, mul, m, dm)
        m = k.stt(sp, y2, 0.0, lw, ALU.max, add, m)
        lrm = k.ts(lnr, lns, -0.5, mul, lsm)
        g = col(8)
        gm = k.stt(blocks(g, 4), blocks(sp[:, 8:16], 4), -1.0, again(ea[:, 0:4], 2, 4), mul, mul, m, em)
        yield
        cbank, free = k.psum.take()
        k.mm(cbank[:, 0:8], cst("tri"), g, True, True, gm, free)
        d = k.mm(cbank[:, 8:16], ones, g, True, True, signal=True)
        cum, tot, av, rv, sv, er, es, ekd, beta = (col(8) for _ in range(9))
        k.cp(cum, cbank[:, 0:8], d)
        m = k.cp(tot, cbank[:, 8:16], d)
        k.psum.give(cbank, m)
        lnk, lnq = lnr[:, 0:8], lnr[:, 8:16]
        avm = k.tt(av, lnk, cum, sub, m, lrm)
        m1 = k.tt(rv, cum, sp[:, 0:8], sub, m)
        rm = k.tt(rv, rv, lnk, add, m1)
        sm = k.stt(sv, cum, -0.5 * float(np.log(128.0)), lnq, add, add, m, lrm)
        kdm = k.tt(ekd, tot, av, add, avm)
        erm = k.fn(er, rv, ACT.Exp, rm)
        esm = k.fn(es, sv, ACT.Exp, sm)
        kdm = k.fn(ekd, ekd, ACT.Exp, kdm)
        btm = k.fn(beta, sp[:, 0:8], ACT.Exp, m1, scale=-1.0)
        yield
        aqm = {}
        pend = []
        for i in range(4):
            bank, free = k.psum.take()
            for u_ in (2 * i, 2 * i + 1):
                dg, f = diags.take()
                k.ts(dg[:, 0:128], ident, rv[:, u_:u_ + 1], mul, rm, f)
                m = k.ts(dg[:, 128:256], ident, sv[:, u_:u_ + 1], mul, sm)
                o_ = (u_ % 2) * 256
                d = k.mm(bank[:, o_:o_ + 256], ones, dg[:, :], True, True, m, free, signal=True)
                diags.give(dg, d)
            m = k.tt(AQ[:, 2 * i:2 * i + 2, :], blocks(bank[:, :], 256), again(cst("gmask"), 2, 256), add, d, k.xnread)
            k.psum.give(bank, m)
            for u_ in (2 * i, 2 * i + 1):
                a = k.fn(AQ[:, u_, :], AQ[:, u_, :], ACT.Exp, m, avm, bias=av[:, u_:u_ + 1])
            yield
            bank, free = k.psum.take()
            for u_ in (2 * i, 2 * i + 1):
                c, h = u_ // 4, u_ % 4
                s = slice(c * 128, c * 128 + 128)
                o_ = (u_ % 2) * 256
                d = k.mm(blocks(bank[:, o_:o_ + 256], 128), kq[:, h, 0, s], kq[:, h, :, s], True, True, kqm["k", h],
                         kqm["q", h], free, signal=True)
            m = k.tt(AQ[:, 2 * i:2 * i + 2, :], AQ[:, 2 * i:2 * i + 2, :], blocks(bank[:, :], 256), mul, a, d)
            k.psum.give(bank, m)
            aqm[i // 2] = m
        lvl = cst("level")
        tm, ttm, amread, xread = [None, None], [None, None], [None, None], [None, None]
        for c in (0, 1):
            us = slice(c * 4, c * 4 + 4)
            m = k.tt(AM[c][:, :, :], AQ[:, us, 0:128], again(lvl[:, 0:128], 4, 128), mul, aqm[c])
            ttm[c] = k.tt(TT[:, us, :], again(ident, 4, 128), AM[c][:, :, :], sub, m)
            amread[c] = ttm[c]
        yield
        for c in (0, 1):
            bank, free = k.psum.take()
            for h in range(4):
                d = k.tr(bank[:, h * 128:h * 128 + 128], TT[:, c * 4 + h, :], ttm[c], free, signal=h == 3)
            tm[c] = k.acp(T[:, c * 4:c * 4 + 4, :], blocks(bank[:, :], 128), d)
            k.psum.give(bank, tm[c])
        bvm = {}
        for c in (0, 1):
            bank, free = k.psum.take()
            for h in range(4):
                d = k.tr(bank[:, h * 128:h * 128 + 128], vT[:, h, c * 128:c * 128 + 128], vm[h], free, signal=h == 3)
            bvm[c] = k.tt(vB[:, c * 4:c * 4 + 4, :], blocks(bank[:, :], 128), spread(beta[:, c * 4:c * 4 + 4], 4, 128),
                          mul, d, btm)
            k.psum.give(bank, bvm[c])
        vtread = d
        yield
        for l in range(1, 7):
            xm = [None, None]
            for c in (0, 1):
                us = slice(c * 4, c * 4 + 4)
                m = k.tt(AM[c][:, :, :], AQ[:, us, 0:128], again(lvl[:, l * 128:l * 128 + 128], 4, 128), mul, aqm[c],
                         amread[c])
                bank, free = k.psum.take()
                for h in range(4):
                    d = k.mm(bank[:, h * 128:h * 128 + 128], AM[c][:, h, :], T[:, c * 4 + h, :], True, True, m, tm[c],
                             free, signal=h == 3)
                amread[c] = d
                xm[c] = k.acp(X[c][:, :, :], blocks(bank[:, :], 128), d, xread[c])
                k.psum.give(bank, xm[c])
            yield
            for c in (0, 1):
                us = slice(c * 4, c * 4 + 4)
                if l < 6:
                    bank, free = k.psum.take()
                    for h in range(4):
                        d = k.mm(bank[:, h * 128:h * 128 + 128], TT[:, c * 4 + h, :], X[c][:, h, :], True, True, xm[c],
                                 ttm[c], free, signal=h == 3)
                    bank2, free = k.psum.take()
                else:
                    bank2, free = k.psum.take()
                for h in range(4):
                    d2 = k.mm(bank2[:, h * 128:h * 128 + 128], X[c][:, h, :], TT[:, c * 4 + h, :], True, True, xm[c],
                              ttm[c], free, signal=h == 3)
                xread[c] = d2
                if l < 6:
                    tm[c] = k.tt(T[:, us, :], T[:, us, :], blocks(bank[:, :], 128), sub, d, d2, tm[c])
                    k.psum.give(bank, tm[c])
                ttm[c] = k.tt(TT[:, us, :], TT[:, us, :], blocks(bank2[:, :], 128), sub, d2)
                k.psum.give(bank2, ttm[c])
            yield
        solved = list(ttm)

        def bank4(f, *marks):
            bank, free = k.psum.take()
            for h in range(4):
                l, r = f(h)
                d = k.mm(bank[:, h * 128:h * 128 + 128], l, r, True, True, free, *marks, signal=h == 3)
            return bank, blocks(bank[:, :], 128), d

        bank, b, d = bank4(lambda h: (TT[:, h, :], vB[:, h, :]), solved, bvm[0])
        vnm = k.acp(vn[0][:, :, :], b, d, vtread)
        k.psum.give(bank, vnm)
        bank, free = k.psum.take()
        for h in range(4):
            d = k.tr(bank[:, h * 128:h * 128 + 128], kq[:, h, 0, 0:128], free, signal=h == 3)
        kdm = k.tt(kd[:, :, :], blocks(bank[:, :], 128), spread(ekd[:, 0:4], 4, 128), mul, d, kdm, solved, xread)
        k.psum.give(bank, kdm)
        yield
        bank, b, d = bank4(lambda h: (kd[:, h, :], vn[0][:, h, :]), vnm, kdm)
        s1m = k.acp(S1[:, :, :], b, d, solved)
        k.psum.give(bank, s1m)
        bank, b, d = bank4(lambda h: (AQ[:, h, 128:256], vn[0][:, h, :]), vnm, aqm[0])
        om = [k.cp(o[:, 0:4, :], b, d, solved, xread), None]
        k.psum.give(bank, om[0])
        yield
        bank, b, d = bank4(lambda h: (kq[:, h, 0, 128:256], S1[:, h, :]), s1m)
        m = k.tt(r1[:, :, :], b, spread(er[:, 4:8], 4, 128), mul, d, erm, amread)
        k.psum.give(bank, m)
        rm1 = k.tt(r1[:, :, :], vB[:, 4:8, :], r1[:, :, :], sub, m)
        bank, b, d = bank4(lambda h: (kq[:, h, 1, 128:256], S1[:, h, :]), s1m)
        qsm = k.tt(qs[:, :, :], b, spread(es[:, 4:8], 4, 128), mul, d, esm, amread)
        k.psum.give(bank, qsm)
        yield
        bank, b, d = bank4(lambda h: (TT[:, 4 + h, :], r1[:, h, :]), rm1)
        vnm = k.acp(vn[1][:, :, :], b, d, vtread)
        k.psum.give(bank, vnm)
        yield
        bank, b, d = bank4(lambda h: (AQ[:, 4 + h, 128:256], vn[1][:, h, :]), vnm, aqm[1])
        om[1] = k.tt(o[:, 4:8, :], b, qs[:, :, :], add, d, qsm)
        k.psum.give(bank, om[1])
        sq = k.sb([128, 8, 128], aqat)
        ss = col(8)
        m = k.tt(sq[:, :, :], o[:, :, :], o[:, :, :], mul, om, d)
        m = k.red(ss, sq[:, :, :], add, m)
        r, rm_ = k.rstd(ss, 8, 1.0 / 128, m)
        m = k.tt(o[:, :, :], o[:, :, :], spread(r, 8, 128), mul, rm_)
        m = k.tt(o[:, :, :], o[:, :, :], zg[:, :, :].rearrange("p t (h d) -> p (t h) d", d=128), mul, m,
                 list(zm.values()))
        yield
        for pair in (0, 1):
            bank, free = k.psum.take()
            for h_ in (0, 1):
                for t in (0, 1):
                    o_ = h_ * 256 + t * 128
                    d = k.tr(bank[:, o_:o_ + 128], o[:, t * 4 + pair * 2 + h_, :], m, free, signal=h_ == 1 and t == 1)
            s = slice(2 * pair, 2 * pair + 2)
            a = k.acp(k.yh[:, s, :], blocks(bank[:, :], 256), d)
            lm_ = k.tt(k.yl[:, s, :], blocks(bank[:, :], 256), k.yh[:, s, :].bitcast(F32), sub, a)
            k.psum.give(bank, lm_)
            ym[2 * pair] = ym[2 * pair + 1] = lm_
        yield

    for kind in "qkv":
        for pair in (0, 1):
            k.run(k.feature_major((kind, pair), conv_piece(kind, pair), hm))
    for pair in (0, 1):
        k.run(k.token_major(("z", pair), z_piece(pair), hm))
    k.start(delta())
    for pair in (0, 1):
        k.run(k.feature_major(("qb", pair), swa_qk(qb, qbm, pair, -0.125), hm))
        k.run(k.feature_major(("kb", pair), swa_qk(kb, kbm, pair, None), hm))
        k.run(k.token_major(("vb", pair), swa_v(pair), hm))
        k.start(swa(range(pair * 4, pair * 4 + 4)))
    k.drain()
    k.run(k.project(("wo",), (2, 3, 0, 1), (k.yh, k.yl), lambda kt: ym[kt]))
    k.add_sums()


def first_ffn(k, at):
    def room(*shape, dt=F32):
        nonlocal at
        t = k.sb([128, *shape], at, dt)
        at += int(np.prod(shape)) * 4
        return t

    fence = k.fence
    xn = room(2, 1024)
    tmp = Turns([room(512) for _ in range(2)])
    ys = Turns([room(256) for _ in range(2)])
    gs = Turns([room(256) for _ in range(2)])
    ams = Turns([room(256) for _ in range(2)])
    aps = Turns([(room(256, dt=F32R), room(256, dt=F32R)) for _ in range(3)])
    lnf = room(1024)
    assert at <= k.f2end
    lcount = Count(k.nc, "lnf")
    src = k.lnf
    lm = k.act.dma(lambda e: e.dma_start(lnf[:, :], src), lcount, fence)
    k.dve.wait(fence)
    k.act.wait(fence)
    hm = k.front((k.cst("ln2"), k.cmark), None, xn, [], tmp, [k.hread])
    taps = k.cst("fconv")
    banks = [k.psum.take() for _ in range(4)]
    acts = {}

    def gate_up(c):
        bank, free = k.psum.take()
        for half in (0, 1):
            hi, lo, m = k.staged(("gu", c), half)
            for kt in range(8):
                s = slice(kt * 128, kt * 128 + 128)
                d = k.mm3(bank[:, half * 256:half * 256 + 256], (hi[:, s], lo[:, s]), (k.hh[:, kt, :], k.hl[:, kt, :]),
                          kt == 0, kt == 7, m, free, hm, signal=kt == 7)
            k.unstage(hi, lo, d)
        k.hread = d
        y, yf = ys.take()
        m = conv_taps(k, y[:, :], bank, 0, taps[:, c * 3:c * 3 + 3], 3, d, yf)
        g, gf = gs.take()
        a = k.fn(g[:, :], y[:, :], ACT.Silu, m, gf)
        ys.give(y, a)
        f, ff = ams.take()
        m = k.tt(f[:, :], g[:, :], bank[:, 256:512], ALU.mult, a, d, ff)
        k.psum.give(bank, m)
        gs.give(g, m)
        (ah, al), af = aps.take()
        a = k.acp(ah[:, :], f[:, :], m, af)
        m = k.tt(al[:, :], f[:, :], ah[:, :].bitcast(F32), ALU.subtract, a, m, af)
        ams.give(f, m)
        acts[c] = (ah, al, m)

    def down(c):
        ah, al, am = acts.pop(c)
        hi, lo, m = k.staged(("wd", c // 2), c % 2)
        for t in (0, 1):
            for nh in (0, 1):
                s = slice(nh * 512, nh * 512 + 512)
                q = slice(t * 128, t * 128 + 128)
                bank, free = banks[t * 2 + nh]
                d = k.mm3(bank[:, :], (ah[:, q], al[:, q]), (hi[:, s], lo[:, s]), c == 0, c == 21, m, am, free,
                          signal=t == 1 and nh == 1)
        k.unstage(hi, lo, d)
        aps.give((ah, al), d)
        k.sumsmark = d

    for c in range(23):
        if c < 22:
            gate_up(c)
        k.tick()
        if c >= 1:
            down(c - 1)
        k.tick()
    k.sums = [b for b, _ in banks]
    k.add_sums()
    ss = k.col(2)
    ms = [k.fn(xn[:, t, :], k.x[:, t, :], ACT.Square, k.xmarks[t], k.xnread, accum=ss[:, t:t + 1]) for t in (0, 1)]
    r, m = k.rstd(ss, 2, 1.0 / 1024, ms)
    for t in (0, 1):
        xs = k.x[:, t, :]
        k.xnew.append((t, k.stt(xs, xs, r[:, t:t + 1], lnf[:, :], ALU.mult, ALU.mult, m, lm, k.xmarks[t])))
    k.settle()


def modulation(k, layer, accs, rows, gates):
    ones = k.cst("ones")
    for v in range(6):
        acc, free = accs.take()
        for s in range(4):
            w, load, slot = k.piece(("ada", layer, v, s))
            for kk in (0, 1):
                kt = 2 * s + kk
                part, scalar = w[:, kk * 1024:kk * 1024 + 1024], k.csil[:, kt:kt + 1]
                if kt == 0:
                    m = k.ts(acc[:, :], part, scalar, ALU.mult, load, free, k.csilm)
                else:
                    m = k.stt(acc[:, :], part, scalar, acc[:, :], ALU.mult, ALU.add, m, load)
                yield
            k.piece_done(slot, m)
        if v in (2, 5):
            r = (layer * 2 + v // 5) * 32
            for nh in (0, 1):
                n = slice(nh * 512, nh * 512 + 512)
                bank, free = k.psum.take()
                k.mm(bank[:, :], ones, acc[:, n], True, False, m, free)
                d = k.mm(bank[:, :], ones[r:r + 1, :], rows[r:r + 1, n], False, True, k.rowsm, signal=True)
                a = k.acp(gates[v // 5][:, n], bank[:, :], d, k.gatefree[layer])
                k.psum.give(bank, a)
            k.gate[layer, v // 5] = (gates[v // 5], a)
        else:
            i = (0, 1, None, 2, 3)[v]
            bank, free = k.psum.take()
            for j in range(8):
                d = k.mm(bank[:, j:j + 1], acc[:, j * 128:j * 128 + 128], ones[:, 0:1], True, True, m, free, signal=j == 7)
            c = k.col(8)
            o = (layer * 4 + i) * 8
            mc = k.tt(c, bank[:, 0:8], k.cst("adab")[:, o:o + 8], ALU.add, d)
            k.psum.give(bank, mc)
            if v in (0, 3):
                k.shift[layer, v // 3] = (c, mc)
            else:
                g = k.col(8)
                gain = k.cst("nmix" if v == 1 else "nffn")[:, layer * 8:layer * 8 + 8]
                k.gain[layer, v // 3] = (g, k.stt(g, c, 1.0, gain, ALU.add, ALU.mult, mc))
        accs.give(acc, d)
        yield


def load_bias(k, bias, rounds, src, step, first, mark, fence):
    corner = again(k.cst("corner"), 4, 256)
    marks = []
    for g in range(bias.shape[1] // 4):
        w, count, free = rounds[g % len(rounds)]
        at = bass.AP(tensor=src.tensor, offset=g * 4 * step + first, ap=[[1, 128], [step, 4], [1, 256]])
        m = k.act.dma(lambda e, w=w, at=at: e.dma_start(w[:, :, :], at), count, mark, fence, free)
        yield
        yield
        m = k.tt(bias[:, g * 4:g * 4 + 4, :], corner, w[:, :, 255::-1], ALU.subtract, m, fence)
        rounds[g % len(rounds)] = (w, count, [m])
        marks.append(m)
    k.biasm = marks


def second_mixer(k, layer, at, end):
    def room(*shape, dt=F32):
        nonlocal at
        t = k.sb([128, *shape], at, dt)
        at += int(np.prod(shape)) * 4
        return t

    fence = k.fence
    mul, add, sub = ALU.mult, ALU.add, ALU.subtract
    bias = k.bias[layer]
    xnat = at
    qTs = Turns([room(2, 256) for _ in range(2)])
    kTs = Turns([room(2, 256) for _ in range(2)])
    vs = Turns([room(2, 256) for _ in range(2)])
    xn = k.sb([128, 2, 1024], xnat)
    tmps = [room(512) for _ in range(2)]
    tmp = Turns(tmps)
    sqs = Turns([room(512) for _ in range(2)])
    ns = Turns([room(512) for _ in range(2)])
    Ss = Turns([room(384) for _ in range(6 if layer == 0 else 3)])
    PTs = Turns([room(384) for _ in range(3)])
    assert at <= end, (at, end)
    for lane in (k.dve, k.act, k.pool):
        lane.wait(fence)
    hm = k.front(k.gain[layer, 0], k.shift[layer, 0], xn, [], tmp, [k.hread])
    gcol = k.col(2)
    gains = k.cst("qk")[:, layer * 2:layer * 2 + 2]
    k.ts(gcol[:, 0:1], gains[:, 0:1], -0.125, mul)
    gm = k.cp(gcol[:, 1:2], gains[:, 1:2])
    parts = (slice(0, 128), slice(128, 384))

    def qk_piece(g, store, which):
        def then(bank, d):
            sq, f = sqs.take()
            a = k.fn(sq[:, :], bank[:, :], ACT.Square, d, f)
            ss = k.col(8)
            m = k.red(ss, blocks(sq[:, :], 64), add, a)
            sqs.give(sq, m)
            r, m = k.rstd(ss, 8, 1.0 / 64, m)
            n, f = ns.take()
            m = k.tt(blocks(n[:, :], 64), blocks(bank[:, :], 64), spread(r, 8, 64), mul, m, d, f)
            k.psum.give(bank, m)
            yield
            b2, free = k.psum.take()
            for j in (0, 1):
                for t in (0, 1):
                    o = (j * 2 + t) * 128
                    d = k.tr(b2[:, o:o + 128], n[:, t * 256 + j * 128:t * 256 + j * 128 + 128], m, free,
                             signal=j == 1 and t == 1)
            ns.give(n, d)
            dest, f = (qTs, kTs)[which].take()
            a = k.acp(dest[:, :, :], blocks(b2[:, :], 256), d, f, gm, k.xnread, scale=gcol[:, which:which + 1])
            k.psum.give(b2, a)
            store[which] = (dest, a)
            yield
        return then

    def v_piece(g, store):
        def then(bank, d):
            v, f = vs.take()
            a = k.acp(v[:, :, :], blocks(bank[:, :], 256), d, f, k.xnread)
            k.psum.give(bank, a)
            store[2] = (v, a)
            yield
        return then

    ym = {}

    def weights(store, j, r, head):
        (q, qm), (kk, km) = store[0], store[1]
        rows = slice(64 * r, 64 * r + 64)
        bank, free = k.psum.take()
        k.mm(bank[:, 0:128], q[rows, j, 0:128], kk[rows, j, 0:128], True, True, qm, km, free)
        d = k.mm(bank[:, 128:384], q[rows, j, 128:256], kk[rows, j, :], True, True, signal=True)
        S, f = Ss.take()
        nm, den, inv = k.col(2), k.col(2), k.col(2)
        windows = (bias[:, head, 128:256], bias[:, head, :])
        ms = [k.ttr(S[:, p], bank[:, p], windows[i], add, ALU.min, FAR * 4, nm[:, i:i + 1], d, f, k.biasm)
              for i, p in enumerate(parts)]
        k.psum.give(bank, ms[1])
        es = [k.fn(S[:, p], S[:, p], ACT.Exp, ms[i], bias=nm[:, i:i + 1], scale=-1.0, accum=den[:, i:i + 1])
              for i, p in enumerate(parts)]
        return S, inv, k.rec(inv, den, es)

    def turned(S, m):
        bank, free = k.psum.take()
        for j in range(3):
            d = k.tr(bank[:, j * 128:j * 128 + 128], S[:, j * 128:j * 128 + 128], m, free, signal=j == 2)
        Ss.give(S, d)
        PT, f = PTs.take()
        a = k.acp(PT[:, :], bank[:, 0:384], d, f)
        k.psum.give(bank, a)
        return PT, a

    def single(g, store):
        state = {}

        def scores(i):
            S, inv, rv = weights(store, i // 2, i % 2, g * 4 + i)
            for j, p in enumerate(parts):
                m = k.ts(S[:, p], S[:, p], inv[:, j:j + 1], mul, rv)
            state[i] = (S, m)

        def values(i):
            PT, a = state.pop(i)
            v, vm = store[2]
            r = slice(64 * (i % 2), 64 * (i % 2) + 64)
            if i % 2 == 0:
                state["out"] = k.psum.take()
            bank, free = state["out"]
            c = slice(i * 64, i * 64 + 64)
            k.mm(bank[r, 0:256], v[:, 0, c], PT[:, 0:256], True, False, a, vm, free)
            d = k.mm(bank[r, 128:256], v[:, 1, c], PT[:, 256:384], False, True, signal=True)
            PTs.give(PT, d)
            if i % 2 == 1:
                kt = 2 * g + i // 2
                a = k.acp(k.yh[:, kt, :], bank[:, 0:256], d, k.yread)
                m = k.tt(k.yl[:, kt, :], bank[:, 0:256], k.yh[:, kt, :].bitcast(F32), sub, a)
                k.psum.give(bank, m)
                ym[kt] = m
            return d

        for i in range(6):
            if i < 4:
                scores(i)
            if 1 <= i <= 4:
                state[i - 1] = turned(*state[i - 1])
            if i >= 2:
                d = values(i - 2)
            yield
        for turns, (t, _) in zip((qTs, kTs, vs), (store[0], store[1], store[2])):
            turns.give(t, d)

    def double(g, store):
        state = {}

        def scores(i):
            S0, inv0, r0 = weights(store, i, 0, 2 * g + i)
            S1, inv1, r1 = weights(store, i, 1, 2 * g + i)
            c1 = k.col(2)
            cm = k.ts(c1, inv1, k.neglam, mul, r1, k.neglamm)
            for j, p in enumerate(parts):
                m = k.ts(S1[:, p], S1[:, p], c1[:, j:j + 1], mul, cm)
                m = k.stt(S0[:, p], S0[:, p], inv0[:, j:j + 1], S1[:, p], mul, add, m, r0)
            Ss.give(S1, m)
            state[i] = (S0, m)

        def values(i):
            PT, a = state[i]
            v, vm = store[2]
            c = slice(i * 128, i * 128 + 128)
            bank, free = k.psum.take()
            k.mm(bank[:, 0:128], PT[:, 0:128], v[:, 0, c], True, True, a, vm, free)
            k.mm(bank[:, 128:256], PT[:, 128:256], v[:, 0, c], True, False)
            d = k.mm(bank[:, 128:256], PT[:, 256:384], v[:, 1, c], False, True, signal=True)
            PTs.give(PT, d)
            sq, f = sqs.take()
            a = k.fn(sq[:, 0:256], bank[:, 0:256], ACT.Square, d, f)
            ss = k.col(2)
            m = k.red(ss, blocks(sq[:, 0:256], 128), add, a)
            r, m = k.rstd(ss, 2, 1.0 / 128, m)
            m = k.tt(blocks(sq[:, 0:256], 128), blocks(bank[:, 0:256], 128), spread(r, 2, 128), mul, m)
            k.psum.give(bank, m)
            state[i] = (sq, m)
            return d

        def out(i):
            o, m = state.pop(i)
            bank, free = k.psum.take()
            for t in (0, 1):
                d = k.tr(bank[:, t * 128:t * 128 + 128], o[:, t * 128:t * 128 + 128], m, free, signal=t == 1)
            f, ff = tmp.take()
            m = k.ts(f[:, 0:256], bank[:, 0:256], k.cst("subln"), mul, d, ff, s2=1.0 - LAMBDA_INIT, op1=mul)
            k.psum.give(bank, m)
            sqs.give(o, d)
            kt = 2 * g + i
            a = k.acp(k.yh[:, kt, :], f[:, 0:256], m, k.yread)
            m = k.tt(k.yl[:, kt, :], f[:, 0:256], k.yh[:, kt, :].bitcast(F32), sub, a, m)
            tmp.give(f, m)
            ym[kt] = m

        for i in range(5):
            if i < 2:
                scores(i)
            if 1 <= i <= 2:
                state[i - 1] = turned(*state[i - 1])
            if 2 <= i <= 3:
                d = values(i - 2)
            if i >= 3:
                out(i - 3)
            yield
        for turns, (t, _) in zip((qTs, kTs, vs), (store[0], store[1], store[2])):
            turns.give(t, d)

    for g in range(4):
        store = {}
        k.run(k.token_major(("aq", layer, g), qk_piece(g, store, 0), hm))
        k.run(k.token_major(("ak", layer, g), qk_piece(g, store, 1), hm))
        k.run(k.token_major(("av", layer, g), v_piece(g, store), hm))
        k.tick()
        k.tick()
        k.start((double if layer == 0 else single)(g, store))
    k.drain()
    k.run(k.project(("ao", layer), range(4), (k.yh, k.yl), lambda kt: ym[kt]))
    k.add_sums(k.gate[layer, 0], tmp)


SLOTS = 64
EXTRA = 7


def experts(k, layer, at, end, last):
    def room(*shape, dt=F32):
        nonlocal at
        t = k.sb([128, *shape], at, dt)
        at += int(np.prod(shape)) * 4
        return t

    mul, add, sub, eq = ALU.mult, ALU.add, ALU.subtract, ALU.is_equal
    cst, ones, ident = k.cst, k.cst("ones"), k.ident
    fence = k.fence
    gain, shift = k.gain[layer, 1], k.shift[layer, 1]
    hgat = at
    hg = [room(8, 256) for _ in range(2)]
    hgfree = [[], []]
    xn, hT = k.sb([128, 2, 1024], hgat), k.sb([128, 8, 256], hgat + 8192)
    sgs = Turns([room(512) for _ in range(2)])
    acs = Turns([room(512) for _ in range(2)])
    aTs = Turns([room(512) for _ in range(2)])
    rt = room(24, 32)
    GS = room(8)
    M3 = room(2, 48)
    ov = room(96)
    number = k.sb([1, 16], at, I32); at += 64
    huat = at
    assert at <= end, (at, end)
    xh, xl = k.sb([128, 2, 1024], k.hhat, F32R), k.sb([128, 2, 1024], k.hlat, F32R)
    P = k.sb([128, 2, 1024], k.yhat, F32R)
    PT = k.sb([128, 8, 256], k.ylat, F32R)
    for lane in (k.dve, k.act, k.pool):
        lane.wait(fence)

    xm = k.norm_x(xn, [])
    xs = []
    for t in (0, 1):
        a = k.acp(xh[:, t, :], xn[:, t, :], xm[t], k.hread)
        xs.append(k.tt(xl[:, t, :], xn[:, t, :], xh[:, t, :].bitcast(F32), sub, a, xm[t], k.hread))
    for j in range(4):
        bank, free = k.psum.take()
        for kk in (0, 1):
            for t in (0, 1):
                o, c = (kk * 2 + t) * 128, (2 * j + kk) * 128
                d = k.tr(bank[:, o:o + 128], xn[:, t, c:c + 128], free, xm, signal=kk == 1 and t == 1)
        for kk in (0, 1):
            kt = 2 * j + kk
            hm = k.ts(hT[:, kt, :], bank[:, kk * 256:kk * 256 + 256], gain[0][:, kt:kt + 1], mul, d, gain[1], shift[1],
                      s2=shift[0][:, kt:kt + 1], op1=add)
        k.psum.give(bank, hm)
    xnread = [d, xs]
    bank, free = k.psum.take()
    for t in (0, 1):
        for kt in range(8):
            d = k.mm(bank[:, t * 16:t * 16 + 16], hT[:, kt, t * 128:t * 128 + 128], cst("rw")[:, kt * 16:kt * 16 + 16],
                     kt == 0, kt == 7, hm, free, signal=t == 1 and kt == 7)
    hTread = d
    n = iter(range(24))
    r = lambda w=32: rt[:, next(n), 0:w]
    sc, sel, gates, M, posm = r(), r(), r(), r(), r()
    z, a, b, c, d4, gs, g2 = r(), r(8), r(8), r(8), r(8), r(8), r(8)
    top, key, ktop = r(2), r(), r(2)
    m = k.fn(z, bank[:, 0:32], ACT.Exp, d, scale=-1.0)
    k.psum.give(bank, m)
    m = k.ts(z, z, 1.0, add, m)
    m = k.rec(sc, z, m)
    m = k.tt(blocks(sel, 16), blocks(sc, 16), again(cst("rbias"), 2, 16), add, m)
    s4 = blocks(sel, 4)
    k.tt(a, s4[:, :, 0], s4[:, :, 1], ALU.max, m)
    k.tt(b, s4[:, :, 0], s4[:, :, 1], ALU.min)
    k.tt(c, s4[:, :, 2], s4[:, :, 3], ALU.max)
    m = k.tt(d4, s4[:, :, 2], s4[:, :, 3], ALU.min)
    k.tt(gs, a, c, ALU.max, m)
    k.tt(g2, a, c, ALU.min)
    m = k.tt(b, b, d4, ALU.max)
    m = k.tt(g2, g2, b, ALU.max, m)
    m = k.tt(gs, gs, g2, add, m)

    def first_best(values, w, weight, hit, m):
        m = k.red(top, blocks(values, w), ALU.max, m)
        m = k.tt(blocks(hit, w), blocks(values, w), spread(top, 2, w), eq, m)
        m = k.tt(key[:, 0:2 * w], hit, weight, mul, m)
        m = k.red(ktop, blocks(key[:, 0:2 * w], w), ALU.max, m)
        return k.tt(blocks(hit, w), blocks(key[:, 0:2 * w], w), spread(ktop, 2, w), eq, m)

    m = first_best(gs, 4, cst("w4"), a, m)
    mk, pen = r(), r(8)
    k.tt(blocks(mk, 4), s4, spread(a, 8, 4), mul, m)
    m = k.ts(pen, a, -1.0, add, m, s2=FAR, op1=mul)
    m = k.tt(blocks(mk, 4), blocks(mk, 4), spread(pen, 8, 4), add, m)
    one, two = r(), r()
    m = first_best(mk, 16, cst("w16"), one, m)
    m = k.stt(mk, one, -4 * FAR, mk, mul, add, m)
    m = first_best(mk, 16, cst("w16"), two, m)
    Mm = k.tt(M, one, two, add, m)
    w, ws, wi = r(), r(2), r(2)
    m = k.tt(w, sc, M, mul, Mm)
    m = k.red(ws, blocks(w, 16), add, m)
    m = k.rec(wi, ws, m)
    gm = k.tt(blocks(gates, 16), blocks(w, 16), spread(wi, 2, 16), mul, m)
    bank, free = k.psum.take()
    k.mm(bank[:, 0:16], cst("stri"), M[:, 0:16], True, True, Mm, free)
    k.mm(bank[:, 16:32], cst("stri"), M[:, 16:32], True, False)
    d = k.mm(bank[:, 16:32], ones, M[:, 0:16], False, True, signal=True)
    m = k.stt(posm, bank[:, 0:32], 1.0, M, add, mul, d)
    k.psum.give(bank, m)
    posmm = k.ts(posm, posm, -1.0, add, m)
    pm = [k.tt(blocks(P[:, t, :], 64), again(cst("iota"), 16, 64), spread(posm[:, t * 16:t * 16 + 16], 16, 64), eq, posmm,
               k.yread) for t in (0, 1)]

    def gather(q):
        dest, made = hg[q % 2], []
        for j in range(4):
            bank, free = k.psum.take()
            for kk in (0, 1):
                c = slice((2 * j + kk) * 128, (2 * j + kk) * 128 + 128)
                for t in (0, 1):
                    for part in (xh, xl):
                        d = k.mm(bank[:, kk * 256:kk * 256 + 256], part[:, t, c], P[:, t, q * 256:q * 256 + 256],
                                 t == 0 and part is xh, t == 1 and part is xl, pm, xs, free,
                                 signal=kk == 1 and t == 1 and part is xl)
            wait = [d, xnread, hTread, hgfree[q % 2], gain[1], shift[1]]
            for kk in (0, 1):
                kt = 2 * j + kk
                src, g, s = bank[:, kk * 256:kk * 256 + 256], gain[0][:, kt:kt + 1], shift[0][:, kt:kt + 1]
                if j % 2:
                    m = k.fn(dest[:, kt, :], src, ACT.Identity, wait, scale=g, bias=s)
                else:
                    m = k.ts(dest[:, kt, :], src, g, mul, wait, s2=s, op1=add)
            k.psum.give(bank, m)
            made.append(m)
        return made

    hgm = gather(0)
    ptm = []
    for i in range(4):
        bank, free = k.psum.take()
        for pp in (0, 1):
            p = 2 * i + pp
            for t in (0, 1):
                o = (pp * 2 + t) * 128
                d = k.tr(bank[:, o:o + 128], P[:, t, p * 128:p * 128 + 128].bitcast(F32), free, pm,
                         signal=pp == 1 and t == 1)
        ptm.append(k.acp(PT[:, 2 * i:2 * i + 2, :], blocks(bank[:, :], 256), d, k.yread))
        k.psum.give(bank, ptm[-1])
    bank, free = k.psum.take()
    for p in range(8):
        for t in (0, 1):
            d = k.mm(bank[:, p * 16:p * 16 + 16], P[:, t, p * 128:p * 128 + 128].bitcast(F32),
                     gates[:, t * 16:t * 16 + 16], t == 0, t == 1, gm, pm, free, signal=p == 7 and t == 1)
    k.cp(GS[0:64, :], bank[0:64, 0:127:18], d)
    gsm = k.cp(GS[64:128, :], bank[64:128, 1:128:18], d)
    k.psum.give(bank, gsm)

    ind, rank, T8 = ov[0:48, 0:1], ov[0:48, 1:2], ov[0:48, 2:10]
    m = [k.cp(blocks(M3[:, t, :], 16), again(M[:, t * 16:t * 16 + 16], 3, 16), Mm) for t in (0, 1)]
    bank, free = k.psum.take()
    for t in (0, 1):
        d = k.mm(bank[0:48, 0:1], M3[:, t, :], ones[:, 0:1], t == 0, t == 1, m, free, signal=t == 1)
    m = k.tt(ind, bank[0:48, 0:1], cst("cut")[0:48, :], ALU.is_gt, d)
    d = k.mm(bank[0:48, 1:2], cst("stri")[0:48, 0:48], ind, True, True, m, signal=True)
    m = k.cp(rank, bank[0:48, 1:2], d)
    m = k.ts(T8, cst("iota")[0:48, 0:8], rank, eq, m, s2=ind, op1=mul)
    k.mm(bank[0:1, 2:3], ind, ones[0:48, 0:1], True, True, m)
    d = k.mm(bank[0:1, 8:16], cst("where")[0:48, :], T8, True, True, m, signal=True)
    k.cp(number[0:1, 0:1], bank[0:1, 2:3], d)
    nm = k.cp(number[0:1, 1:9], bank[0:1, 8:16], d)
    k.psum.give(bank, nm)

    sums = [k.psum.take() for _ in range(4)]
    base = len(k.order)
    ys = {}

    def gate_up(p):
        (G, gf), (U, uf) = k.psum.take(), k.psum.take()
        h = hg[(p // 2) % 2]
        for s in range(4):
            ws = [k.piece(("mu", layer, 2 * p + j, s)) for j in (0, 1)]
            for kk in (0, 1):
                kt = 2 * s + kk
                for out, free, c in ((G, gf, 0), (U, uf, 512)):
                    for j in (0, 1):
                        w, load, slot = ws[j]
                        o = ((2 * p + j) % 4) * 64
                        d = k.mm(out[64 * j:64 * j + 64, :], h[:, kt, o:o + 64], w[:, kk * 1024 + c:kk * 1024 + c + 512],
                                 kt == 0, kt == 7, load, free, hgm, signal=kk == 1 and c == 512 and j == 1)
            for j in (0, 1):
                k.piece_done(ws[j][2], d)
        hgfree[(p // 2) % 2] = [d]
        sg, f = sgs.take()
        a = k.fn(sg[:, :], G[:, :], ACT.Silu, d, f)
        k.psum.give(G, a)
        ac, f = acs.take()
        m = k.tt(ac[:, :], sg[:, :], U[:, :], mul, a, f, d)
        k.psum.give(U, m)
        sgs.give(sg, m)
        ys[p] = (ac, m)

    def down(p):
        ac, m = ys[p]
        bank, free = k.psum.take()
        for c in range(4):
            d = k.tr(bank[:, c * 128:c * 128 + 128], ac[:, c * 128:c * 128 + 128], m, free, signal=c == 3)
        acs.give(ac, d)
        aT, f = aTs.take()
        am = k.acp(aT[:, :], bank[:, :], d, f)
        k.psum.give(bank, am)
        ds = [k.psum.take() for _ in (0, 1)]
        for s in (0, 1):
            ws = [k.piece(("md", layer, 2 * p + j, s)) for j in (0, 1)]
            for kk in (0, 1):
                c = 2 * s + kk
                for nh in (0, 1):
                    for j in (0, 1):
                        w, load, slot = ws[j]
                        d = k.mm(ds[nh][0][64 * j:64 * j + 64, :], aT[:, c * 128 + 64 * j:c * 128 + 64 * j + 64],
                                 w[:, kk * 1024 + nh * 512:kk * 1024 + nh * 512 + 512], c == 0, c == 3, load, am, ds[nh][1],
                                 signal=kk == 1 and nh == 1 and j == 1)
            for j in (0, 1):
                k.piece_done(ws[j][2], d)
        aTs.give(aT, d)
        (yh, yl), f = k.stages.take()
        for nh in (0, 1):
            n_ = slice(nh * 512, nh * 512 + 512)
            a = k.acp(yh[:, n_], ds[nh][0][:, :], d, f, gsm, scale=GS[:, p:p + 1])
            m = k.stt(yl[:, n_], ds[nh][0][:, :], GS[:, p:p + 1], yh[:, n_].bitcast(F32), mul, sub, a, f, d)
            k.psum.give(ds[nh][0], m)
        ys[p] = (yh, yl, m)

    def scatter(p):
        yh, yl, m = ys.pop(p)
        for t in (0, 1):
            for nh in (0, 1):
                for part in (yh, yl):
                    bank, free = sums[t * 2 + nh]
                    d = k.mm(bank[:, :], PT[:, p, t * 128:t * 128 + 128], part[:, nh * 512:nh * 512 + 512],
                             p == 0 and part is yh, p == 7 and part is yl, m, ptm, free,
                             signal=t == 1 and nh == 1 and part is yl)
        k.stages.give((yh, yl), d)
        return d

    for p in range(8):
        gate_up(p)
        if p % 2 == 1 and p < 7:
            hgm = gather(p // 2 + 1)
        if p:
            scatter(p - 1)
        down(p)
    d = scatter(7)
    k.hread = k.yread = d

    lanes = (k.pe, k.act, k.dve, k.sp)
    counts = [Count(k.nc, f"more{layer}{i}") for i in range(4)]
    loads = [Count(k.nc, f"moreload{layer}{i}") for i in range(2)]
    wbuf = [k.sb([128, 2048], hgat + 8192 * i) for i in range(2)]
    wfree = [[d], [d]]
    hu, Pu, PTu, yu = (k.sb([128, 512], huat), k.sb([128, 2, 64], huat + 2048), k.sb([128, 256], huat + 2560),
                       k.sb([128, 1024], huat + 3584))
    tab, pu, gu, gsu = (k.sb([128, 32], huat + 7680), k.sb([128, 32], huat + 7808), k.sb([128, 32], huat + 7936),
                        k.sb([128, 32], huat + 8064))
    assert huat + 8192 <= end
    ac, aT, sg = (t.free[0][0] for t in (acs, aTs, sgs))
    tail = [d, [f for t in (acs, aTs, sgs) for _, f in t.free]]
    spare = [b for b, _ in k.psum.free][0:4]
    tail.append([f for _, f in k.psum.free])
    lists = [[] for _ in lanes]
    for u in range(EXTRA):
        for lane, count in zip(lanes, counts):
            lane.open(count)
        b0, b1, b2, b3 = spare
        d = k.mm(b0[:, 0:17], T8[:, u:u + 1].to_broadcast([48, 128]), cst("unit")[0:48, :], True, True, tail, nm, signal=True)
        m = k.cp(tab[:, 0:17], b0[:, 0:17], d, tail)
        for src, out in ((posm, pu), (gates, gu)):
            q = k.tt(blocks(yu[:, 0:32], 16), blocks(src, 16), again(tab[:, 0:16], 2, 16), mul, m, gm, posmm)
            m = k.red(out[:, 0:2], blocks(yu[:, 0:32], 16), add, q)
        m = k.ts(pu[:, 0:2], pu[:, 0:2], tab[:, 16:17], sub, m)
        pum = k.tt(Pu[:, :, :], again(cst("iota"), 2, 64), spread(pu[:, 0:2], 2, 64), eq, m)
        for kt in range(8):
            for t in (0, 1):
                for part in (xh, xl):
                    d = k.mm(b1[:, kt * 64:kt * 64 + 64], part[:, t, kt * 128:kt * 128 + 128].bitcast(F32), Pu[:, t, :],
                             t == 0 and part is xh, t == 1 and part is xl, pum, signal=kt == 7 and t == 1 and part is xl)
        for t in (0, 1):
            k.tr(b2[0:64, t * 128:t * 128 + 128], Pu[:, t, :])
        for t in (0, 1):
            d = k.mm(b2[0:64, 256:257], Pu[:, t, :], gu[:, t:t + 1], t == 0, t == 1, signal=t == 1)
        m = k.tt(blocks(hu[:, :], 64), blocks(b1[:, :], 64), spread(gain[0], 8, 64), mul, d)
        hum = k.tt(blocks(hu[:, :], 64), blocks(hu[:, :], 64), spread(shift[0], 8, 64), add, m)
        k.cp(PTu[0:64, :], b2[0:64, 0:256], d)
        ptum = k.cp(gsu[0:64, 0:1], b2[0:64, 256:257], d)
        ws = []
        for s in range(6):
            slot = s % 2

            def fetch(e, s=s, u=u, slot=slot):
                i = e.value_load(number[0:1, 1 + u:2 + u], min_val=0, max_val=85)
                src = k.weights[bass.ds(i + (base + 2 * s), 1), :, :].rearrange("a p n -> p (a n)")
                return e.dma_start(wbuf[slot][:, :], src)

            lm = k.sp.dma(fetch, loads[slot], nm, tail, wfree[slot])
            if s < 4:
                for kk in (0, 1):
                    kt = 2 * s + kk
                    for out, c in ((b0, 0), (b3, 512)):
                        d = k.mm(out[0:64, :], hu[:, kt * 64:kt * 64 + 64], wbuf[slot][:, kk * 1024 + c:kk * 1024 + c + 512],
                                 kt == 0, kt == 7, lm, hum, signal=kk == 1 and c == 512)
                if s == 3:
                    a = k.fn(sg[0:64, :], b0[0:64, :], ACT.Silu, d)
                    m = k.tt(ac[0:64, :], sg[0:64, :], b3[0:64, :], mul, a)
                    for c in range(4):
                        t4 = k.tr(b1[:, c * 64:c * 64 + 64], ac[0:64, c * 128:c * 128 + 128], m, signal=c == 3, rows=64)
                    atm = k.cp(aT[:, 0:256], b1[:, 0:256], t4)
            else:
                for kk in (0, 1):
                    c = 2 * (s - 4) + kk
                    for nh, out in ((0, b0), (1, b3)):
                        d = k.mm(out[0:64, :], aT[:, c * 64:c * 64 + 64],
                                 wbuf[slot][:, kk * 1024 + nh * 512:kk * 1024 + nh * 512 + 512], c == 0, c == 3, lm, atm,
                                 signal=kk == 1 and nh == 1)
            wfree[slot] = [d]
        for nh, out in ((0, b0), (1, b3)):
            m = k.ts(yu[0:64, nh * 512:nh * 512 + 512], out[0:64, :], gsu[0:64, 0:1], mul, d, ptum)
        for t in (0, 1):
            for nh in (0, 1):
                bank, _ = sums[t * 2 + nh]
                d = k.mm(bank[:, :], PTu[0:64, t * 128:t * 128 + 128], yu[0:64, nh * 512:nh * 512 + 512], False, True, m,
                         signal=t == 1 and nh == 1)
        tail = [d]
        for lane in lanes:
            lane.wait(d)
        for i, lane in enumerate(lanes):
            lists[i].append(lane.close())
    for lane, inner in zip(lanes, lists):
        lane.wait(nm)
        lane.branch(number[0:1, 0:1], inner)
    k.sums, k.sumsmark = [b for b, _ in sums], k.yread
    k.add_sums(k.gate[layer, 1], sgs)
    k.fence = k.marks()


def mixer_halves(layer):
    keys = [(n, layer, g) for g in range(4) for n in ("aq", "ak", "av")] + [("ao", layer, j) for j in range(4)]
    return [(key, half) for key in keys for half in (0, 1)]


def first_halves():
    keys = ([(s, p) for s in "qkvz" for p in (0, 1)] + [(s, p) for p in (0, 1) for s in ("qb", "kb", "vb")]
            + [("wo", j) for j in (2, 3, 0, 1)])
    seq = [(key, half) for key in keys for half in (0, 1)]
    for c in range(23):
        if c < 22:
            seq += [(("gu", c), 0), (("gu", c), 1)]
        if c >= 1:
            seq.append((("wd", (c - 1) // 2), (c - 1) % 2))
    return seq


def setup(k, io, at):
    nc = k.nc
    k.csil = k.col(8)
    k.csilm = k.fn(k.csil, k.cst("c"), ACT.Silu, k.cmark)
    mul, add, sub = ALU.mult, ALU.add, ALU.subtract
    lam = k.cst("lam")
    junk, s, e, l = k.col(64), k.col(2), k.col(2), k.col(1)
    k.neglam = k.col(1)
    m = k.ttr(junk, lam[:, 0:64], lam[:, 64:128], mul, add, 0.0, s[:, 0:1], k.cmark)
    m = k.ttr(junk, lam[:, 128:192], lam[:, 192:256], mul, add, 0.0, s[:, 1:2], m)
    m = k.fn(e, s, ACT.Exp, m)
    m = k.tt(l, e[:, 1:2], e[:, 0:1], sub, m)
    k.neglamm = k.ts(k.neglam, l, -LAMBDA_INIT, add, m)
    bank, free = k.psum.take()
    d = k.mm(bank[0:8, :], k.cst("t5")[0:32, :], k.cst("hot")[0:32, :], True, True, k.cmark, free, signal=True)
    t5 = k.sb([8, 512], at)
    a = k.acp(t5[:, :], bank[0:8, :], d)
    k.psum.give(bank, a)
    count = Count(nc, "t5")
    dst = io["scratch"]
    k.t5m = k.act.dma(lambda e: e.dma_start(dst, t5[:, :]), count, a)
    k.outs.append(k.t5m)
    rows, count = k.sb([128, 1024], at + 2048), Count(nc, "rows")
    for r in range(4):
        src = io["rows"][r:r + 1, :]
        k.rowsm = k.act.dma(lambda e, r=r, src=src: e.dma_start(rows[32 * r:32 * r + 1, :], src), count)
    k.gate, k.shift, k.gain, k.gatefree, k.bias = {}, {}, {}, {0: [], 1: []}, {}
    return rows


def build(nc, io):
    k = Core(nc)
    k.weights = io["weights"]
    k.lnf = io["lnf"]
    at = LOCAL0
    k.x = k.sb([128, 2, 1024], at); at += 8192
    k.cstt = k.sb([128, NCST], at); at += (NCST * 4 + 31) // 32 * 32
    k.cols = k.sb([128, 1600], at); at += 6400
    k.colat = 0
    k.hhat = at
    k.hh = k.sb([128, 8, 256], at, F32R); at += 8192
    k.hlat = at
    k.hl = k.sb([128, 8, 256], at, F32R); at += 8192
    k.yhat = at
    k.yh = k.sb([128, 8, 256], at, F32R); at += 8192
    k.ylat = at
    k.yl = k.sb([128, 8, 256], at, F32R); at += 8192
    k.stages = Turns([(k.sb([128, 1024], at + 8192 * i, F32R), k.sb([128, 1024], at + 8192 * i + 4096, F32R))
                      for i in range(2)])
    at += 16384
    for i in range(4):
        k.add_slot(at); at += 8192
    k.ident = k.cst("ident")
    k.xnew = []
    xc, cc = Count(nc, "x"), Count(nc, "cst")
    xin, cin = io["x"], io["cst"]
    xm = k.sp.dma(lambda e: e.dma_start(k.x[:, :, :], xin), xc)
    k.xmarks = [[xm], [xm]]
    k.cmark = k.act.dma(lambda e: e.dma_start(k.cstt[:, :], cin), cc)
    for l in (k.pe, k.dve, k.act, k.pool):
        l.wait(k.cmark)
    rows = setup(k, io, at); at += 6144
    accs = Turns([k.sb([128, 1024], at + 4096 * i) for i in range(2)]); at += 8192
    gates = [k.sb([128, 1024], at + 4096 * i) for i in range(2)]; at += 8192
    gates1 = [k.sb([128, 1024], LIMIT // 32 * 32 - 8192 + 4096 * i) for i in range(2)]
    local = at
    k.f1end = LIMIT
    k.feed(first_halves() + mixer_halves(0))
    k.start(modulation(k, 0, accs, rows, gates))
    first_mixer(k, local)
    k.fence = k.marks()
    k.gatefree[1] = k.fence
    k.f2end = local + 41984
    bias0 = k.sb([128, 8, 256], k.f2end)
    bias1 = k.sb([128, 16, 256], k.f2end)
    k.bias = {0: bias0, 1: bias1}
    rounds = [(k.sb([128, 4, 256], k.f2end + 16384 + 4096 * i), Count(nc, f"window{i}"), []) for i in range(2)]
    k.start(load_bias(k, bias0, rounds, io["scratch"], 512, 128, k.t5m, k.fence))
    k.start(modulation(k, 1, accs, rows, gates1))
    first_ffn(k, local)
    k.drain()
    k.fence = k.marks()
    kept = k.colat
    second_mixer(k, 0, local, k.f2end)
    k.fence = k.marks()
    experts(k, 0, local, local + 41984, False)
    k.colat = kept
    k.feed(mixer_halves(1))
    k.start(load_bias(k, bias1, rounds, io["rel"], 513, 129, None, k.fence))
    second_mixer(k, 1, local, k.f2end)
    k.fence = k.marks()
    experts(k, 1, local, local + 41984, True)
    finish(k, io)
    return k.order


def finish(k, io):
    oc = Count(k.nc, "out")
    out = io["out"]
    m = k.sp.dma(lambda e: e.dma_start(out, k.x[:, :, :]), oc, k.xmarks[0], k.xmarks[1])
    k.sp.wait(m, *k.outs)
    assert not k.live
    with k.nc.Block() as block:
        @block.sync
        def _(e):
            k.sp.emit(e)

        @block.gpsimd
        def _(e):
            k.pool.emit(e)

        @block.scalar
        def _(e):
            k.act.emit(e)

        @block.vector
        def _(e):
            k.dve.emit(e)

        @block.tensor
        def _(e):
            k.pe.emit(e)




def _columns(w, a):
    return w[:, a:a + 256].reshape(8, 128, 2, 128).transpose(1, 2, 0, 3).reshape(128, 2048)


def _block(w, a):
    return w[:, a:a + 256].reshape(8, 128, 256).transpose(1, 0, 2).reshape(128, 2048)


def _chunk(w, c):
    return w[:, c * 128:c * 128 + 128].reshape(8, 128, 128).transpose(1, 0, 2).reshape(128, 1024)


def _rows(w, j):
    return w[j * 256:j * 256 + 256].reshape(2, 128, 1024).transpose(1, 0, 2).reshape(128, 2048)


def _piece(key, inp):
    name, n = key[0], key[1]
    w_in = inp["w_in"][0]
    if name in ("q", "k", "v"):
        return _columns(w_in, "qkv".index(name) * 512 + 256 * n)
    if name == "z":
        return _block(w_in, 1536 + 256 * n)
    if name == "qb":
        return _columns(w_in, 2056 + 256 * n)
    if name == "kb":
        return _columns(w_in, 2568 + 256 * n)
    if name == "vb":
        return _block(w_in, 3080 + 256 * n)
    if name == "wo":
        return _rows(inp["w_out"][0], n)
    if name == "gu":
        return np.concatenate([_chunk(inp["w_gate"][0], n), _chunk(inp["w_up"][0], n)], 1)
    if name == "wd":
        return _rows(inp["w_down"][0], n)
    if name in ("aq", "ak", "av"):
        w = inp["a_w_qkv_2"][0] if n == 0 else inp["b_w_qkv_2"][0]
        return _block(w, ("aq", "ak", "av").index(name) * 1024 + 256 * key[2])
    if name == "ao":
        return _rows(inp["a_w_o_2"][0] if n == 0 else inp["b_w_o_2"][0], key[2])
    if name == "ada":
        return _rows(inp["ada_w_2"][n][:, key[2] * 1024:key[2] * 1024 + 1024], key[3])
    if name == "mu":
        g, u = (inp[f"moe_w_{s}_2"][n, key[2]][key[3] * 256:key[3] * 256 + 256].reshape(2, 128, 512) for s in ("gate", "up"))
        return np.concatenate([g, u], 2).transpose(1, 0, 2).reshape(128, 2048)
    assert name == "md"
    return _rows(inp["moe_w_down_2"][n, key[2]], key[3])


def _params(inp):
    def cols(v, n):
        return v.reshape(n, 128).T

    def wide(v):
        return np.broadcast_to(v.reshape(1, -1), (128, v.size))

    def twice(v):
        return np.tile(v.reshape(64), 2)[:, None]

    out = dict(constants())
    out["ln1"], out["ln2"] = cols(inp["ln1"], 8), cols(inp["ln2"], 8)
    out["conv"] = inp["conv_qkv"][0].reshape(4, 12, 128).transpose(2, 1, 0).reshape(128, 48)
    out["fconv"] = inp["ffn_conv"][0].reshape(3, 22, 128).transpose(2, 1, 0).reshape(128, 66)
    out["alog"], out["dtb"], out["gain"] = wide(inp["a_log"]), wide(inp["dt_bias"]), wide(inp["gdn_norm"])
    out["wba"] = inp["w_in"][0][:, 2048:2056].reshape(8, 128, 8).transpose(1, 0, 2).reshape(128, 64)
    out["nmix"], out["nffn"] = cols(inp["norm_mix_g_2"], 16), cols(inp["norm_ffn_g_2"], 16)
    out["qk"] = np.concatenate([twice(inp[n]) for n in ("a_q_gain_2", "a_k_gain_2", "b_q_gain_2", "b_k_gain_2")], 1)
    out["subln"] = inp["a_subln_g_2"].reshape(128, 1)
    out["lam"] = wide(inp["a_lambda_2"])
    out["rw"] = inp["router_w_2"].reshape(8, 128, 16).transpose(1, 0, 2).reshape(128, 128)
    out["rbias"] = wide(inp["router_bias_2"])
    out["c"] = cols(inp["c_2"], 8)
    out["adab"] = inp["ada_b_2"].reshape(2, 6, 8, 128)[:, [0, 1, 3, 4]].transpose(3, 0, 1, 2).reshape(128, 64)
    out["t5"] = np.concatenate([inp["t5_bias_2"], np.zeros((96, 8), np.float32)], 0)
    return np.concatenate([out[name] for name in PLACE], 1)


def kernel(**inputs):
    import numpy as _np
    import concourse.bacc as _bacc
    from concourse import mybir as _mybir
    from concourse.bass_utils import run_bass_kernel_spmd as _run

    inp = {k: _np.asarray(v) for k, v in inputs.items()}
    arrays = {
        "x": inp["x"][0],
        "cst": _params(inp),
        "lnf": _np.broadcast_to(inp["ln_f"], (128, 1024)),
        "rows": inp["ada_b_2"].reshape(2, 6, 1024)[:, [2, 5]].reshape(4, 1024),
        "rel": inp["b_rel_bias_2"][0][:, ::-1],
        "weights": None,
    }
    nc = _bacc.Bacc("TRN2", target_bir_lowering=False, num_devices=1)
    io = {}
    for name, a in arrays.items():
        shape = [PIECES, 128, 2048] if a is None else list(a.shape)
        io[name] = nc.dram_tensor(f"in_{name}_dram", shape, _mybir.dt.float32, kind="ExternalInput").ap()
    io["scratch"] = nc.dram_tensor("scratch", [8, 512], _mybir.dt.float32, kind="Internal").ap()
    out = nc.dram_tensor("out_0_dram", [256, 1024], _mybir.dt.float32, kind="ExternalOutput").ap()
    io["x"] = io["x"].rearrange("(t p) d -> p t d", p=128)
    io["out"] = out.rearrange("(t p) d -> p t d", p=128)
    order = build(nc, io)
    arrays["weights"] = _np.stack([_piece(key, inp) for key in order])
    arrays = {f"in_{name}_dram": _np.ascontiguousarray(a) for name, a in arrays.items()}
    r = _run(nc, [arrays], core_ids=[0])
    return r.results[0]["out_0_dram"].reshape(1, 256, 1024)
```

```python
import math
from collections import deque

import numpy as np
import concourse.bass as bass
from concourse import mybir

F32 = mybir.dt.float32
F32R = mybir.dt.float32r
I32 = mybir.dt.int32
ACT = mybir.ActivationFunctionType
ALU = mybir.AluOpType
AX = mybir.AxisListType

EPS = 1e-6
LAMBDA_INIT = 0.8 - 0.6 * math.exp(-0.3 * 0)
FAR = 1e30
BASE, LIMIT = 16512, 229344
PIECE = 8192
PIECES = 14 + 4 + 33 + 48 + 2 * (16 + 96)
SLOTS = 64
KEPT, ZONE_A, ZONES = 104, 544, 864
EXTRA = 7




def _swa_tables():
    dist = np.zeros((128, 384), np.float32)
    count = np.zeros((128, 384), np.float32)
    for col in range(384):
        tile, key = (0, col) if col < 128 else (1, col - 128)
        for p in range(128):
            d = tile * 128 + p - key
            n = 0
            for window, dilation in ((128, 1), (512, 4), (2048, 16)):
                if d >= 0 and d % dilation == 0 and d // dilation <= window // dilation:
                    n += 1
            count[p, col] = n
            dist[p, col] = d if n else FAR
    return dist, count


def _t5_onehot():
    hot = np.zeros((128, 512), np.float32)
    for i in range(511):
        rel = 255 - i
        n = abs(rel)
        b = n
        if n >= 8:
            b = 8
            while b < 15 and n ** 8 >= 8 ** 8 * 128 ** (b - 8 + 1):
                b += 1
        hot[b + (16 if rel > 0 else 0), i] = 1.0
    return hot


def constants():
    i = np.arange(128)
    out = {}
    out["ident"] = np.eye(128)
    out["tri"] = (i[:, None] <= i[None, :])
    out["stri"] = (i[:, None] < i[None, :])
    out["ones"] = np.ones((128, 128))
    out["iota"] = np.broadcast_to(np.arange(64), (128, 64))
    out["mhalf"] = np.full((128, 16), -0.5)
    out["eps"] = np.full((128, 1), EPS)
    out["rowsum"] = np.broadcast_to(np.eye(8).reshape(1, 64), (128, 64))
    strict = np.where(i[:, None] < i[None, :], 0.0, -FAR)
    causal = np.where(i[:, None] <= i[None, :], 0.0, -FAR)
    out["gmask"] = np.concatenate([strict, causal], 1)
    levels = []
    for l in range(7):
        b = 1 << l
        row, colm = i[None, :], i[:, None]
        levels.append(((row // (2 * b)) == (colm // (2 * b))) & ((row // b) % 2 == 1) & ((colm // b) % 2 == 0))
    out["level"] = np.concatenate(levels, 1)
    out["dist"], out["count"] = _swa_tables()
    corner = np.zeros((128, 256))
    corner[:64, 192:] = FAR
    out["corner"] = corner
    out["hot"] = _t5_onehot()
    e, c = i % 16, i // 16 + 1
    use = i < 48
    out["cut"] = np.where(use, 64.0 * c, 0.0)[:, None]
    out["unit"] = np.concatenate([(e[:, None] == np.arange(16)) & use[:, None], np.where(use, 64.0 * c, 0.0)[:, None]], 1)
    out["where"] = np.where(use, 12 * (e // 2) + e % 2, 0)[:, None]
    out["w4"] = np.broadcast_to(np.tile(np.arange(4, 0, -1), 2), (128, 8))
    out["w16"] = np.broadcast_to(np.tile(np.arange(16, 0, -1), 2), (128, 32))
    return {k: np.ascontiguousarray(v, dtype=np.float32) for k, v in out.items()}


PARAM = dict(ln1=8, ln2=8, conv=48, fconv=66, alog=4, dtb=4, gain=128, wba=64, nmix=16, nffn=16, qk=4, subln=1,
             lam=256, rw=128, rbias=16, adab=96, t5=8)
FIRST_ONLY = ("tri", "gmask", "level", "dist", "count", "hot", "conv", "alog", "dtb", "gain", "wba", "lam", "t5",
              "rowsum")


def places():
    width = {k: v.shape[1] for k, v in constants().items()}
    width.update(PARAM)
    out, at = {}, 0
    for n in [n for n in width if n not in FIRST_ONLY] + list(FIRST_ONLY):
        out[n] = (at, width[n])
        at += width[n]
    return out, out[FIRST_ONLY[0]][0], at


PLACE, NLAST, NCST = places()




class Count:

    def __init__(self, nc, name):
        self.sem, self.n = nc.alloc_semaphore(name), 0

    def step(self, k):
        self.n += k
        return (self, self.n)


class Lane:

    def __init__(self, nc, name):
        self.count, self.items, self.met = Count(nc, "done_" + name), [], {}

    def wait(self, *marks):
        for m in marks:
            if m is None:
                continue
            if isinstance(m, list):
                self.wait(*m)
                continue
            count, value = m
            if self.met.get(count, 0) < value:
                self.met[count] = value
                self.items.append((None, count.sem, value))

    def do(self, op, *marks, signal=True):
        self.wait(*marks)
        if not signal:
            self.items.append((op, None, 0))
            return None
        self.items.append((op, self.count.sem, 1))
        return self.count.step(1)

    def dma(self, op, count, *marks):
        self.wait(*marks)
        self.items.append((op, count.sem, 16))
        return count.step(16)

    def open(self, count):
        self.kept = (self.items, self.met, self.count)
        self.items, self.met, self.count = [], dict(self.met), count

    def close(self):
        inner = self.items
        self.items, self.met, self.count = self.kept
        return inner

    def branch(self, number, lists):
        self.items.append((number, "branch", lists))

    def emit(self, e, items=None):
        for op, sem, n in self.items if items is None else items:
            if sem == "branch":
                self.nest(e, e.value_load(op, min_val=0, max_val=len(n)), n, 0)
            elif op is None:
                e.wait_ge(sem, n)
            elif sem is None:
                op(e)
            else:
                op(e).then_inc(sem, n)

    def nest(self, e, value, lists, i):
        if i < len(lists):
            with e.If(value > i):
                self.emit(e, lists[i])
                self.nest(e, value, lists, i + 1)


class Turns:

    def __init__(self, things, *marks):
        self.free = deque((t, list(marks)) for t in things)

    def take(self):
        return self.free.popleft()

    def give(self, thing, *marks):
        self.free.append((thing, list(marks)))

    def marks(self):
        return [m for _, m in self.free]


def blocks(ap, b):
    return ap.rearrange("p (a b) -> p a b", b=b)


def spread(ap, n, k):
    return ap.unsqueeze(2).to_broadcast([ap.shape[0], n, k])


def again(ap, n, k):
    return ap.unsqueeze(1).to_broadcast([ap.shape[0], n, k])




class Core:
    def __init__(self, nc):
        self.nc = nc
        self.pe, self.act, self.dve, self.pool, self.sp = (Lane(nc, n) for n in ("pe", "act", "dve", "pool", "sp"))
        self.psum = Turns([nc.alloc_psum_tensor(f"bank{i}", [128, 512], F32) for i in range(8)])
        self.names = 0
        self.order, self.slots, self.retired, self.retiring = [], deque(), [], False
        self.live, self.back, self.pace, self.credit = [], iter(()), 0.0, 0.0
        self.todo, self.ready, self.opened = deque(), deque(), {}
        self.written, self.xnew = None, []
        self.kept_at = 0

    def sb(self, shape, offset, dt=F32):
        self.names += 1
        size = int(np.prod(shape[1:])) * 4
        assert offset % 32 == 0 and BASE <= offset and offset + size <= LIMIT, (offset, size)
        return self.nc.alloc_sbuf_tensor_at(f"t{self.names}", shape, dt, offset=offset)


    def add_slot(self, offset, *marks, extra=False):
        self.slots.append(((self.sb([128, 2048], offset), Count(self.nc, f"slot{self.names}"), extra), list(marks)))

    def piece(self, key):
        slot, marks = self.slots.popleft()
        t, count, _ = slot
        src = self.weights[len(self.order)]
        self.order.append(key)
        mark = self.sp.dma(lambda e: e.dma_start(t[:, :], src), count, marks)
        return t, mark, slot

    def piece_done(self, slot, *marks):
        if slot[2] and self.retiring:
            self.retired += marks
        else:
            self.slots.append((slot, list(marks)))


    def mm(self, out, l, r, first, last, *marks, signal=False):
        return self.pe.do(lambda e: e.matmul(out, l, r, start=first, stop=last, skip_group_check=True),
                          *marks, signal=signal)

    def mm3(self, out, l, r, first, last, *marks, signal=False):
        self.mm(out, l[0], r[0], first, False, *marks)
        self.mm(out, l[0], r[1], False, False)
        return self.mm(out, l[1], r[0], False, last, signal=signal)

    def tr(self, out, in_, *marks, signal=False, rows=128):
        ident = self.ident[0:rows, 0:rows]
        return self.pe.do(lambda e: e.transpose(out, in_, ident), *marks, signal=signal)

    def fn(self, out, in_, f, *marks, bias=None, scale=None, accum=None):
        kw = {}
        if bias is not None:
            kw["bias"] = bias
        if scale is not None:
            kw["scale"] = scale
        if accum is not None:
            kw["accum_out"] = accum
        return self.act.do(lambda e: e.activation(out, in_, f, **kw), *marks)

    def acp(self, out, in_, *marks, scale=None):
        return self.fn(out, in_, ACT.Copy, *marks, scale=scale)

    def tt(self, out, a, b, op, *marks, lane=None):
        return (lane or self.dve).do(lambda e: e.tensor_tensor(out, a, b, op), *marks)

    def ts(self, out, a, s1, op0, *marks, s2=None, op1=None, lane=None):
        if op1 is None:
            return (lane or self.dve).do(lambda e: e.tensor_scalar(out, a, s1, None, op0), *marks)
        return (lane or self.dve).do(lambda e: e.tensor_scalar(out, a, s1, s2, op0, op1), *marks)

    def stt(self, out, a, s, b, op0, op1, *marks):
        return self.dve.do(lambda e: e.scalar_tensor_tensor(out, a, s, b, op0, op1), *marks)

    def ttr(self, out, a, b, op0, op1, start, accum, *marks):
        return self.dve.do(lambda e: e.tensor_tensor_reduce(out=out, in0=a, in1=b, scale=1.0, scalar=start, op0=op0,
                                                            op1=op1, accum_out=accum), *marks)

    def cp(self, out, in_, *marks, lane=None):
        return (lane or self.dve).do(lambda e: e.tensor_copy(out, in_), *marks)

    def red(self, out, in_, op, *marks):
        return self.dve.do(lambda e: e.tensor_reduce(out, in_, AX.X, op), *marks)

    def rec(self, out, in_, *marks):
        return self.dve.do(lambda e: e.reciprocal(out, in_), *marks)

    def marks(self):
        return [lane.count.step(0) for lane in (self.pe, self.act, self.dve, self.pool)]


    def zone(self, a, end, *marks):
        self.colat, self.colend = a, end
        for lane in (self.act, self.dve, self.pool):
            lane.wait(*marks)

    def col(self, n):
        a = self.colat
        self.colat += n
        assert self.colat <= self.colend, "columns"
        return self.cols[:, a:a + n]

    def keep(self, n):
        a = self.kept_at
        self.kept_at += n
        assert self.kept_at <= KEPT, "lasting columns"
        return self.cols[:, a:a + n]

    def cst(self, name):
        a, n = PLACE[name]
        return self.cstt[:, a:a + n] if a < NLAST else self.cstf[:, a - NLAST:a - NLAST + n]

    def rstd(self, ss, n, scale, *marks):
        w, free = self.newton.take()
        v, r0, a, b = (w[:, 16 * i:16 * i + n] for i in range(4))
        r = self.col(n)
        m = self.ts(v, ss, scale, ALU.mult, *marks, free, s2=EPS, op1=ALU.add, lane=self.pool)
        m = self.tt(r0, v, self.cst("mhalf")[:, 0:n], ALU.pow, m, lane=self.pool)
        m = self.tt(a, r0, r0, ALU.mult, m)
        m = self.stt(b, a, -0.5, v, ALU.mult, ALU.mult, m)
        m = self.stt(r, b, 1.5, r0, ALU.add, ALU.mult, m)
        self.newton.give(w, m)
        return r, m


    def start(self, gen, first=False):
        if first:
            self.live.insert(0, gen)
        else:
            self.live.append(gen)

    def tick(self):
        for g in list(self.live):
            if next(g, self) is self:
                self.live.remove(g)

    def drain(self):
        while self.live:
            self.tick()
            self.top()

    def half(self):
        self.tick()
        self.top()
        self.credit += self.pace
        while self.credit >= 1:
            self.credit -= 1
            next(self.back, None)

    def run(self, gen):
        for _ in gen:
            self.half()


    def feed(self, halves):
        self.todo.extend(halves)

    def top(self, most=8):
        while self.todo and self.stages.free and most:
            most -= 1
            key, half = self.todo.popleft()
            if half == 0:
                self.opened[key] = self.piece(key)
            w, load, slot = self.opened[key]
            st, free = self.stages.take()
            hi, lo, _ = st
            src = w[:, half * 1024:half * 1024 + 1024]
            m = self.acp(hi[:, :], src, load, free)
            m = self.tt(lo[:, :], src, hi[:, :].bitcast(F32), ALU.subtract, m, load, free)
            if half == 1:
                self.piece_done(slot, m)
            self.ready.append((key, half, st, m))

    def staged(self, key, half):
        k, h, st, m = self.ready.popleft()
        assert (k, h) == (key, half), (k, h, key, half)
        return st[0], st[1], m, st

    def feature_major(self, key, then, hm):
        bank, free = self.psum.take()
        for c in (0, 1):
            hi, lo, m, st = self.staged(key, c)
            for kt in range(8):
                s = slice(kt * 128, kt * 128 + 128)
                d = self.mm3(bank[:, c * 256:c * 256 + 256], (hi[:, s], lo[:, s]),
                             (self.hh[:, kt, :], self.hl[:, kt, :]), kt == 0, kt == 7, m, free, hm[kt // 2],
                             signal=kt == 7)
            self.stages.give(st, d)
            if c == 1:
                self.start(then(bank, d))
            yield
        self.hread = d

    def token_major(self, key, then, hm):
        bank, free = self.psum.take()
        for half in (0, 1):
            hi, lo, m, st = self.staged(key, half)
            for t in (0, 1):
                for kk in range(4):
                    kt = half * 4 + kk
                    s = slice(kk * 256, kk * 256 + 256)
                    q = slice(t * 128, t * 128 + 128)
                    d = self.mm3(bank[:, t * 256:t * 256 + 256], (self.hh[:, kt, q], self.hl[:, kt, q]),
                                 (hi[:, s], lo[:, s]), kt == 0 and t == 0, kt == 7, m, free, hm[kt // 2],
                                 signal=kk == 3 and t == 1)
            self.stages.give(st, d)
            if half == 1:
                self.start(then(bank, d))
            yield
        self.hread = d

    def project_open(self):
        self.sums = [self.psum.take() for _ in range(4)]

    def project(self, key, kt, half, src, mark, first, last):
        yh, yl = src
        hi, lo, m, st = self.staged(key, half)
        for t in (0, 1):
            for nh in (0, 1):
                s = slice(nh * 512, nh * 512 + 512)
                q = slice(t * 128, t * 128 + 128)
                bank, free = self.sums[t * 2 + nh]
                d = self.mm3(bank[:, :], (yh[:, q], yl[:, q]) if kt is None else (yh[:, kt, q], yl[:, kt, q]),
                             (hi[:, s], lo[:, s]), first, last, m, free, mark, signal=last or (t == 1 and nh == 1))
                if last:
                    self.sumsm[t * 2 + nh] = d
        self.stages.give(st, d)
        return d


    def squares(self, t, nh, m):
        junk, free = self.junk.take()
        a = self.fn(junk[:, :], self.x[:, t, nh * 512:nh * 512 + 512], ACT.Square, m, free,
                    accum=self.ss4[:, 2 * t + nh:2 * t + nh + 1])
        self.junk.give(junk, a)
        self.ssm.append(a)

    def open_squares(self):
        self.ss4, self.ssm = self.col(4), []

    def add_sums(self, gate=None, tmp=None, squares=True, out=None):
        if squares:
            self.open_squares()
        for t in (0, 1):
            for nh in (0, 1):
                bank, _ = self.sums[t * 2 + nh]
                done = self.sumsm[t * 2 + nh]
                s = slice(nh * 512, nh * 512 + 512)
                xs = self.x[:, t, s]
                if gate is None:
                    m = self.tt(xs, bank[:, :], xs, ALU.add, done, self.xmarks[t])
                    self.psum.give(bank, m)
                else:
                    f, free = tmp.take()
                    m = self.tt(f[:, :], bank[:, :], gate[0][:, s], ALU.mult, done, gate[1], free)
                    self.psum.give(bank, m)
                    m = self.tt(xs, f[:, :], xs, ALU.add, m, self.xmarks[t])
                    tmp.give(f, m)
                self.xnew.append((t, m))
                if squares:
                    self.squares(t, nh, m)
                if out is not None:
                    out(t, s, m)
        self.settle()

    def settle(self):
        for t in (0, 1):
            self.xmarks[t] = [m for u, m in self.xnew if u == t]
        self.xnew = []

    def scales(self):
        s2 = self.col(2)
        m = self.tt(s2, self.ss4[:, 0:4:2], self.ss4[:, 1:4:2], ALU.add, self.ssm)
        r, m = self.rstd(s2, 2, 1.0 / 1024, m)
        self.dm = [self.ts(self.diag[:, t, :], self.ident, r[:, t:t + 1], ALU.mult, m, self.dread) for t in (0, 1)]
        return r, m

    def turn_x(self, j):
        bank, free = self.psum.take()
        for kk in (0, 1):
            for t in (0, 1):
                o = (kk * 2 + t) * 128
                c = (2 * j + kk) * 128
                d = self.mm(bank[:, o:o + 128], self.x[:, t, c:c + 128], self.diag[:, t, :], True, True, free, self.dm,
                            self.xmarks, signal=kk == 1 and t == 1)
        self.dread = d
        return bank, d

    def front(self, gain, shift, tmp, hfree):
        self.scales()
        self.top(2)
        hm = []
        for j in range(4):
            bank, d = self.turn_x(j)
            pair = slice(2 * j, 2 * j + 2)
            if shift is None:
                for kk in (0, 1):
                    a = self.acp(self.hh[:, 2 * j + kk, :], bank[:, kk * 256:kk * 256 + 256], d, gain[1], hfree,
                                 scale=gain[0][:, 2 * j + kk:2 * j + kk + 1])
                for kk in (0, 1):
                    kt = 2 * j + kk
                    m = self.stt(self.hl[:, kt, :], bank[:, kk * 256:kk * 256 + 256], gain[0][:, kt:kt + 1],
                                 self.hh[:, kt, :].bitcast(F32), ALU.mult, ALU.subtract, a, d, gain[1], hfree)
                self.psum.give(bank, m)
            else:
                f, free = tmp.take()
                for kk in (0, 1):
                    kt = 2 * j + kk
                    s = slice(kk * 256, kk * 256 + 256)
                    a = self.fn(f[:, s], bank[:, s], ACT.Identity, d, free, gain[1], shift[1],
                                scale=gain[0][:, kt:kt + 1], bias=shift[0][:, kt:kt + 1])
                self.psum.give(bank, a)
                m = self.cp(self.hh[:, pair, :], blocks(f[:, :], 256), a, hfree)
                m = self.tt(self.hl[:, pair, :], blocks(f[:, :], 256), self.hh[:, pair, :].bitcast(F32), ALU.subtract, m)
                tmp.give(f, m)
            hm.append(m)
        self.top()
        return hm


def conv_taps(k, out, bank, at, taps, width, mark, free):
    m = k.acp(out[:, :], bank[:, at:at + 256], mark, free, scale=taps[:, width - 1:width])
    for j in range(1, width):
        m = k.stt(out[:, j:256], bank[:, at:at + 256 - j], taps[:, width - 1 - j:width - j], out[:, j:256],
                  ALU.mult, ALU.add, m, mark)
    return m


def first_mixer(k, base):
    at = base

    def room(*shape):
        nonlocal at
        t = k.sb([128, *shape], at)
        at += int(np.prod(shape)) * 4
        return t

    kq = room(4, 2, 256)
    zg = room(2, 512)
    qb, kb = room(4, 256), room(4, 256)
    vb = room(2, 512)
    AQ = room(8, 256)
    tat = at
    T = room(8, 128)
    TT = room(8, 128)
    vTat = at
    vT = room(4, 256)
    vBat = at
    vB = room(8, 128)
    ys = Turns([room(256) for _ in range(3)])
    sqs = Turns([room(256) for _ in range(2)])
    diags = Turns([room(256) for _ in range(2)])
    biases = Turns([room(384) for _ in range(2)])
    Ss = Turns([room(384) for _ in range(3)])
    PTs = Turns([room(384) for _ in range(3)])
    bs = room(768)
    assert at <= k.f1end, (at, k.f1end)
    AM = [k.sb([128, 4, 128], k.ylat), k.sb([128, 4, 128], k.ylat + 2048)]
    X = [k.sb([128, 4, 128], k.yhat), k.sb([128, 4, 128], k.yhat + 2048)]
    r1, qs = k.sb([128, 4, 128], k.ylat), k.sb([128, 4, 128], k.ylat + 2048)
    kd, S1 = k.sb([128, 4, 128], tat), k.sb([128, 4, 128], tat + 2048)
    o = k.sb([128, 8, 128], tat)
    vn = [k.sb([128, 4, 128], vTat), k.sb([128, 4, 128], vTat + 2048)]
    k.junk = Turns([k.sb([128, 512], tat), k.sb([128, 512], tat + 2048)])

    cst, col, mul, add, sub = k.cst, k.col, ALU.mult, ALU.add, ALU.subtract
    ones, ident = cst("ones"), k.ident
    k.open_squares()
    for t in (0, 1):
        for nh in (0, 1):
            k.squares(t, nh, k.xmarks[t])
    hm = k.front((cst("ln1"), k.cmark), None, None, [])
    k.setup(vBat)
    taps = cst("conv")
    kqm, vm, zm, ssm = {}, {}, {}, []
    sbank, sfree = k.psum.take()

    def conv_piece(kind, pair):
        def then(bank, d):
            got, made = [], []
            for c in (0, 1):
                y, yfree = ys.take()
                chunk = {"q": 0, "k": 4, "v": 8}[kind] + pair * 2 + c
                w = taps[:, chunk * 4:chunk * 4 + 4]
                got.append((y, w, k.acp(y[:, :], bank[:, c * 256:c * 256 + 256], d, yfree, scale=w[:, 3:4])))
            a = got[1][2]
            for c, (y, w, _) in enumerate(got):
                m = a
                for j in (1, 2, 3):
                    m = k.stt(y[:, j:256], bank[:, c * 256:c * 256 + 256 - j], w[:, 3 - j:4 - j], y[:, j:256], mul, add, m, d)
                h = pair * 2 + c
                if kind == "v":
                    made.append((h, y, m))
                    continue
                dest = kq[:, h, int(kind == "q"), :]
                a2 = k.fn(dest, y[:, :], ACT.Silu, m)
                ys.give(y, a2)
                kqm[kind, h] = a2
                sq, sqfree = sqs.take()
                made.append((h, sq, k.fn(sq[:, :], dest, ACT.Square, a2, sqfree)))
            k.psum.give(bank, m)
            if kind == "v":
                for h, y, m in made:
                    a = k.fn(vT[:, h, :], y[:, :], ACT.Tanh, m, scale=0.5)
                    vm[h] = k.stt(vT[:, h, :], vT[:, h, :], 1.0, y[:, :], add, mul, a)
                    ys.give(y, vm[h])
                return
            yield
            for h, sq, a in made:
                i = (kind == "q") * 4 + h
                s = k.mm(sbank[0:8, 0:256], cst("rowsum")[:, i * 8:i * 8 + 8], sq[:, :], kind == "k" and h == 0,
                         kind == "q" and h == 3, a, sfree, signal=True)
                sqs.give(sq, s)
                ssm.append(s)
        return then

    def z_piece(pair):
        def then(bank, d):
            s = slice(pair * 256, pair * 256 + 256)
            a = k.fn(zg[:, :, s], blocks(bank[:, :], 256), ACT.Tanh, d, scale=0.5)
            m = k.stt(zg[:, :, s], zg[:, :, s], 1.0, blocks(bank[:, :], 256), add, mul, a, d)
            k.psum.give(bank, m)
            for t in (0, 1):
                zm[pair, t] = k.stt(blocks(zg[:, t, s], 128), blocks(zg[:, t, s], 128), 0.5, again(cst("gain"), 2, 128),
                                    mul, mul, m)
            yield
        return then

    qbm, kbm, vbm = {}, {}, {}

    def swa_qk(dest, marks, pair, scale):
        def then(bank, d):
            a = k.acp(dest[:, 2 * pair:2 * pair + 2, :], blocks(bank[:, :], 256), d, scale=scale)
            k.psum.give(bank, a)
            marks[pair] = a
            yield
        return then

    def swa_v(pair):
        def then(bank, d):
            a = k.acp(vb[:, :, pair * 256:pair * 256 + 256], blocks(bank[:, :], 256), d)
            k.psum.give(bank, a)
            vbm[pair] = a
            yield
        return then

    ym = {}

    def swa(heads):
        state = {}
        parts = (slice(0, 128), slice(128, 384))

        def scores(h):
            ch, r = h // 2, slice(64 * (h % 2), 64 * (h % 2) + 64)
            pair = ch // 2
            bt, bfree = biases.take()
            b = k.acp(bt[:, :], cst("dist"), bfree, scale=float(2.0 ** -(h + 1)))
            bank, free = k.psum.take()
            k.mm(bank[:, 0:128], qb[r, ch, 0:128], kb[r, ch, 0:128], True, True, qbm[pair], kbm[pair], free)
            d = k.mm(bank[:, 128:384], qb[r, ch, 128:256], kb[r, ch, :], True, True, signal=True)
            S, f = Ss.take()
            nm, den, inv = col(2), col(2), col(2)
            ms = [k.ttr(S[:, p], bank[:, p], bt[:, p], add, ALU.min, FAR * 4, nm[:, i:i + 1], d, b, f)
                  for i, p in enumerate(parts)]
            k.psum.give(bank, ms[1])
            biases.give(bt, ms[1])
            es = [k.fn(S[:, p], S[:, p], ACT.Exp, ms[i], bias=nm[:, i:i + 1], scale=-1.0) for i, p in enumerate(parts)]
            state[h] = (S, es, den, inv)

        def normal(h):
            S, es, den, inv = state[h]
            cs = [k.ttr(S[:, p], S[:, p], cst("count")[:, p], mul, add, 0.0, den[:, i:i + 1], es[i])
                  for i, p in enumerate(parts)]
            rv = k.rec(inv, den, cs)
            for i, p in enumerate(parts):
                m = k.ts(S[:, p], S[:, p], inv[:, i:i + 1], mul, rv)
            state[h] = (S, m)

        def turn(h):
            S, m = state[h]
            bank, free = k.psum.take()
            for j in range(3):
                d = k.tr(bank[:, j * 128:j * 128 + 128], S[:, j * 128:j * 128 + 128], m, free, signal=j == 2)
            Ss.give(S, d)
            PT, f = PTs.take()
            a = k.acp(PT[:, :], bank[:, 0:384], d, f)
            k.psum.give(bank, a)
            state[h] = (PT, a)

        def values(h):
            PT, a = state.pop(h)
            r = slice(64 * (h % 2), 64 * (h % 2) + 64)
            if h % 2 == 0:
                state["out"] = k.psum.take()
            bank, free = state["out"]
            v = slice(h * 64, h * 64 + 64)
            k.mm(bank[r, 0:256], vb[:, 0, v], PT[:, 0:256], True, False, a, vbm[h // 4], free)
            d = k.mm(bank[r, 128:256], vb[:, 1, v], PT[:, 256:384], False, True, signal=True)
            PTs.give(PT, d)
            if h % 2 == 1:
                kt = 4 + h // 2
                a = k.acp(k.yh[:, kt, :], bank[:, 0:256], d)
                m = k.tt(k.yl[:, kt, :], bank[:, 0:256], k.yh[:, kt, :].bitcast(F32), sub, a)
                k.psum.give(bank, m)
                ym[kt] = m

        n = len(heads)
        for i in range(n + 2):
            if 1 <= i <= n:
                turn(heads[i - 1])
            if i >= 2:
                values(heads[i - 2])
            if i < n:
                scores(heads[i])
                normal(heads[i])
            yield

    def delta():
        eps = cst("eps")
        while len(ssm) < 8:
            yield
        bbank, free = k.psum.take()
        wba = cst("wba")
        for kt in range(8):
            for i, part in enumerate((k.hh, k.hl)):
                ba = k.mm(bbank[32 * i:32 * i + 8, 0:256], wba[:, kt * 8:kt * 8 + 8], part[:, kt, :].bitcast(F32), kt == 0,
                          kt == 7, free, hm, signal=kt == 7)
        k.cp(bs[0:8, 0:256], bbank[0:8, 0:256], ba)
        k.cp(bs[0:8, 256:512], bbank[32:40, 0:256], ba)
        m = k.cp(bs[0:8, 512:768], sbank[0:8, 0:256], ssm)
        k.psum.give(bbank, m)
        k.psum.give(sbank, m)
        yield
        bank, free = k.psum.take()
        for t in (0, 1):
            for i in (0, 1):
                q = slice(i * 256 + t * 128, i * 256 + t * 128 + 128)
                k.mm(bank[:, t * 8:t * 8 + 8], bs[0:8, q], ident[0:8, 0:8], i == 0, i == 1, m, free)
        for t in (0, 1):
            q = slice(512 + t * 128, 512 + t * 128 + 128)
            d = k.mm(bank[:, 16 + t * 8:24 + t * 8], bs[0:8, q], ident[0:8, 0:8], True, True, signal=t == 1)
        y2, ss = col(16), col(16)
        b3 = blocks(bank[:, 0:16], 8)
        k.ts(blocks(y2[:, 0:8], 4), b3[:, :, 0:4], -1.0, mul, d)
        bam = k.tt(blocks(y2[:, 8:16], 4), b3[:, :, 4:8], again(cst("dtb"), 2, 4), add, d)
        s3 = blocks(bank[:, 16:32], 8)
        k.cp(blocks(ss[:, 0:8], 4), s3[:, :, 0:4], d)
        ssum = k.cp(blocks(ss[:, 8:16], 4), s3[:, :, 4:8], d)
        k.psum.give(bank, ssum)
        ab, u, w, lw, den, sp, ea, lns, lnr = (col(16) for _ in range(9))
        m = k.stt(ab, y2, -1.0, y2, mul, ALU.max, bam)
        uu = k.fn(u, ab, ACT.Exp, m, scale=-1.0)
        em = k.fn(ea[:, 0:4], cst("alog"), ACT.Exp, k.cmark)
        wm = k.ts(w, u, 1.0, add, uu)
        lm = k.fn(lw, w, ACT.Ln, wm)
        lsm = k.fn(lns, ss, ACT.Ln, ssum, bias=eps)
        dm = k.ts(den, w, -1.0, add, wm, s2=1e-30, op1=add)
        dm = k.rec(den, den, dm)
        m = k.stt(lw, lw, 1e-30, u, add, mul, lm)
        m = k.tt(lw, lw, den, mul, m, dm)
        m = k.stt(sp, y2, 0.0, lw, ALU.max, add, m)
        lrm = k.ts(lnr, lns, -0.5, mul, lsm)
        g = col(8)
        gm = k.stt(blocks(g, 4), blocks(sp[:, 8:16], 4), -1.0, again(ea[:, 0:4], 2, 4), mul, mul, m, em)
        yield
        cbank, free = k.psum.take()
        k.mm(cbank[:, 0:8], cst("tri"), g, True, True, gm, free)
        d = k.mm(cbank[:, 8:16], ones, g, True, True, signal=True)
        cum, tot, av, rv, sv, er, es, ekd, beta = (col(8) for _ in range(9))
        k.cp(cum, cbank[:, 0:8], d)
        m = k.cp(tot, cbank[:, 8:16], d)
        k.psum.give(cbank, m)
        lnk, lnq = lnr[:, 0:8], lnr[:, 8:16]
        avm = k.tt(av, lnk, cum, sub, m, lrm)
        m1 = k.tt(rv, cum, sp[:, 0:8], sub, m)
        sm = k.stt(sv, cum, -0.5 * float(np.log(128.0)), lnq, add, add, m, lrm)
        rm = k.tt(rv, rv, lnk, add, m1)
        kdm = k.tt(ekd, tot, av, add, avm)
        erm = k.fn(er, rv, ACT.Exp, rm)
        esm = k.fn(es, sv, ACT.Exp, sm)
        kdm = k.fn(ekd, ekd, ACT.Exp, kdm)
        btm = k.fn(beta, sp[:, 0:8], ACT.Exp, m1, scale=-1.0)
        btm = k.ts(beta, beta, 0.5, mul, btm)
        aqm = {}

        def decays(i):
            bank, free = k.psum.take()
            for u_ in (2 * i, 2 * i + 1):
                dg, f = diags.take()
                k.ts(dg[:, 0:128], ident, rv[:, u_:u_ + 1], mul, rm, f)
                m = k.ts(dg[:, 128:256], ident, sv[:, u_:u_ + 1], mul, sm)
                o_ = (u_ % 2) * 256
                d = k.mm(bank[:, o_:o_ + 256], ones, dg[:, :], True, True, m, free, signal=True)
                diags.give(dg, d)
            m = k.tt(AQ[:, 2 * i:2 * i + 2, :], blocks(bank[:, :], 256), again(cst("gmask"), 2, 256), add, d)
            k.psum.give(bank, m)
            for u_ in (2 * i, 2 * i + 1):
                a = k.fn(AQ[:, u_, :], AQ[:, u_, :], ACT.Exp, m, avm, bias=av[:, u_:u_ + 1])
            return a

        def products(i, a):
            bank, free = k.psum.take()
            for u_ in (2 * i, 2 * i + 1):
                c, h = u_ // 4, u_ % 4
                s = slice(c * 128, c * 128 + 128)
                o_ = (u_ % 2) * 256
                d = k.mm(blocks(bank[:, o_:o_ + 256], 128), kq[:, h, 0, s], kq[:, h, :, s], True, True, kqm["k", h],
                         kqm["q", h], free, signal=True)
            m = k.tt(AQ[:, 2 * i:2 * i + 2, :], AQ[:, 2 * i:2 * i + 2, :], blocks(bank[:, :], 256), mul, a, d)
            k.psum.give(bank, m)
            aqm[i // 2] = m

        yield
        prev = decays(0)
        for i in range(4):
            nxt = decays(i + 1) if i < 3 else None
            yield
            products(i, prev)
            prev = nxt
        lvl = cst("level")
        tm, ttm, amread, xread = [None, None], [None, None], [None, None], [None, None]
        for c in (0, 1):
            us = slice(c * 4, c * 4 + 4)
            m = k.tt(AM[c][:, :, :], AQ[:, us, 0:128], again(lvl[:, 0:128], 4, 128), mul, aqm[c])
            ttm[c] = k.tt(TT[:, us, :], again(ident, 4, 128), AM[c][:, :, :], sub, m, k.ssm)
            amread[c] = ttm[c]
        yield
        for c in (0, 1):
            bank, free = k.psum.take()
            for h in range(4):
                d = k.tr(bank[:, h * 128:h * 128 + 128], TT[:, c * 4 + h, :], ttm[c], free, signal=h == 3)
            tm[c] = k.acp(T[:, c * 4:c * 4 + 4, :], blocks(bank[:, :], 128), d, k.ssm)
            k.psum.give(bank, tm[c])
        bvm = {}

        def values(c):
            bank, free = k.psum.take()
            for h in range(4):
                d = k.tr(bank[:, h * 128:h * 128 + 128], vT[:, h, c * 128:c * 128 + 128], vm[h], free, signal=h == 3)
            bvm[c] = k.tt(vB[:, c * 4:c * 4 + 4, :], blocks(bank[:, :], 128), spread(beta[:, c * 4:c * 4 + 4], 4, 128),
                          mul, d, btm, k.t5m)
            k.psum.give(bank, bvm[c])
            return d

        yield
        for l in range(1, 7):
            xm = [None, None]
            for c in (0, 1):
                us = slice(c * 4, c * 4 + 4)
                m = k.tt(AM[c][:, :, :], AQ[:, us, 0:128], again(lvl[:, l * 128:l * 128 + 128], 4, 128), mul, aqm[c],
                         amread[c])
                bank, free = k.psum.take()
                for h in range(4):
                    d = k.mm(bank[:, h * 128:h * 128 + 128], AM[c][:, h, :], T[:, c * 4 + h, :], True, True, m, tm[c],
                             free, signal=h == 3)
                amread[c] = d
                xm[c] = k.acp(X[c][:, :, :], blocks(bank[:, :], 128), d, xread[c])
                k.psum.give(bank, xm[c])
            yield
            for c in (0, 1):
                us = slice(c * 4, c * 4 + 4)
                if l < 6:
                    bank, free = k.psum.take()
                    for h in range(4):
                        d = k.mm(bank[:, h * 128:h * 128 + 128], TT[:, c * 4 + h, :], X[c][:, h, :], True, True, xm[c],
                                 ttm[c], free, signal=h == 3)
                bank2, free = k.psum.take()
                for h in range(4):
                    d2 = k.mm(bank2[:, h * 128:h * 128 + 128], X[c][:, h, :], TT[:, c * 4 + h, :], True, True, xm[c],
                              ttm[c], free, signal=h == 3)
                xread[c] = d2
                if l < 6:
                    tm[c] = k.tt(T[:, us, :], T[:, us, :], blocks(bank[:, :], 128), sub, d, tm[c])
                    k.psum.give(bank, tm[c])
                ttm[c] = k.tt(TT[:, us, :], TT[:, us, :], blocks(bank2[:, :], 128), sub, d2)
                k.psum.give(bank2, ttm[c])
            yield
            if l in (2, 3):
                vread = values(l - 2)
        solved = list(ttm)

        def bank4(f, *marks):
            bank, free = k.psum.take()
            for h in range(4):
                l, r = f(h)
                d = k.mm(bank[:, h * 128:h * 128 + 128], l, r, True, True, free, *marks, signal=h == 3)
            return bank, blocks(bank[:, :], 128), d

        bank, free = k.psum.take()
        for h in range(4):
            d = k.tr(bank[:, h * 128:h * 128 + 128], kq[:, h, 0, 0:128], free, signal=h == 3)
        kdm = k.tt(kd[:, :, :], blocks(bank[:, :], 128), spread(ekd[:, 0:4], 4, 128), mul, d, kdm, solved, xread, amread)
        k.psum.give(bank, kdm)
        bank, b, d = bank4(lambda h: (TT[:, h, :], vB[:, h, :]), solved, bvm[0])
        vnm = k.acp(vn[0][:, :, :], b, d, vread)
        k.psum.give(bank, vnm)
        yield
        bank, b, d = bank4(lambda h: (kd[:, h, :], vn[0][:, h, :]), vnm, kdm)
        s1m = k.acp(S1[:, :, :], b, d, solved, amread)
        k.psum.give(bank, s1m)
        kdread = d
        ofirst, b0, d0 = bank4(lambda h: (AQ[:, h, 128:256], vn[0][:, h, :]), vnm, aqm[0])
        om = [k.cp(o[:, 0:4, :], b0, d0, kdread), None]
        k.psum.give(ofirst, om[0])
        yield
        bank, b, d = bank4(lambda h: (kq[:, h, 0, 128:256], S1[:, h, :]), s1m)
        m = k.tt(r1[:, :, :], b, spread(er[:, 4:8], 4, 128), mul, d, erm, amread)
        k.psum.give(bank, m)
        rm1 = k.tt(r1[:, :, :], vB[:, 4:8, :], r1[:, :, :], sub, m, bvm[1])
        bank, b, d = bank4(lambda h: (kq[:, h, 1, 128:256], S1[:, h, :]), s1m)
        qsm = k.tt(qs[:, :, :], b, spread(es[:, 4:8], 4, 128), mul, d, esm, amread)
        k.psum.give(bank, qsm)
        sread = d
        yield
        bank, b, d = bank4(lambda h: (TT[:, 4 + h, :], r1[:, h, :]), rm1, solved)
        vnm = k.acp(vn[1][:, :, :], b, d, vread)
        k.psum.give(bank, vnm)
        yield
        bank, b, d = bank4(lambda h: (AQ[:, 4 + h, 128:256], vn[1][:, h, :]), vnm, aqm[1])
        om[1] = k.tt(o[:, 4:8, :], b, qs[:, :, :], add, d, qsm, sread)
        k.psum.give(bank, om[1])
        sq = k.sb([128, 8, 128], base + 24576)
        ss = col(8)
        m = k.tt(sq[:, :, :], o[:, :, :], o[:, :, :], mul, om, d, d0)
        m = k.red(ss, sq[:, :, :], add, m)
        r, rm_ = k.rstd(ss, 8, 1.0 / 128, m)
        m = k.tt(o[:, :, :], o[:, :, :], zg[:, :, :].rearrange("p t (h d) -> p (t h) d", d=128), mul, m,
                 list(zm.values()))
        m = k.tt(o[:, :, :], o[:, :, :], spread(r, 8, 128), mul, rm_, m)
        yield
        for pair in (0, 1):
            bank, free = k.psum.take()
            for h_ in (0, 1):
                for t in (0, 1):
                    o_ = h_ * 256 + t * 128
                    d = k.tr(bank[:, o_:o_ + 128], o[:, t * 4 + pair * 2 + h_, :], m, free, signal=h_ == 1 and t == 1)
            s = slice(2 * pair, 2 * pair + 2)
            a = k.acp(k.yh[:, s, :], blocks(bank[:, :], 256), d, xread)
            lm_ = k.tt(k.yl[:, s, :], blocks(bank[:, :], 256), k.yh[:, s, :].bitcast(F32), sub, a, qsm, rm1, d)
            k.psum.give(bank, lm_)
            ym[2 * pair] = ym[2 * pair + 1] = lm_
        yield

    for kind in "kq":
        for pair in (0, 1):
            k.run(k.feature_major((kind, pair), conv_piece(kind, pair), hm))
    k.start(delta(), first=True)
    for pair in (0, 1):
        k.run(k.feature_major(("v", pair), conv_piece("v", pair), hm))
    for pair in (0, 1):
        k.run(k.token_major(("z", pair), z_piece(pair), hm))
    for pair in (0, 1):
        k.run(k.feature_major(("qb", pair), swa_qk(qb, qbm, pair, -0.125), hm))
        k.run(k.feature_major(("kb", pair), swa_qk(kb, kbm, pair, None), hm))
        k.run(k.token_major(("vb", pair), swa_v(pair), hm))
        k.half()
        k.start(swa(range(pair * 4, pair * 4 + 4)))
    rows = lambda j, half, first, last: k.project(("wo", j), 2 * j + half, half, (k.yh, k.yl), ym[2 * j + half], first, last)
    while 5 not in ym:
        k.half()
    k.project_open()
    k.sumsm = [None] * 4
    for half in (0, 1):
        rows(2, half, half == 0, False)
        k.half()
    while 7 not in ym:
        k.half()
    for half in (0, 1):
        rows(3, half, False, False)
        k.half()
    while k.live:
        k.half()
    for half in (0, 1):
        rows(0, half, False, False)
    for half in (0, 1):
        k.yread = rows(1, half, False, half == 1)
    k.add_sums()


def first_ffn(k, base):
    at = base

    def room(*shape, dt=F32):
        nonlocal at
        t = k.sb([128, *shape], at, dt)
        at += int(np.prod(shape)) * 4
        return t

    ys = Turns([room(256) for _ in range(2)], k.fence)
    gs = Turns([room(256) for _ in range(2)], k.fence)
    ams = Turns([room(256) for _ in range(2)], k.fence)
    aps = Turns([(room(256, dt=F32R), room(256, dt=F32R)) for _ in range(3)], k.fence)
    lnf = room(1024)
    junk = Turns([room(512) for _ in range(2)], k.fence)
    assert at <= base + k.f2size
    count, src = Count(k.nc, "lnf"), k.lnf
    hm = k.front((k.cst("ln2"), k.cmark), None, None, [k.hread])
    taps = k.cst("fconv")
    k.project_open()
    k.sumsm = [None] * 4
    acts = {}

    def gate_up(c):
        bank, free = k.psum.take()
        for half in (0, 1):
            hi, lo, m, st = k.staged(("gu", c), half)
            for kt in range(8):
                s = slice(kt * 128, kt * 128 + 128)
                d = k.mm3(bank[:, half * 256:half * 256 + 256], (hi[:, s], lo[:, s]), (k.hh[:, kt, :], k.hl[:, kt, :]),
                          kt == 0, kt == 7, m, free, hm[kt // 2], signal=kt == 7)
            k.stages.give(st, d)
            if half == 1:
                k.hread = d
                k.start(activate(c, bank, d))
            yield

    def activate(c, bank, d):
        y, yf = ys.take()
        m = conv_taps(k, y, bank, 0, taps[:, c * 3:c * 3 + 3], 3, d, yf)
        g, gf = gs.take()
        a = k.fn(g[:, :], y[:, :], ACT.Silu, m, gf)
        ys.give(y, a)
        f, ff = ams.take()
        m = k.tt(f[:, :], g[:, :], bank[:, 256:512], ALU.mult, a, d, ff)
        k.psum.give(bank, m)
        gs.give(g, m)
        part, af = aps.take()
        a = k.acp(part[0][:, :], f[:, :], m, af)
        m = k.tt(part[1][:, :], f[:, :], part[0][:, :].bitcast(F32), ALU.subtract, a, m, af)
        ams.give(f, m)
        acts[c] = (part, m)
        yield

    def down(c):
        part, am = acts.pop(c)
        d = k.project(("wd", c // 2), None, c % 2, part, am, c == 0, c == 21)
        aps.give(part, d)

    for c in range(23):
        if c == 2:
            lm = k.act.dma(lambda e: e.dma_start(lnf[:, :], src), count, k.fence)
        if c < 22:
            k.run(gate_up(c))
        else:
            k.half()
        if c >= 1:
            down(c - 1)
            k.half()
    k.junk = junk
    k.add_sums()
    s2 = k.col(2)
    m = k.tt(s2, k.ss4[:, 0:4:2], k.ss4[:, 1:4:2], ALU.add, k.ssm)
    r, m = k.rstd(s2, 2, 1.0 / 1024, m)
    k.open_squares()
    for t in (0, 1):
        for nh in (0, 1):
            s = slice(nh * 512, nh * 512 + 512)
            xs = k.x[:, t, s]
            mx = k.stt(xs, xs, r[:, t:t + 1], lnf[:, s], ALU.mult, ALU.mult, m, lm, k.xmarks[t])
            k.xnew.append((t, mx))
            k.squares(t, nh, mx)
    k.settle()


def first_halves():
    keys = ([(s, p) for s in "kqvz" for p in (0, 1)] + [(s, p) for p in (0, 1) for s in ("qb", "kb", "vb")]
            + [("wo", j) for j in (2, 3, 0, 1)])
    seq = [(key, half) for key in keys for half in (0, 1)]
    for c in range(23):
        if c < 22:
            seq += [(("gu", c), 0), (("gu", c), 1)]
        if c >= 1:
            seq.append((("wd", (c - 1) // 2), (c - 1) % 2))
    return seq


def modulation(k):
    for layer in (0, 1):
        for v in range(6):
            c = k.keep(8)
            for s in range(4):
                w, load, slot = k.piece(("ada", layer, v, s))
                for kk in (0, 1):
                    j = 2 * s + kk
                    part = w[:, kk * 1024:kk * 1024 + 1024]
                    m = k.ttr(part, part, k.csr[:, :], ALU.mult, ALU.add, 0.0, c[:, j:j + 1], load, k.csrm)
                    if kk == 1:
                        k.piece_done(slot, m)
                    if j == 7:
                        a = (layer * 6 + v) * 8
                        m = k.tt(c, c, k.cst("adab")[:, a:a + 8], ALU.add, m)
                        if v in (1, 4):
                            gain = k.cst("nmix" if v == 1 else "nffn")[:, layer * 8:layer * 8 + 8]
                            m = k.stt(c, c, 1.0, gain, ALU.add, ALU.mult, m)
                        k.mod[layer, v] = (c, m)
                    yield


def need(k, layer, v):
    while (layer, v) not in k.mod:
        next(k.back)
    return k.mod[layer, v]


def gate_rows(k, layer, v, tmp):
    c, m = need(k, layer, v)
    for half in (0, 1):
        dg, free = tmp.take()
        for j in range(4):
            i = half * 4 + j
            e = k.ts(dg[:, j * 128:j * 128 + 128], k.ident, c[:, i:i + 1], ALU.mult, m, free)
        yield
        bank, free = k.psum.take()
        d = k.mm(bank[:, :], k.cst("ones"), dg[:, :], True, True, e, free, signal=True)
        tmp.give(dg, d)
        a = k.acp(k.gbuf[:, half * 512:half * 512 + 512], bank[:, :], d, k.gread)
        k.psum.give(bank, a)
    k.gate = (k.gbuf, a)
    yield


def load_bias(k, bias, windows, src, step, first, mark, marks):
    corner = again(k.cst("corner"), 4, 256)
    k.biasm = []
    pend = []

    def flip():
        w, g, m = pend.pop(0)
        m = k.tt(bias[:, g * 4:g * 4 + 4, :], corner, w[0][:, :, 255::-1], ALU.subtract, m, marks)
        windows.give(w, m)
        k.biasm.append(m)

    for g in range(bias.shape[1] // 4):
        w, free = windows.take()
        at = bass.AP(tensor=src.tensor, offset=g * 4 * step + first, ap=[[1, 128], [step, 4], [1, 256]])
        m = k.act.dma(lambda e, w=w, at=at: e.dma_start(w[0][:, :, :], at), w[1], mark, marks, free)
        pend.append((w, g, m))
        yield
        if len(windows.free) == 0:
            flip()
    while pend:
        flip()
        yield


def second_mixer(k, layer, base, windows):
    at = base

    def room(*shape):
        nonlocal at
        t = k.sb([128, *shape], at)
        at += int(np.prod(shape)) * 4
        return t

    mul, add, sub = ALU.mult, ALU.add, ALU.subtract
    fence = k.fence
    bias = k.bias[layer]
    qTs, kTs, vs = (Turns([room(2, 256) for _ in range(2)], fence) for _ in range(3))
    tmp = Turns([room(512) for _ in range(2)], fence)
    sqs = Turns([room(512) for _ in range(2)], fence)
    ns = Turns([room(512) for _ in range(2)], fence)
    wmarks = windows.marks
    Ss = Turns([room(384) for _ in range(6)], fence, k.biasm)
    PTs = Turns([room(384) for _ in range(3)], fence, k.biasm)
    assert at <= base + k.asize
    hm = k.front(need(k, layer, 1), need(k, layer, 0), tmp, [k.hread])
    gcol = k.col(2)
    gains = k.cst("qk")[:, layer * 2:layer * 2 + 2]
    k.ts(gcol[:, 0:1], gains[:, 0:1], -0.125, mul)
    gm = k.cp(gcol[:, 1:2], gains[:, 1:2])
    parts = (slice(0, 128), slice(128, 384))

    def qk_piece(g, store, which):
        def then(bank, d):
            sq, f = sqs.take()
            a = k.fn(sq[:, :], bank[:, :], ACT.Square, d, f)
            ss = k.col(8)
            m = k.red(ss, blocks(sq[:, :], 64), add, a)
            sqs.give(sq, m)
            r, m = k.rstd(ss, 8, 1.0 / 64, m)
            yield
            n, f = ns.take()
            m = k.tt(blocks(n[:, :], 64), blocks(bank[:, :], 64), spread(r, 8, 64), mul, m, d, f)
            k.psum.give(bank, m)
            yield
            b2, free = k.psum.take()
            for j in (0, 1):
                for t in (0, 1):
                    o = (j * 2 + t) * 128
                    d = k.tr(b2[:, o:o + 128], n[:, t * 256 + j * 128:t * 256 + j * 128 + 128], m, free,
                             signal=j == 1 and t == 1)
            ns.give(n, d)
            dest, f = (qTs, kTs)[which].take()
            a = k.acp(dest[:, :, :], blocks(b2[:, :], 256), d, f, gm, scale=gcol[:, which:which + 1])
            k.psum.give(b2, a)
            store[which] = (dest, a)
            yield
        return then

    def v_piece(g, store):
        def then(bank, d):
            v, f = vs.take()
            a = k.acp(v[:, :, :], blocks(bank[:, :], 256), d, f)
            k.psum.give(bank, a)
            store[2] = (v, a)
            yield
        return then

    ym = {}

    def weights(store, j, r, head):
        (q, qm), (kk, km) = store[0], store[1]
        rows = slice(64 * r, 64 * r + 64)
        bank, free = k.psum.take()
        k.mm(bank[:, 0:128], q[rows, j, 0:128], kk[rows, j, 0:128], True, True, qm, km, free)
        d = k.mm(bank[:, 128:384], q[rows, j, 128:256], kk[rows, j, :], True, True, signal=True)
        S, f = Ss.take()
        nm, den, inv = k.col(2), k.col(2), k.col(2)
        windows = (bias[:, head, 128:256], bias[:, head, :])
        ms = [k.ttr(S[:, p], bank[:, p], windows[i], add, ALU.min, FAR * 4, nm[:, i:i + 1], d, f, k.biasm)
              for i, p in enumerate(parts)]
        k.psum.give(bank, ms[1])
        es = [k.fn(S[:, p], S[:, p], ACT.Exp, ms[i], bias=nm[:, i:i + 1], scale=-1.0, accum=den[:, i:i + 1])
              for i, p in enumerate(parts)]
        return S, inv, den, es

    def turned(S, m):
        bank, free = k.psum.take()
        for j in range(3):
            d = k.tr(bank[:, j * 128:j * 128 + 128], S[:, j * 128:j * 128 + 128], m, free, signal=j == 2)
        Ss.give(S, d)
        PT, f = PTs.take()
        a = k.acp(PT[:, :], bank[:, 0:384], d, f)
        k.psum.give(bank, a)
        return PT, a

    def single(g, store):
        state = {}

        def scores(i):
            S, inv, den, es = weights(store, i // 2, i % 2, g * 4 + i)
            rv = k.rec(inv, den, es)
            for j, p in enumerate(parts):
                m = k.ts(S[:, p], S[:, p], inv[:, j:j + 1], mul, rv)
            state[i] = (S, m)

        def values(i):
            PT, a = state.pop(i)
            v, vm = store[2]
            r = slice(64 * (i % 2), 64 * (i % 2) + 64)
            if i % 2 == 0:
                state["out"] = k.psum.take()
            bank, free = state["out"]
            c = slice(i * 64, i * 64 + 64)
            k.mm(bank[r, 0:256], v[:, 0, c], PT[:, 0:256], True, False, a, vm, free)
            d = k.mm(bank[r, 128:256], v[:, 1, c], PT[:, 256:384], False, True, signal=True)
            PTs.give(PT, d)
            if i % 2 == 1:
                kt = 2 * g + i // 2
                a = k.acp(k.yh[:, kt, :], bank[:, 0:256], d, k.yread)
                m = k.tt(k.yl[:, kt, :], bank[:, 0:256], k.yh[:, kt, :].bitcast(F32), sub, a, k.yread)
                k.psum.give(bank, m)
                ym[kt] = m
            return d

        for i in range(6):
            if 1 <= i <= 4:
                state[i - 1] = turned(*state[i - 1])
            if i >= 2:
                d = values(i - 2)
            if i < 4:
                scores(i)
            yield
        for turns, (t, _) in zip((qTs, kTs, vs), (store[0], store[1], store[2])):
            turns.give(t, d)

    def double(g, store):
        state = {}

        def scores(i):
            S0, inv0, den0, e0 = weights(store, i, 0, 2 * g + i)
            S1, inv1, den1, e1 = weights(store, i, 1, 2 * g + i)
            r0 = k.rec(inv0, den0, e0)
            r1 = k.rec(inv1, den1, e1)
            c1 = k.col(2)
            cm = k.ts(c1, inv1, k.neglam, mul, r1, k.neglamm)
            for j, p in enumerate(parts):
                m = k.ts(S1[:, p], S1[:, p], c1[:, j:j + 1], mul, cm)
                m = k.stt(S0[:, p], S0[:, p], inv0[:, j:j + 1], S1[:, p], mul, add, m, r0)
            Ss.give(S1, m)
            state[i] = (S0, m)

        def values(i):
            PT, a = state[i]
            v, vm = store[2]
            c = slice(i * 128, i * 128 + 128)
            bank, free = k.psum.take()
            k.mm(bank[:, 0:128], PT[:, 0:128], v[:, 0, c], True, True, a, vm, free)
            k.mm(bank[:, 128:256], PT[:, 128:256], v[:, 0, c], True, False)
            d = k.mm(bank[:, 128:256], PT[:, 256:384], v[:, 1, c], False, True, signal=True)
            PTs.give(PT, d)
            sq, f = sqs.take()
            a = k.fn(sq[:, 0:256], bank[:, 0:256], ACT.Square, d, f)
            ss = k.col(2)
            m = k.red(ss, blocks(sq[:, 0:256], 128), add, a)
            r, m = k.rstd(ss, 2, 1.0 / 128, m)
            m = k.tt(blocks(sq[:, 0:256], 128), blocks(bank[:, 0:256], 128), spread(r, 2, 128), mul, m)
            k.psum.give(bank, m)
            state[i] = (sq, m)
            return d

        def out(i):
            o, m = state.pop(i)
            bank, free = k.psum.take()
            for t in (0, 1):
                d = k.tr(bank[:, t * 128:t * 128 + 128], o[:, t * 128:t * 128 + 128], m, free, signal=t == 1)
            sqs.give(o, d)
            f, ff = tmp.take()
            a = k.acp(f[:, 0:256], bank[:, 0:256], d, ff, k.sublnm, scale=k.subln)
            k.psum.give(bank, a)
            kt = 2 * g + i
            m = k.cp(k.yh[:, kt, :], f[:, 0:256], a, k.yread)
            m = k.tt(k.yl[:, kt, :], f[:, 0:256], k.yh[:, kt, :].bitcast(F32), sub, m, k.yread)
            tmp.give(f, m)
            ym[kt] = m

        for i in range(5):
            if 1 <= i <= 2:
                state[i - 1] = turned(*state[i - 1])
            if 2 <= i <= 3:
                d = values(i - 2)
            if i >= 3:
                out(i - 3)
            if i < 2:
                scores(i)
            yield
        for turns, (t, _) in zip((qTs, kTs, vs), (store[0], store[1], store[2])):
            turns.give(t, d)

    def rows(j, half):
        d = k.project(("ao", layer, j), 2 * j + half, half, (k.yh, k.yl), ym[2 * j + half], j == 0 and half == 0,
                      j == 3 and half == 1)
        k.half()
        return d

    for g in range(4):
        store = {}
        k.run(k.token_major(("aq", layer, g), qk_piece(g, store, 0), hm))
        k.run(k.token_major(("ak", layer, g), qk_piece(g, store, 1), hm))
        k.run(k.token_major(("av", layer, g), v_piece(g, store), hm))
        k.half()
        while 2 not in store or 1 not in store or 0 not in store:
            k.half()
        k.start((double if layer == 0 else single)(g, store), first=True)
        if g == 2:
            k.start(gate_rows(k, layer, 2, tmp))
    k.project_open()
    k.sumsm = [None] * 4
    for j in range(4):
        for half in (0, 1):
            while 2 * j + half not in ym:
                k.half()
            k.yread = rows(j, half)
    k.drain()
    k.junk = sqs
    k.add_sums(k.gate, tmp)
    k.gread = k.xmarks


def mixer_halves(layer):
    keys = [(n, layer, g) for g in range(4) for n in ("aq", "ak", "av")] + [("ao", layer, j) for j in range(4)]
    return [(key, half) for key in keys for half in (0, 1)]


def experts(k, layer, base, out=None):
    at = base

    def room(*shape, dt=F32):
        nonlocal at
        t = k.sb([128, *shape], at, dt)
        at += (int(np.prod(shape)) * 4 + 31) // 32 * 32
        return t

    mul, add, sub, eq = ALU.mult, ALU.add, ALU.subtract, ALU.is_equal
    cst, ones, ident = k.cst, k.cst("ones"), k.ident
    fence = k.fence
    gain, shift = need(k, layer, 4), need(k, layer, 3)
    work = at
    sg, ac, aT, sg2, ac2, aT2 = (room(512) for _ in range(6))
    hT = k.sb([128, 8, 256], work)
    rt = room(24, 32)
    GS = room(8)
    M3 = room(2, 48)
    ov = room(16)
    lg = room(256)
    number = k.sb([1, 16], at, I32)
    at += 64
    Pu, PTu, tab, pu, gu, gsu = room(2, 64), room(256), room(32), room(32), room(32), room(32)
    assert at <= base + k.msize, (at - base, k.msize)
    xh, xl = k.sb([128, 2, 1024], k.hhat, F32R), k.sb([128, 2, 1024], k.hlat, F32R)
    P = k.sb([128, 2, 1024], k.yhat, F32R)
    PT = k.sb([128, 8, 256], k.ylat, F32R)
    taken = [k.stages.take() for _ in (0, 1)]
    hg = [st[2] for st, _ in taken]
    hgfree = [f for _, f in taken]
    for lane in (k.dve, k.act, k.pool):
        lane.wait(fence)

    r, rm = k.scales()
    lbank, lfree = k.psum.take()
    for j in range(4):
        bank, d = k.turn_x(j)
        for kk in (0, 1):
            kt = 2 * j + kk
            src, g, s = bank[:, kk * 256:kk * 256 + 256], gain[0][:, kt:kt + 1], shift[0][:, kt:kt + 1]
            if j % 2 == 0:
                m = k.fn(hT[:, kt, :], src, ACT.Identity, d, gain[1], shift[1], scale=g, bias=s)
            else:
                m = k.ts(hT[:, kt, :], src, g, mul, d, gain[1], shift[1], s2=s, op1=add)
        k.psum.give(bank, m)
        for kt in (2 * j, 2 * j + 1):
            d = k.mm(lbank[0:16, 0:256], cst("rw")[:, kt * 16:kt * 16 + 16], hT[:, kt, :], kt == 0, kt == 7, m, lfree,
                     signal=kt == 7)
    hTread = d
    m = k.cp(lg[0:16, :], lbank[0:16, 0:256], d)
    k.psum.give(lbank, m)
    xa = [k.acp(xh[:, t, :], k.x[:, t, :], rm, k.xmarks[t], k.hread, scale=r[:, t:t + 1]) for t in (0, 1)]
    bank, free = k.psum.take()
    for t in (0, 1):
        d = k.tr(bank[:, t * 16:t * 16 + 16], lg[0:16, t * 128:t * 128 + 128], m, free, signal=t == 1, rows=16)
    n = iter(range(24))
    take = lambda w=32: rt[:, next(n), 0:w]
    sc, sel, gates, M, posm = take(), take(), take(), take(), take()
    z, a, b, c, d4, gs, g2 = take(), take(8), take(8), take(8), take(8), take(8), take(8)
    top, key, ktop = take(2), take(), take(2)
    m = k.fn(z, bank[:, 0:32], ACT.Exp, d, scale=-1.0)
    k.psum.give(bank, m)
    m = k.ts(z, z, 1.0, add, m)
    m = k.rec(sc, z, m)
    m = k.tt(blocks(sel, 16), blocks(sc, 16), again(cst("rbias"), 2, 16), add, m)
    s4 = blocks(sel, 4)
    k.tt(a, s4[:, :, 0], s4[:, :, 1], ALU.max, m)
    k.tt(b, s4[:, :, 0], s4[:, :, 1], ALU.min)
    k.tt(c, s4[:, :, 2], s4[:, :, 3], ALU.max)
    m = k.tt(d4, s4[:, :, 2], s4[:, :, 3], ALU.min)
    k.tt(gs, a, c, ALU.max, m)
    k.tt(g2, a, c, ALU.min)
    m = k.tt(b, b, d4, ALU.max)
    m = k.tt(g2, g2, b, ALU.max, m)
    m = k.tt(gs, gs, g2, add, m)

    def first_best(values, w, weight, hit, m):
        m = k.red(top, blocks(values, w), ALU.max, m)
        m = k.tt(blocks(hit, w), blocks(values, w), spread(top, 2, w), eq, m)
        m = k.tt(key[:, 0:2 * w], hit, weight, mul, m)
        m = k.red(ktop, blocks(key[:, 0:2 * w], w), ALU.max, m)
        return k.tt(blocks(hit, w), blocks(key[:, 0:2 * w], w), spread(ktop, 2, w), eq, m)

    m = first_best(gs, 4, cst("w4"), a, m)
    mk, pen = take(), take(8)
    k.tt(blocks(mk, 4), s4, spread(a, 8, 4), mul, m)
    m = k.ts(pen, a, -1.0, add, m, s2=FAR, op1=mul)
    m = k.tt(blocks(mk, 4), blocks(mk, 4), spread(pen, 8, 4), add, m)
    one, two = take(), take()
    m = first_best(mk, 16, cst("w16"), one, m)
    m = k.stt(mk, one, -4 * FAR, mk, mul, add, m)
    m = first_best(mk, 16, cst("w16"), two, m)
    Mm = k.tt(M, one, two, add, m)
    bank, free = k.psum.take()
    k.mm(bank[:, 0:16], cst("stri"), M[:, 0:16], True, True, Mm, free)
    k.mm(bank[:, 16:32], cst("stri"), M[:, 16:32], True, False)
    d = k.mm(bank[:, 16:32], ones, M[:, 0:16], False, True, signal=True)
    xs = [k.stt(xl[:, t, :], k.x[:, t, :], r[:, t:t + 1], xh[:, t, :].bitcast(F32), mul, sub, xa[t], rm, k.hread)
          for t in (0, 1)]
    m = k.stt(posm, bank[:, 0:32], 1.0, M, add, mul, d)
    k.psum.give(bank, m)
    posmm = k.ts(posm, posm, -1.0, add, m)
    pm = [k.tt(blocks(P[:, t, :], 64), again(cst("iota"), 16, 64), spread(posm[:, t * 16:t * 16 + 16], 16, 64), eq, posmm,
               k.yread) for t in (0, 1)]
    w, ws, wi = take(), take(2), take(2)
    m = k.tt(w, sc, M, mul, Mm)
    m = k.red(ws, blocks(w, 16), add, m)
    m = k.rec(wi, ws, m)
    gm = k.tt(blocks(gates, 16), blocks(w, 16), spread(wi, 2, 16), mul, m)

    def gather(q):
        dest, made = hg[q % 2], []
        for j in range(4):
            bank, free = k.psum.take()
            for kk in (0, 1):
                c = slice((2 * j + kk) * 128, (2 * j + kk) * 128 + 128)
                for t in (0, 1):
                    for part in (xh, xl):
                        d = k.mm(bank[:, kk * 256:kk * 256 + 256], part[:, t, c], P[:, t, q * 256:q * 256 + 256],
                                 t == 0 and part is xh, t == 1 and part is xl, pm[t], xs[t], free,
                                 signal=kk == 1 and t == 1 and part is xl)
            for kk in (0, 1):
                kt = 2 * j + kk
                src, g, s = bank[:, kk * 256:kk * 256 + 256], gain[0][:, kt:kt + 1], shift[0][:, kt:kt + 1]
                to = dest[:, kt * 256:kt * 256 + 256]
                if j % 2:
                    m = k.fn(to, src, ACT.Identity, d, hgfree[q % 2], scale=g, bias=s)
                else:
                    m = k.ts(to, src, g, mul, d, hgfree[q % 2], s2=s, op1=add)
            k.psum.give(bank, m)
            made.append(m)
        return made

    ptm, gsm, nm = [], [], []
    ind, rank, T8 = ov[0:48, 0:1], ov[0:48, 1:2], ov[0:48, 2:10]

    def slot_rows():
        for i in range(4):
            bank, free = k.psum.take()
            for pp in (0, 1):
                p = 2 * i + pp
                for t in (0, 1):
                    o = (pp * 2 + t) * 128
                    d = k.tr(bank[:, o:o + 128], P[:, t, p * 128:p * 128 + 128].bitcast(F32), free, pm,
                             signal=pp == 1 and t == 1)
            ptm.append(k.acp(PT[:, 2 * i:2 * i + 2, :], blocks(bank[:, :], 256), d, k.yread))
            k.psum.give(bank, ptm[-1])
        bank, free = k.psum.take()
        for p in range(8):
            for t in (0, 1):
                d = k.mm(bank[:, p * 16:p * 16 + 16], P[:, t, p * 128:p * 128 + 128].bitcast(F32),
                         gates[:, t * 16:t * 16 + 16], t == 0, t == 1, gm, pm, free, signal=p == 7 and t == 1)
        k.cp(GS[0:64, :], bank[0:64, 0:127:18], d)
        gsm.append(k.cp(GS[64:128, :], bank[64:128, 1:128:18], d))
        k.psum.give(bank, gsm[0])
        m = [k.cp(blocks(M3[:, t, :], 16), again(M[:, t * 16:t * 16 + 16], 3, 16), Mm) for t in (0, 1)]
        bank, free = k.psum.take()
        for t in (0, 1):
            d = k.mm(bank[0:48, 0:1], M3[:, t, :], ones[:, 0:1], t == 0, t == 1, m, free, signal=t == 1)
        m = k.tt(ind, bank[0:48, 0:1], cst("cut")[0:48, :], ALU.is_gt, d)
        yield
        d = k.mm(bank[0:48, 1:2], cst("stri")[0:48, 0:48], ind, True, True, m, signal=True)
        m = k.cp(rank, bank[0:48, 1:2], d)
        m = k.ts(T8, cst("iota")[0:48, 0:8], rank, eq, m, s2=ind, op1=mul)
        yield
        k.mm(bank[0:1, 2:3], ind, ones[0:48, 0:1], True, True, m)
        d = k.mm(bank[0:1, 8:16], cst("where")[0:48, :], T8, True, True, m, signal=True)
        k.cp(number[0:1, 0:1], bank[0:1, 2:3], d)
        nm.append(k.cp(number[0:1, 1:9], bank[0:1, 8:16], d))
        k.psum.give(bank, nm[0])
        yield

    hgm = [None, None]
    hgm[0] = gather(0)
    first_piece = len(k.order)
    sgs = Turns([sg, sg2], hTread)
    acs = Turns([ac, ac2], hTread)
    aTs = Turns([aT, aT2], hTread)
    ys = {}

    def gate_up(p):
        (G, gf), (U, uf) = k.psum.take(), k.psum.take()
        q = (p // 2) % 2
        h = hg[q]
        for s in range(4):
            ws = [k.piece(("mu", layer, 2 * p + j, s)) for j in (0, 1)]
            for kk in (0, 1):
                kt = 2 * s + kk
                for o, free, c in ((G, gf, 0), (U, uf, 512)):
                    for j in (0, 1):
                        w, load, _ = ws[j]
                        a = kt * 256 + ((2 * p + j) % 4) * 64
                        d = k.mm(o[64 * j:64 * j + 64, :], h[:, a:a + 64], w[:, kk * 1024 + c:kk * 1024 + c + 512],
                                 kt == 0, kt == 7, load, free, hgm[q][kt // 2], signal=kk == 1 and c == 512 and j == 1)
            for j in (0, 1):
                k.piece_done(ws[j][2], d)
        hgfree[q] = [d]
        t1, f = sgs.take()
        a = k.fn(t1[:, :], G[:, :], ACT.Silu, d, f)
        k.psum.give(G, a)
        t2, f = acs.take()
        m = k.tt(t2[:, :], t1[:, :], U[:, :], mul, a, f, d)
        k.psum.give(U, m)
        sgs.give(t1, m)
        ys[p] = (t2, m)

    def down(p):
        t2, m = ys[p]
        bank, free = k.psum.take()
        for c in range(4):
            d = k.tr(bank[:, c * 128:c * 128 + 128], t2[:, c * 128:c * 128 + 128], m, free, signal=c == 3)
        acs.give(t2, d)
        t3, f = aTs.take()
        am = k.acp(t3[:, :], bank[:, :], d, f)
        k.psum.give(bank, am)
        ds = [k.psum.take() for _ in (0, 1)]
        for s in (0, 1):
            ws = [k.piece(("md", layer, 2 * p + j, s)) for j in (0, 1)]
            for kk in (0, 1):
                c = 2 * s + kk
                for nh in (0, 1):
                    for j in (0, 1):
                        w, load, _ = ws[j]
                        d = k.mm(ds[nh][0][64 * j:64 * j + 64, :], t3[:, c * 128 + 64 * j:c * 128 + 64 * j + 64],
                                 w[:, kk * 1024 + nh * 512:kk * 1024 + nh * 512 + 512], c == 0, c == 3, load, am, ds[nh][1],
                                 signal=kk == 1 and nh == 1 and j == 1)
            for j in (0, 1):
                k.piece_done(ws[j][2], d)
        aTs.give(t3, d)
        st, f = k.stages.take()
        for nh in (0, 1):
            s = slice(nh * 512, nh * 512 + 512)
            a = k.acp(st[0][:, s], ds[nh][0][:, :], d, f, gsm, scale=GS[:, p:p + 1])
            m = k.stt(st[1][:, s], ds[nh][0][:, :], GS[:, p:p + 1], st[0][:, s].bitcast(F32), mul, sub, a, f, d)
            k.psum.give(ds[nh][0], m)
        ys[p] = (st, m)

    def scatter(p):
        st, m = ys.pop(p)
        for t in (0, 1):
            for nh in (0, 1):
                for part in st[0:2]:
                    bank, free = k.sums[t * 2 + nh]
                    d = k.mm(bank[:, :], PT[:, p, t * 128:t * 128 + 128], part[:, nh * 512:nh * 512 + 512],
                             p == 0 and part is st[0], p == 7 and part is st[1], m, ptm, free,
                             signal=part is st[1] and (p == 7 or (t == 1 and nh == 1)))
                if p == 7:
                    k.sumsm[t * 2 + nh] = d
        k.stages.give(st, d)
        return d

    rows = slot_rows()
    tmp = Turns([ac, ac2])
    for p in range(8):
        if p == 7:
            k.retiring = True
        gate_up(p)
        next(rows, None)
        if p % 2 == 1 and p < 7:
            hgm[(p // 2 + 1) % 2] = gather(p // 2 + 1)
        if p == 0:
            k.project_open()
            k.sumsm = [None] * 4
        else:
            scatter(p - 1)
        down(p)
    d = scatter(7)
    k.hread = k.yread = d
    k.retiring = False

    lanes = (k.pe, k.act, k.dve, k.sp)
    counts = [Count(k.nc, f"more{layer}{i}") for i in range(4)]
    loads = [Count(k.nc, f"moreload{layer}{i}") for i in range(2)]
    wfree = [[d], [d]]
    hu, yu = sg2, k.sb([128, 1024], work + 8192)
    tail = [d, nm, gsm, [t.marks() for t in (acs, aTs, sgs, k.psum)]]
    b0, b1, b2, b3 = [b for b, _ in k.psum.free][0:4]
    lists = [[] for _ in lanes]
    for u in range(EXTRA):
        for lane, count in zip(lanes, counts):
            lane.open(count)
        d = k.mm(b0[:, 0:17], T8[:, u:u + 1].to_broadcast([48, 128]), cst("unit")[0:48, :], True, True, tail, signal=True)
        m = k.cp(tab[:, 0:17], b0[:, 0:17], d, tail)
        for src, res in ((posm, pu), (gates, gu)):
            q = k.tt(blocks(yu[:, 0:32], 16), blocks(src, 16), again(tab[:, 0:16], 2, 16), mul, m, gm, posmm)
            m = k.red(res[:, 0:2], blocks(yu[:, 0:32], 16), add, q)
        m = k.ts(pu[:, 0:2], pu[:, 0:2], tab[:, 16:17], sub, m)
        pum = k.tt(Pu[:, :, :], again(cst("iota"), 2, 64), spread(pu[:, 0:2], 2, 64), eq, m)
        for kt in range(8):
            for t in (0, 1):
                for part in (xh, xl):
                    d = k.mm(b1[:, kt * 64:kt * 64 + 64], part[:, t, kt * 128:kt * 128 + 128].bitcast(F32), Pu[:, t, :],
                             t == 0 and part is xh, t == 1 and part is xl, pum, signal=kt == 7 and t == 1 and part is xl)
        for t in (0, 1):
            k.tr(b2[0:64, t * 128:t * 128 + 128], Pu[:, t, :])
        for t in (0, 1):
            d = k.mm(b2[0:64, 256:257], Pu[:, t, :], gu[:, t:t + 1], t == 0, t == 1, signal=t == 1)
        m = k.tt(blocks(hu[:, :], 64), blocks(b1[:, :], 64), spread(gain[0], 8, 64), mul, d)
        hum = k.tt(blocks(hu[:, :], 64), blocks(hu[:, :], 64), spread(shift[0], 8, 64), add, m)
        k.cp(PTu[0:64, :], b2[0:64, 0:256], d)
        ptum = k.cp(gsu[0:64, 0:1], b2[0:64, 256:257], d)
        for s in range(6):
            slot = s % 2

            def fetch(e, s=s, u=u, slot=slot):
                i = e.value_load(number[0:1, 1 + u:2 + u], min_val=0, max_val=85)
                src = k.weights[bass.ds(i + (first_piece + 2 * s), 1), :, :].rearrange("a p n -> p (a n)")
                return e.dma_start(hg[slot][:, :], src)

            lm = k.sp.dma(fetch, loads[slot], tail, wfree[slot])
            if s < 4:
                for kk in (0, 1):
                    kt = 2 * s + kk
                    for o, c in ((b0, 0), (b3, 512)):
                        d = k.mm(o[0:64, :], hu[:, kt * 64:kt * 64 + 64], hg[slot][:, kk * 1024 + c:kk * 1024 + c + 512],
                                 kt == 0, kt == 7, lm, hum, signal=kk == 1 and c == 512)
                if s == 3:
                    a = k.fn(sg[0:64, :], b0[0:64, :], ACT.Silu, d)
                    m = k.tt(ac[0:64, :], sg[0:64, :], b3[0:64, :], mul, a)
                    for c in range(4):
                        t4 = k.tr(b1[:, c * 64:c * 64 + 64], ac[0:64, c * 128:c * 128 + 128], m, signal=c == 3, rows=64)
                    atm = k.cp(aT[:, 0:256], b1[:, 0:256], t4)
            else:
                for kk in (0, 1):
                    c = 2 * (s - 4) + kk
                    for nh, o in ((0, b0), (1, b3)):
                        d = k.mm(o[0:64, :], aT[:, c * 64:c * 64 + 64],
                                 hg[slot][:, kk * 1024 + nh * 512:kk * 1024 + nh * 512 + 512], c == 0, c == 3, lm, atm,
                                 signal=kk == 1 and nh == 1)
            wfree[slot] = [d]
        for nh, o in ((0, b0), (1, b3)):
            m = k.ts(yu[0:64, nh * 512:nh * 512 + 512], o[0:64, :], gsu[0:64, 0:1], mul, d, ptum)
        for t in (0, 1):
            for nh in (0, 1):
                bank, _ = k.sums[t * 2 + nh]
                d = k.mm(bank[:, :], PTu[0:64, t * 128:t * 128 + 128], yu[0:64, nh * 512:nh * 512 + 512], False, True, m,
                         signal=t == 1 and nh == 1)
        tail = [d]
        for lane in lanes:
            lane.wait(d)
        for i, lane in enumerate(lanes):
            lists[i].append(lane.close())
    for lane, inner in zip(lanes, lists):
        lane.wait(nm)
        lane.branch(number[0:1, 0:1], inner)
    for (st, _), f in zip(taken, hgfree):
        k.stages.give(st, f)
    gate = gate_rows(k, layer, 5, sgs)
    for _ in gate:
        pass
    k.junk = acs
    k.add_sums(k.gate, sgs, squares=out is None, out=out)
    k.gread = k.xmarks


def setup(k, io, at):
    nc = k.nc
    mul, add, sub = ALU.mult, ALU.add, ALU.subtract
    bank, free = k.psum.take()
    d = k.mm(bank[0:8, :], k.cst("t5")[0:32, :], k.cst("hot")[0:32, :], True, True, k.cmark, free, signal=True)
    t5 = k.sb([8, 512], at)
    a = k.acp(t5[:, :], bank[0:8, :], d)
    k.psum.give(bank, a)
    count = Count(nc, "t5")
    dst = io["scratch"]
    k.t5m = k.act.dma(lambda e: e.dma_start(dst, t5[:, :]), count, a)
    count, src = Count(nc, "c"), io["c"]
    m = k.sp.dma(lambda e: e.dma_start(k.csr[:, :], src), count)
    k.csrm = k.fn(k.csr[:, :], k.csr[:, :], ACT.Silu, m)
    k.subln, k.neglam = k.keep(1), k.keep(1)
    k.sublnm = k.ts(k.subln, k.cst("subln"), 1.0 - LAMBDA_INIT, mul, k.cmark)
    lam = k.cst("lam")
    junk, s, e, l = k.col(64), k.col(2), k.col(2), k.col(1)
    m = k.ttr(junk, lam[:, 0:64], lam[:, 64:128], mul, add, 0.0, s[:, 0:1], k.cmark)
    m = k.ttr(junk, lam[:, 128:192], lam[:, 192:256], mul, add, 0.0, s[:, 1:2], m)
    m = k.fn(e, s, ACT.Exp, m)
    m = k.tt(l, e[:, 1:2], e[:, 0:1], sub, m)
    k.neglamm = k.ts(k.neglam, l, -LAMBDA_INIT, add, m)


def build(nc, io):
    k = Core(nc)
    k.weights, k.lnf = io["weights"], io["lnf"]
    at = BASE

    def place(size):
        nonlocal at
        a, at = at, at + (size + 31) // 32 * 32
        return a

    k.x = k.sb([128, 2, 1024], place(8192))
    k.cstt = k.sb([128, NLAST], place(NLAST * 4))
    k.cols = k.sb([128, ZONES], place(ZONES * 4))
    k.zone(KEPT, ZONE_A)
    k.newton = Turns([k.sb([128, 64], place(256)) for _ in range(6)])
    k.diag, k.dread = k.sb([128, 2, 128], place(1024)), []
    k.hhat, k.hlat, k.yhat, k.ylat = (place(8192) for _ in range(4))
    k.hh, k.hl, k.yh, k.yl = (k.sb([128, 8, 256], a, F32R) for a in (k.hhat, k.hlat, k.yhat, k.ylat))
    stages = []
    for _ in range(4):
        a = place(8192)
        stages.append((k.sb([128, 1024], a, F32R), k.sb([128, 1024], a + 4096, F32R), k.sb([128, 2048], a)))
    k.stages = Turns(stages)
    k.csr = k.sb([128, 1024], place(4096))
    k.gbuf, k.gread = k.sb([128, 1024], place(4096)), []
    local = at
    ring = LIMIT - 8 * PIECE
    more = ring - 4 * PIECE
    k.f1end = ring + 4 * PIECE
    cf = k.f1end - (NCST - NLAST) * 4 // 32 * 32 - 32
    k.f1end = cf
    k.cstf = k.sb([128, NCST - NLAST], cf)
    k.f2size, k.asize, k.msize = 24576, ring - 16384 - local, more - local
    bias = [k.sb([128, 8, 256], ring - 8192), k.sb([128, 16, 256], ring - 16384)]
    k.bias = bias
    windows = Turns([(k.sb([128, 4, 256], local + 24576 + 4096 * i), Count(nc, f"window{i}")) for i in range(3)])
    for i in range(4, 8):
        k.add_slot(ring + i * PIECE)

    k.ident = k.cst("ident")
    counts = [Count(nc, n) for n in ("x0", "x1", "cst", "cstf")]
    xin, cin = io["x"], io["cst"]
    k.xmarks = []
    for t in (0, 1):
        k.xmarks.append([k.sp.dma(lambda e, t=t: e.dma_start(k.x[:, t, :], xin[:, t, :]), counts[t])])
    last = k.sp.dma(lambda e: e.dma_start(k.cstt[:, :], cin[:, 0:NLAST]), counts[2])
    k.mod = {}
    k.feed(first_halves())
    for lane in (k.pe, k.dve, k.act, k.pool):
        lane.wait(last)
    k.top(4)
    k.cmark = k.sp.dma(lambda e: e.dma_start(k.cstf[:, :], cin[:, NLAST:NCST]), counts[3])
    k.back = modulation(k)
    k.setup = lambda at: setup(k, io, at)
    first_mixer(k, local)
    k.fence = k.marks()
    for i in range(4):
        k.add_slot(ring + i * PIECE, k.fence)
    k.feed(mixer_halves(0))
    k.start(load_bias(k, bias[0], windows, io["scratch"], 512, 128, k.t5m, k.fence))
    k.pace = 0.5
    first_ffn(k, local)
    k.drain()
    for layer in (0, 1):
        k.fence = k.marks()
        if layer == 0:
            ffn = k.fence
            k.zone(ZONE_A, ZONES)
        k.pace = 1.0
        second_mixer(k, layer, local, windows)
        k.pace = 0.0
        k.fence = k.marks()
        if layer == 0:
            mixed = k.fence
            k.zone(KEPT, ZONE_A, ffn)
        else:
            k.zone(ZONE_A, ZONES, mixed)
        for i in range(4):
            if layer == 0:
                k.add_slot(more + i * PIECE, k.fence, extra=True)
            else:
                k.slots.append((k.extras[i], k.fence))
        if layer == 0:
            k.extras = [s for s, _ in k.slots if s[2]]
        experts(k, layer, local, None if layer == 0 else writer(k, io))
        if layer == 0:
            k.feed(mixer_halves(1))
            windows = Turns([w for w, _ in windows.free], k.marks())
            k.start(load_bias(k, bias[1], windows, io["rel"], 513, 129, None, [k.retired, k.marks()]))
    return finish(k, io)


def writer(k, io):
    count = Count(k.nc, "out")

    def write(t, s, m):
        dst = io["out"][:, t, s]
        k.written = k.sp.dma(lambda e: e.dma_start(dst, k.x[:, t, s]), count, m)

    return write


def finish(k, io):
    if k.written is None:
        write = writer(k, io)
        for t in (0, 1):
            write(t, slice(0, 1024), k.xmarks[t])
    k.sp.wait(k.t5m, k.written)
    assert not k.live
    with k.nc.Block() as block:
        @block.sync
        def _(e):
            k.sp.emit(e)

        @block.gpsimd
        def _(e):
            k.pool.emit(e)

        @block.scalar
        def _(e):
            k.act.emit(e)

        @block.vector
        def _(e):
            k.dve.emit(e)

        @block.tensor
        def _(e):
            k.pe.emit(e)
    return k.order




def _columns(w, a):
    return w[:, a:a + 256].reshape(8, 128, 2, 128).transpose(1, 2, 0, 3).reshape(128, 2048)


def _block(w, a):
    return w[:, a:a + 256].reshape(8, 128, 256).transpose(1, 0, 2).reshape(128, 2048)


def _chunk(w, c):
    return w[:, c * 128:c * 128 + 128].reshape(8, 128, 128).transpose(1, 0, 2).reshape(128, 1024)


def _rows(w, j):
    return w[j * 256:j * 256 + 256].reshape(2, 128, 1024).transpose(1, 0, 2).reshape(128, 2048)


def _piece(key, inp):
    name, n = key[0], key[1]
    w_in = inp["w_in"][0]
    if name in ("q", "k", "v"):
        return _columns(w_in, "qkv".index(name) * 512 + 256 * n)
    if name == "z":
        return _block(w_in, 1536 + 256 * n)
    if name == "qb":
        return _columns(w_in, 2056 + 256 * n)
    if name == "kb":
        return _columns(w_in, 2568 + 256 * n)
    if name == "vb":
        return _block(w_in, 3080 + 256 * n)
    if name == "wo":
        return _rows(inp["w_out"][0], n)
    if name == "gu":
        return np.concatenate([_chunk(inp["w_gate"][0], n), _chunk(inp["w_up"][0], n)], 1)
    if name == "wd":
        return _rows(inp["w_down"][0], n)
    if name in ("aq", "ak", "av"):
        w = inp["a_w_qkv_2"][0] if n == 0 else inp["b_w_qkv_2"][0]
        return _block(w, ("aq", "ak", "av").index(name) * 1024 + 256 * key[2])
    if name == "ao":
        return _rows(inp["a_w_o_2"][0] if n == 0 else inp["b_w_o_2"][0], key[2])
    if name == "ada":
        w = inp["ada_w_2"][n][:, key[2] * 1024 + key[3] * 256:key[2] * 1024 + key[3] * 256 + 256]
        return w.T.reshape(2, 128, 1024).transpose(1, 0, 2).reshape(128, 2048)
    if name == "mu":
        g, u = (inp[f"moe_w_{s}_2"][n, key[2]][key[3] * 256:key[3] * 256 + 256].reshape(2, 128, 512) for s in ("gate", "up"))
        return np.concatenate([g, u], 2).transpose(1, 0, 2).reshape(128, 2048)
    assert name == "md"
    return _rows(inp["moe_w_down_2"][n, key[2]], key[3])


def _params(inp):
    def cols(v, n):
        return v.reshape(n, 128).T

    def wide(v):
        return np.broadcast_to(v.reshape(1, -1), (128, v.size))

    def twice(v):
        return np.tile(v.reshape(64), 2)[:, None]

    out = dict(constants())
    out["ln1"], out["ln2"] = cols(inp["ln1"], 8), cols(inp["ln2"], 8)
    out["conv"] = inp["conv_qkv"][0].reshape(4, 12, 128).transpose(2, 1, 0).reshape(128, 48)
    out["fconv"] = inp["ffn_conv"][0].reshape(3, 22, 128).transpose(2, 1, 0).reshape(128, 66)
    out["alog"], out["dtb"], out["gain"] = wide(inp["a_log"]), wide(inp["dt_bias"]), wide(inp["gdn_norm"])
    out["wba"] = inp["w_in"][0][:, 2048:2056].reshape(8, 128, 8).transpose(1, 0, 2).reshape(128, 64)
    out["nmix"], out["nffn"] = cols(inp["norm_mix_g_2"], 16), cols(inp["norm_ffn_g_2"], 16)
    out["qk"] = np.concatenate([twice(inp[n]) for n in ("a_q_gain_2", "a_k_gain_2", "b_q_gain_2", "b_k_gain_2")], 1)
    out["subln"] = inp["a_subln_g_2"].reshape(128, 1)
    out["lam"] = wide(inp["a_lambda_2"])
    out["rw"] = inp["router_w_2"].reshape(8, 128, 16).transpose(1, 0, 2).reshape(128, 128)
    out["rbias"] = wide(inp["router_bias_2"])
    out["adab"] = cols(inp["ada_b_2"], 96)
    out["t5"] = np.concatenate([inp["t5_bias_2"], np.zeros((96, 8), np.float32)], 0)
    return np.concatenate([out[name] for name in PLACE], 1)


def kernel(**inputs):
    import numpy as _np
    import concourse.bacc as _bacc
    from concourse import mybir as _mybir
    from concourse.bass_utils import run_bass_kernel_spmd as _run

    inp = {k: _np.asarray(v) for k, v in inputs.items()}
    arrays = {
        "x": inp["x"][0],
        "cst": _params(inp),
        "lnf": _np.broadcast_to(inp["ln_f"], (128, 1024)),
        "rel": inp["b_rel_bias_2"][0][:, ::-1],
        "c": _np.broadcast_to(inp["c_2"], (128, 1024)),
    }
    nc = _bacc.Bacc("TRN2", target_bir_lowering=False, num_devices=1)
    io = {}
    shapes = {name: list(a.shape) for name, a in arrays.items()}
    shapes["weights"] = [PIECES, 128, 2048]
    for name, shape in shapes.items():
        io[name] = nc.dram_tensor(f"in_{name}_dram", shape, _mybir.dt.float32, kind="ExternalInput").ap()
    io["scratch"] = nc.dram_tensor("scratch", [8, 512], _mybir.dt.float32, kind="Internal").ap()
    out = nc.dram_tensor("out_0_dram", [256, 1024], _mybir.dt.float32, kind="ExternalOutput").ap()
    io["x"] = io["x"].rearrange("(t p) d -> p t d", p=128)
    io["out"] = out.rearrange("(t p) d -> p t d", p=128)
    order = build(nc, io)
    arrays["weights"] = _np.stack([_piece(key, inp) for key in order])
    arrays = {f"in_{name}_dram": _np.ascontiguousarray(a) for name, a in arrays.items()}
    r = _run(nc, [arrays], core_ids=[0])
    return r.results[0]["out_0_dram"].reshape(1, 256, 1024)
```

```python
import math
from collections import deque

import numpy as np
import concourse.bass as bass
from concourse import mybir

F32 = mybir.dt.float32
F32R = mybir.dt.float32r
I32 = mybir.dt.int32
ACT = mybir.ActivationFunctionType
ALU = mybir.AluOpType
AX = mybir.AxisListType

EPS = 1e-6
LAMBDA_INIT = 0.8 - 0.6 * math.exp(-0.3 * 0)
FAR = 1e30
BASE, LIMIT = 16512, 229344
PIECE = 8192
PIECES = 14 + 4 + 33 + 48 + 2 * (16 + 96)
KEPT, ZONE_A, ZONES = 104, 464, 728
PACES = {"first mixer": (0.5, -0.6, 99.0), "first ffn": (99.0, -0.6, 99.0), "mixer 0": (99.0, -0.6, 99.0),
         "mixer 1": (99.0, -0.6, 99.0)}
EXTRA = 7




def _swa_tables():
    dist = np.zeros((128, 384), np.float32)
    count = np.zeros((128, 384), np.float32)
    for col in range(384):
        tile, key = (0, col) if col < 128 else (1, col - 128)
        for p in range(128):
            d = tile * 128 + p - key
            n = 0
            for window, dilation in ((128, 1), (512, 4), (2048, 16)):
                if d >= 0 and d % dilation == 0 and d // dilation <= window // dilation:
                    n += 1
            count[p, col] = n
            dist[p, col] = d if n else FAR
    return dist, count


def _t5_onehot():
    hot = np.zeros((128, 512), np.float32)
    for i in range(511):
        rel = 255 - i
        n = abs(rel)
        b = n
        if n >= 8:
            b = 8
            while b < 15 and n ** 8 >= 8 ** 8 * 128 ** (b - 8 + 1):
                b += 1
        hot[b + (16 if rel > 0 else 0), i] = 1.0
    return hot


def constants():
    i = np.arange(128)
    out = {}
    out["ident"] = np.eye(128)
    out["tri"] = (i[:, None] <= i[None, :])
    out["stri"] = (i[:, None] < i[None, :])
    out["ones"] = np.ones((128, 128))
    out["iota"] = np.broadcast_to(np.arange(1, 65), (128, 64))
    out["mhalf"] = np.full((128, 16), -0.5)
    out["eps"] = np.full((128, 1), EPS)
    out["rowsum"] = np.broadcast_to(np.eye(8).reshape(1, 64), (128, 64))
    own = (i[None, :] + 64 * (i[:, None] // 64)) % 128
    strict = np.where(i[:, None] < own, 0.0, -FAR)
    causal = np.where(i[:, None] <= i[None, :], 0.0, -FAR)
    out["gmask"] = np.concatenate([strict, causal], 1)
    half = i[:, None] % 64
    row = i[None, 0:64]
    levels = [((row >> l + 1) == (half >> l + 1)) & (row >> l & 1 == 1) & (half >> l & 1 == 0) for l in range(6)]
    out["level"] = np.concatenate(levels, 1)
    out["twice"] = half == row
    out["dist"], out["count"] = _swa_tables()
    corner = np.zeros((128, 256))
    corner[:64, 192:] = FAR
    out["corner"] = corner
    out["hot"] = _t5_onehot()
    e, c = i % 16, i // 16 + 1
    use = i < 48
    out["fold"] = (i[:, None] % 32 == np.arange(16))
    out["cut"] = np.where(use, 64.0 * c, 0.0)[:, None]
    out["unit"] = np.concatenate([(e[:, None] == np.arange(16)) & use[:, None], np.where(use, 64.0 * c, 0.0)[:, None]], 1)
    out["where"] = np.where(use, 12 * (e // 2) + e % 2, 0)[:, None]
    return {k: np.ascontiguousarray(v, dtype=np.float32) for k, v in out.items()}


PARAM = dict(ln1=8, ln2=8, lnf=8, conv=48, fconv=66, alog=4, dtb=4, gain=128, wba=64, nmix=16, nffn=16, qk=4, subln=1,
             lam=256, rw=128, rbias=16, adab=96, t5=8)
AT_ONCE = ("ident", "mhalf", "ln1")
FIRST_ONLY = ("conv", "wba", "alog", "dtb", "tri", "gain", "rowsum", "gmask", "level", "twice", "dist", "count", "hot", "lam", "t5")


def places():
    width = {k: v.shape[1] for k, v in constants().items()}
    width.update(PARAM)
    out, at = {}, 0
    for n in AT_ONCE + tuple(n for n in width if n not in AT_ONCE + FIRST_ONLY) + FIRST_ONLY:
        out[n] = (at, width[n])
        at += width[n]
    return out, sum(width[n] for n in AT_ONCE), out[FIRST_ONLY[0]][0], out["gmask"][0], at


PLACE, NONCE, NLAST, NSOON, NCST = places()




class Count:

    def __init__(self, nc, name):
        self.sem, self.n, self.at = nc.alloc_semaphore(name), 0, {0: 0.0}

    def step(self, k, time):
        self.n += k
        self.at[self.n] = time
        return (self, self.n)

    def mark(self):
        return (self, self.n)


def when(marks):
    if marks is None:
        return 0.0
    if isinstance(marks, tuple) and isinstance(marks[0], Count):
        return marks[0].at[marks[1]]
    return max([when(m) for m in marks], default=0.0)


class Lane:

    loaded = 0.0

    def __init__(self, nc, name):
        self.count, self.items, self.met, self.clock = Count(nc, "done_" + name), [], {}, 0.0

    def wait(self, *marks):
        for m in marks:
            if m is None:
                continue
            if isinstance(m, list):
                self.wait(*m)
                continue
            count, value = m
            self.clock = max(self.clock, count.at[value] + 0.07)
            if self.met.get(count, 0) < value:
                self.met[count] = value
                self.items.append((None, count.sem, value))

    def do(self, op, *marks, cost=0.08, signal=True):
        self.wait(*marks)
        self.clock += cost
        if not signal:
            self.items.append((op, None, 0))
            return None
        self.items.append((op, self.count.sem, 1))
        return self.count.step(1, self.clock + 0.06)

    def dma(self, op, count, *marks, size):
        self.wait(*marks)
        self.clock += 0.05
        self.items.append((op, count.sem, 16))
        Lane.loaded = max(Lane.loaded, self.clock + 1.5) + size / 360e3
        return count.step(16, Lane.loaded + 1.0)

    def open(self, count):
        self.kept = (self.items, self.met, self.count, self.clock)
        self.items, self.met, self.count = [], dict(self.met), count

    def close(self):
        inner = self.items
        self.items, self.met, self.count, self.clock = self.kept
        return inner

    def branch(self, number, lists):
        self.items.append((number, "branch", lists))

    def emit(self, e, items=None):
        for op, sem, n in self.items if items is None else items:
            if sem == "branch":
                self.nest(e, e.value_load(op, min_val=0, max_val=len(n)), n, 0)
            elif op is None:
                e.wait_ge(sem, n)
            elif sem is None:
                op(e)
            else:
                op(e).then_inc(sem, n)

    def nest(self, e, value, lists, i):
        if i < len(lists):
            with e.If(value > i):
                self.emit(e, lists[i])
                self.nest(e, value, lists, i + 1)


class Turns:

    def __init__(self, things, *marks):
        self.free = deque((t, list(marks)) for t in things)

    def take(self):
        return self.free.popleft()

    def give(self, thing, *marks):
        self.free.append((thing, list(marks)))

    def marks(self):
        return [m for _, m in self.free]


def finish(steps):
    try:
        while True:
            next(steps)
    except StopIteration as end:
        return end.value


def size(ap):
    return int(np.prod(ap.shape[1:]))


def blocks(ap, b):
    return ap.rearrange("p (a b) -> p a b", b=b)


def spread(ap, n, k):
    return ap.unsqueeze(2).to_broadcast([ap.shape[0], n, k])


def again(ap, n, k):
    return ap.unsqueeze(1).to_broadcast([ap.shape[0], n, k])




class Core:
    def __init__(self, nc):
        self.nc = nc
        self.pe, self.act, self.dve, self.pool, self.sp = (Lane(nc, n) for n in ("pe", "act", "dve", "pool", "sp"))
        self.psum = Turns([nc.alloc_psum_tensor(f"bank{i}", [128, 512], F32) for i in range(8)])
        self.names = 0
        self.index, self.order, self.slots, self.lent, self.retired, self.retiring = {}, [], deque(), {}, [], False
        self.live, self.back, self.backing, self.halfway, self.holding = [], None, False, False, False
        self.pace("first mixer")
        Lane.loaded = 0.0
        self.halves = [Count(nc, f"half{j}") for j in range(4)]
        self.todo, self.ready, self.opened = deque(), deque(), {}
        self.written, self.xnew = None, []
        self.kept_at = 0

    def pace(self, phase):
        self.most, self.haste, self.slack = PACES[phase]

    def sb(self, shape, offset, dt=F32):
        self.names += 1
        end = offset + int(np.prod(shape[1:])) * 4
        assert offset % 32 == 0 and BASE <= offset and end <= LIMIT, (offset, end)
        return self.nc.alloc_sbuf_tensor_at(f"t{self.names}", shape, dt, offset=offset)


    def add_slot(self, offset, *marks):
        self.slots.append(((self.sb([128, 2048], offset), Count(self.nc, f"slot{self.names}"), False), list(marks)))

    def lend(self, t, *marks):
        if t.name not in self.lent:
            self.lent[t.name] = (t, Count(self.nc, f"lent{len(self.lent)}"), True)
        self.slots.append((self.lent[t.name], list(marks)))

    def retire(self):
        self.retiring = False
        for slot, marks in list(self.slots):
            if slot[2]:
                self.slots.remove((slot, marks))
                self.retired.append(marks)

    def reserve(self, keys):
        for key in keys:
            self.index[key] = len(self.order)
            self.order.append(key)

    def source(self, key):
        if key not in self.index:
            self.reserve([key])
        return self.weights[self.index[key]]

    def piece(self, key):
        slot, marks = self.slots.popleft()
        t, count, _ = slot
        src = self.source(key)
        mark = self.sp.dma(lambda e: e.dma_start(t[:, :], src), count, marks, size=1 << 20)
        return t, mark, slot

    def split_pieces(self, keys):
        got = [(self.slots.popleft(), self.source(key)) for key in keys]
        marks = [[], []]
        for i in (0, 1):
            for j, (((t, count, _), free), src) in enumerate(got):
                s = slice(i * 1024, i * 1024 + 1024)
                marks[i].append(self.sp.dma(lambda e, t=t, src=src, s=s: e.dma_start(t[:, s], src[:, s]),
                                            count if i else self.halves[j], free, size=1 << 19))
        self.halves = self.halves[2:] + self.halves[0:2]
        return [(slot[0], (marks[0][j], marks[1][j]), slot) for j, ((slot, _), _) in enumerate(got)]

    def piece_done(self, slot, *marks):
        if slot[2] == "once":
            self.once = list(marks)
        elif slot[2] and self.retiring:
            self.retired += marks
        else:
            self.slots.append((slot, list(marks)))


    def mm(self, out, l, r, first, last, *marks, signal=False):
        n = size(out)
        cost = n * 4.27e-4 if r.dtype == F32R and n >= 256 else max(0.213, n * 1.68e-3)
        if out.shape[0] == 64:
            cost = 0.081 if n == 64 else cost * 0.53
        return self.pe.do(lambda e: e.matmul(out, l, r, start=first, stop=last, skip_group_check=True),
                          *marks, cost=cost, signal=signal)

    def mm3(self, out, l, r, first, last, *marks, signal=False):
        self.mm(out, l[0], r[0], first, False, *marks)
        self.mm(out, l[0], r[1], False, False)
        return self.mm(out, l[1], r[0], False, last, signal=signal)

    def tr(self, out, in_, *marks, signal=False, rows=128):
        ident = self.ident[0:rows, 0:rows]
        return self.pe.do(lambda e: e.transpose(out, in_, ident), *marks, cost=0.107, signal=signal)

    def row(self, out, c, *marks, signal=False):
        return self.mm(out, c.to_broadcast([128, 128]), self.ident, True, True, *marks, signal=signal)

    def fn(self, out, in_, f, *marks, bias=None, scale=None, accum=None):
        kw = {}
        if bias is not None:
            kw["bias"] = bias
        if scale is not None:
            kw["scale"] = scale
        if accum is not None:
            kw["accum_out"] = accum
        extra = 0.09 * sum(v is not None and not isinstance(v, float) for v in (bias, scale, accum))
        return self.act.do(lambda e: e.activation(out, in_, f, **kw), *marks, cost=0.09 + 8.3e-4 * size(out) + extra)

    def acp(self, out, in_, *marks, scale=None):
        return self.fn(out, in_, ACT.Copy, *marks, scale=scale)

    def tt(self, out, a, b, op, *marks, lane=None):
        return (lane or self.dve).do(lambda e: e.tensor_tensor(out, a, b, op), *marks,
                                     cost=0.065 + 1.04e-3 * size(out) if lane is None else 0.7)

    def ts(self, out, a, s1, op0, *marks, s2=None, op1=None, lane=None):
        cost = 0.065 + 0.7e-3 * size(out) if lane is None else 0.25
        if op1 is None:
            return (lane or self.dve).do(lambda e: e.tensor_scalar(out, a, s1, None, op0), *marks, cost=cost)
        return (lane or self.dve).do(lambda e: e.tensor_scalar(out, a, s1, s2, op0, op1), *marks, cost=cost)

    def stt(self, out, a, s, b, op0, op1, *marks):
        return self.dve.do(lambda e: e.scalar_tensor_tensor(out, a, s, b, op0, op1), *marks,
                           cost=0.065 + 1.04e-3 * size(out))

    def ttr(self, out, a, b, op0, op1, start, accum, *marks):
        return self.dve.do(lambda e: e.tensor_tensor_reduce(out=out, in0=a, in1=b, scale=1.0, scalar=start, op0=op0,
                                                            op1=op1, accum_out=accum), *marks,
                           cost=0.075 + 1.04e-3 * size(out))

    def cp(self, out, in_, *marks, lane=None):
        return (lane or self.dve).do(lambda e: e.tensor_copy(out, in_), *marks, cost=0.065 + 0.8e-3 * size(out))

    def red(self, out, in_, op, *marks):
        return self.dve.do(lambda e: e.tensor_reduce(out, in_, AX.X, op), *marks, cost=0.065 + 1.04e-3 * size(in_))

    def rec(self, out, in_, *marks):
        return self.dve.do(lambda e: e.reciprocal(out, in_), *marks)

    def marks(self):
        return [lane.count.mark() for lane in (self.pe, self.act, self.dve, self.pool)]


    def zone(self, a, end, *marks):
        self.colat, self.colend = a, end
        for lane in (self.act, self.dve, self.pool):
            lane.wait(*marks)

    def col(self, n):
        a = self.colat
        self.colat += n
        assert self.colat <= self.colend, "columns"
        return self.cols[:, a:a + n]

    def keep(self, n):
        a = self.kept_at
        self.kept_at += n
        assert self.kept_at <= KEPT, "lasting columns"
        return self.cols[:, a:a + n]

    def cst(self, name):
        a, n = PLACE[name]
        assert a < NLAST or self.cstf is not None
        return self.cstt[:, a:a + n] if a < NLAST else self.cstf[:, a - NLAST:a - NLAST + n]

    def rstd_steps(self, ss, n, scale, *marks, rest=None, eps=EPS):
        w, free = self.newton.take()
        v, r0, a, b = (w[:, 8 * i:8 * i + n] for i in range(4))
        r = self.col(n)
        if rest is None:
            m = self.ts(v, ss, scale, ALU.mult, *marks, free, s2=eps, op1=ALU.add, lane=self.pool)
        else:
            m = self.stt(v, ss, eps, rest, ALU.add, ALU.add, *marks, free)
        m = self.tt(r0, v, self.cst("mhalf")[:, 0:n], ALU.pow, m, lane=self.pool)
        yield self.after(m)
        m = self.tt(a, r0, r0, ALU.mult, m)
        m = self.stt(b, a, -0.5, v, ALU.mult, ALU.mult, m)
        m = self.stt(r, b, 1.5, r0, ALU.add, ALU.mult, m)
        self.newton.give(w, m)
        return r, m

    def rstd(self, *args, **kw):
        steps = self.rstd_steps(*args, **kw)
        next(steps)
        return finish(steps)


    def after(self, *marks, take=()):
        return when(list(marks)), take

    def start(self, gen, *marks, take=(), first=False):
        thread = [gen, when(list(marks)), take]
        self.live.insert(0 if first else len(self.live), thread)

    def due(self, thread):
        time = thread[1]
        for turns, n in thread[2]:
            if len(turns.free) < n:
                return math.inf
            time = max([time] + [when(turns.free[i][1]) for i in range(n)])
        return time

    def eager(self, limit=math.inf, most=math.inf):
        moved, end = True, self.pe.clock + most
        while moved and self.pe.clock < end:
            moved = False
            for thread in list(self.live):
                if self.due(thread) <= min(self.pe.clock, limit):
                    self.step(thread)
                    moved = True

    def step(self, thread):
        got = next(thread[0], None)
        if got is None:
            self.live.remove(thread)
        else:
            thread[1:] = got

    def turn(self):
        self.eager(self.dve.clock)
        self.fill()
        self.top()
        self.eager(most=self.most)

    def skip(self, limit=math.inf):
        time = min([self.due(thread) for thread in self.live], default=math.inf)
        if time < limit:
            self.pe.clock = max(self.pe.clock, time)
        return time < limit

    def until(self, done):
        while not done():
            self.turn()
            if not done() and not self.skip():
                assert False, "nothing can go on"

    def drain(self):
        self.until(lambda: not self.live)

    def run(self, gen):
        for _ in gen:
            self.turn()


    def fill(self):
        while self.backing:
            time = max(self.back[1], self.dve.clock)
            if time + self.haste >= self.pe.clock:
                return
            self.push()

    def push(self):
        self.back[1] = next(self.back[0], (math.inf,))[0]

    def halt(self):
        self.backing = False
        while self.halfway:
            self.push()


    def feed(self, halves):
        self.todo.extend(halves)

    def top(self, most=8, force=False):
        while self.todo and self.stages.free and most:
            key, half = self.todo[0]
            if half == 0 and key not in self.opened:
                if not self.slots:
                    return
                self.opened[key] = self.piece(key)
            w, load, slot = self.opened[key]
            if when(load) > self.pe.clock + 1.0 and not force or self.holding and key[0] not in ("gu", "wd"):
                return
            if not force and when(self.stages.free[0][1]) > self.act.clock + self.slack:
                return
            most -= 1
            self.todo.popleft()
            st, free = self.stages.take()
            hi, lo, _ = st
            src = w[:, half * 1024:half * 1024 + 1024]
            m = self.acp(hi[:, :], src, load, free)
            m = self.tt(lo[:, :], src, hi[:, :].bitcast(F32), ALU.subtract, m, load, free)
            if half == 1:
                self.piece_done(slot, m)
            self.ready.append((key, half, st, m))

    def staged(self, key, half):
        if not self.ready:
            self.top(1, force=True)
        k, h, st, m = self.ready.popleft()
        assert (k, h) == (key, half), (k, h, key, half)
        while self.pe.clock < when(m) and self.skip(when(m)):
            self.eager()
        return st[0], st[1], m, st

    def bank(self):
        self.until(lambda: self.psum.free)
        return self.psum.take()

    def feature_major(self, key, then, hm):
        bank, free = self.bank()
        for c in (0, 1):
            hi, lo, m, st = self.staged(key, c)
            for kt in range(8):
                s = slice(kt * 128, kt * 128 + 128)
                d = self.mm3(bank[:, c * 256:c * 256 + 256], (hi[:, s], lo[:, s]),
                             (self.hh[:, kt, :], self.hl[:, kt, :]), kt == 0, kt == 7, m, free, hm[kt // 2],
                             signal=kt == 7)
                if kt == 3:
                    yield
            self.stages.give(st, d)
            if c == 1:
                self.hread = d
                self.start(then(bank, d), d)
            yield

    def token_major(self, key, then, hm):
        bank, free = self.bank()
        for half in (0, 1):
            hi, lo, m, st = self.staged(key, half)
            for t in (0, 1):
                for kk in range(4):
                    kt = half * 4 + kk
                    s = slice(kk * 256, kk * 256 + 256)
                    q = slice(t * 128, t * 128 + 128)
                    d = self.mm3(bank[:, t * 256:t * 256 + 256], (self.hh[:, kt, q], self.hl[:, kt, q]),
                                 (hi[:, s], lo[:, s]), kt == 0 and t == 0, kt == 7, m, free, hm[kt // 2],
                                 signal=kk == 3 and t == 1)
                if t == 0:
                    yield
            self.stages.give(st, d)
            if half == 1:
                self.hread = d
                self.start(then(bank, d), d)
            yield

    def project_open(self):
        self.until(lambda: len(self.psum.free) >= 4)
        self.sums = [self.psum.take() for _ in range(4)]
        self.sumsm = [None] * 4

    def project(self, items, first=False, last=False):
        got = [self.staged(key, half) for key, half, _, _ in items]
        for t in (0, 1):
            for nh in (0, 1):
                for (hi, lo, m, _), (_, _, (yh, yl), mark) in zip(got, items):
                    s = slice(nh * 512, nh * 512 + 512)
                    q = slice(t * 128, t * 128 + 128)
                    bank, free = self.sums[t * 2 + nh]
                    end = last and hi is got[-1][0]
                    d = self.mm3(bank[:, :], (yh[:, q], yl[:, q]), (hi[:, s], lo[:, s]), first and hi is got[0][0], end,
                                 m, free, mark, signal=end or (t == 1 and nh == 1))
                    if end:
                        self.sumsm[t * 2 + nh] = d
            if t == 0 and not last:
                self.turn()
        for _, _, _, st in got:
            self.stages.give(st, d)
        return d


    def open_squares(self):
        self.ss, self.ssm = self.col(4), []

    def square(self, t, nh, src, m):
        junk, free = self.junk.take()
        a = self.fn(junk[:, :], src, ACT.Square, m, free, scale=1 / 32, accum=self.ss[:, 2 * t + nh:2 * t + nh + 1])
        self.junk.give(junk, a)
        self.ssm.append(a)

    def add_sums(self, gate=None, tmp=None, each=None, order=((0, 0), (0, 1), (1, 0), (1, 1))):
        new = {}
        for t, nh in order:
            bank, _ = self.sums[t * 2 + nh]
            done = self.sumsm[t * 2 + nh]
            s = slice(nh * 512, nh * 512 + 512)
            xs = self.x[:, t, s]
            if gate is None:
                m = self.tt(xs, bank[:, :], xs, ALU.add, done, self.xmarks[t])
                self.psum.give(bank, m)
            else:
                f, free = tmp.take()
                m = self.tt(f[:, :], bank[:, :], gate[0][:, s], ALU.mult, done, gate[1], free)
                self.psum.give(bank, m)
                m = self.tt(xs, f[:, :], xs, ALU.add, m, self.xmarks[t])
                tmp.give(f, m)
            new[t, nh] = m
            if each is not None:
                each(t, nh, xs, m)
        self.xmarks = [[new[t, 0], new[t, 1]] for t in (0, 1)]

    def scale_steps(self):
        return self.rstd_steps(self.ss[:, 0:4:2], 2, None, self.ssm, rest=self.ss[:, 1:4:2])

    def scales(self):
        steps = self.scale_steps()
        next(steps)
        return finish(steps)

    def diagonals(self, r, m, also=0):
        args = [(r[:, t + also:t + also + 1], ALU.mult) if also else (None, None) for t in (0, 1)]
        self.dm = [self.ts(self.diag[:, t, :], self.ident, r[:, t:t + 1], ALU.mult, m, self.dread, s2=args[t][0],
                           op1=args[t][1]) for t in (0, 1)]

    def turn_x(self, j, x, marks):
        bank, free = self.psum.take()
        for kk in (0, 1):
            for t in (0, 1):
                o = (kk * 2 + t) * 128
                c = (2 * j + kk) * 128
                d = self.mm(bank[:, o:o + 128], x[:, t, c:c + 128], self.diag[:, t, :], True, True, free, self.dm,
                            marks, signal=kk == 1 and t == 1)
        self.dread = d
        return bank, d

    def front(self, gain, shift, tmp, hfree, x=None, marks=None):
        hm = []
        if x is None:
            x, marks = self.x, self.xmarks
        for j, (bank, d) in enumerate([self.turn_x(j, x, marks) for j in range(4)]):
            pair = slice(2 * j, 2 * j + 2)
            if shift is None:
                for kk in (0, 1):
                    a = self.acp(self.hh[:, 2 * j + kk, :], bank[:, kk * 256:kk * 256 + 256], d, gain[1], hfree,
                                 scale=gain[0][:, 2 * j + kk:2 * j + kk + 1])
                for kk in (0, 1):
                    kt = 2 * j + kk
                    m = self.stt(self.hl[:, kt, :], bank[:, kk * 256:kk * 256 + 256], gain[0][:, kt:kt + 1],
                                 self.hh[:, kt, :].bitcast(F32), ALU.mult, ALU.subtract, a, d, gain[1], hfree)
                self.psum.give(bank, m)
            else:
                f, free = tmp.take()
                for kk in (0, 1):
                    kt = 2 * j + kk
                    s = slice(kk * 256, kk * 256 + 256)
                    a = self.fn(f[:, s], bank[:, s], ACT.Identity, d, free, gain[1], shift[1],
                                scale=gain[0][:, kt:kt + 1], bias=shift[0][:, kt:kt + 1])
                self.psum.give(bank, a)
                m = self.cp(self.hh[:, pair, :], blocks(f[:, :], 256), a, hfree)
                m = self.tt(self.hl[:, pair, :], blocks(f[:, :], 256), self.hh[:, pair, :].bitcast(F32), ALU.subtract, m)
                tmp.give(f, m)
            hm.append(m)
            if j > 1:
                self.top(1)
        return hm


def first_mixer(k, base):
    at = base

    def room(*shape):
        nonlocal at
        t = k.sb([128, *shape], at)
        at += int(np.prod(shape)) * 4
        return t

    kq = room(4, 2, 256)
    zg = room(2, 512)
    AQ = room(8, 256)
    tat = at
    T, Tt = ([k.sb([128, 4, 64], tat + 2048 * c + 1024 * i) for c in (0, 1)] for i in (0, 1))
    at += 4096
    TT = room(8, 128)
    vTat = at
    vT = room(4, 256)
    vBat = at
    vB = room(8, 128)
    qb, kb = room(4, 256), room(4, 256)
    vb = room(2, 512)
    ys = Turns([room(256) for _ in range(4)])
    Ss = Turns([room(384) for _ in range(3)])
    PTs = Turns([room(384) for _ in range(4)])
    biases = Turns([k.sb([128, 384], k.gbufat + 1536 * i) for i in range(2)])
    bs = k.sb([8, 768], tat)
    k.first_constants(at)
    AM = [k.sb([128, 4, 64], k.ylat + 2048 * c) for c in (0, 1)]
    X = [k.sb([128, 4, 64], k.yhat + 2048 * c) for c in (0, 1)]
    r1, qs = k.sb([128, 4, 128], k.ylat), k.sb([128, 4, 128], k.ylat + 2048)
    kd, S1 = k.sb([128, 4, 128], tat), k.sb([128, 4, 128], tat + 2048)
    o = k.sb([128, 8, 128], tat)
    vn = [k.sb([128, 4, 128], vTat), k.sb([128, 4, 128], vTat + 2048)]
    k.junk = Turns([k.sb([128, 512], tat), k.sb([128, 512], tat + 2048)])

    zeroed = k.dve.do(lambda e: e.memset(TT[64:128, :, 0:64], 0.0))
    cst, col, mul, add, sub = k.cst, k.col, ALU.mult, ALU.add, ALU.subtract
    ones, ident, psum = cst("ones"), k.ident, k.psum
    k.open_squares()
    for t in (0, 1):
        for nh in (0, 1):
            k.square(t, nh, k.x[:, t, nh * 512:nh * 512 + 512], k.xmarks[t][nh])
    squared = k.ssm
    for lane in (k.pe, k.act, k.dve, k.pool):
        lane.wait(k.oncem)
    k.diagonals(*k.scales())
    k.top(2, force=True)
    hm = k.front((cst("ln1"), k.oncem), None, None, [])
    for lane in (k.pe, k.act, k.dve, k.pool):
        lane.wait(k.lastm)
    taps = cst("conv")
    kqm, vm, zm, ssm = {}, {}, {}, []
    sbank, sfree = psum.take()

    def conv_piece(kind, pair):
        def then(bank, d):
            yield k.after(d, take=[(ys, 2)])
            got = []
            for c in (0, 1):
                y, yfree = ys.take()
                chunk = {"q": 0, "k": 4, "v": 8}[kind] + pair * 2 + c
                w = taps[:, chunk * 4:chunk * 4 + 4]
                a = k.acp(y[:, :], bank[:, c * 256:c * 256 + 256], d, yfree, k.cmark, scale=w[:, 3:4])
                got.append([y, w, a])
            last = a
            for c, item in enumerate(got):
                y, w, _ = item
                m = last
                for j in (1, 2, 3):
                    m = k.stt(y[:, j:256], bank[:, c * 256:c * 256 + 256 - j], w[:, 3 - j:4 - j], y[:, j:256], mul, add, m, d)
                item[2] = m
            psum.give(bank, m)
            yield k.after(m)
            if kind == "v":
                for c, (y, _, m) in enumerate(got):
                    h = pair * 2 + c
                    got[c][2] = k.fn(vT[:, h, :], y[:, :], ACT.Tanh, m, scale=0.5)
                yield k.after(got[1][2])
                for c, (y, _, a) in enumerate(got):
                    h = pair * 2 + c
                    vm[h] = k.stt(vT[:, h, :], vT[:, h, :], 1.0, y[:, :], add, mul, a)
                    ys.give(y, vm[h])
                meet("value")
                return
            for c, (y, _, m) in enumerate(got):
                h = pair * 2 + c
                dest = kq[:, h, int(kind == "q"), :]
                a = k.fn(dest, y[:, :], ACT.Silu, m)
                kqm[kind, h] = a
                got[c][2] = k.fn(y[:, :], dest, ACT.Square, a)
            yield k.after(got[1][2])
            for c, (y, _, a) in enumerate(got):
                i = (kind == "q") * 4 + pair * 2 + c
                n = len(ssm)
                s = k.mm(sbank[0:8, 0:256], cst("rowsum")[:, i * 8:i * 8 + 8], y[:, :], n == 0, n == 7, a, sfree,
                         signal=True)
                ys.give(y, s)
                ssm.append(s)
            if len(ssm) == 8:
                meet("delta")
        return then

    def z_piece(pair):
        def then(bank, d):
            s = slice(pair * 256, pair * 256 + 256)
            yield k.after(d)
            a = k.fn(zg[:, :, s], blocks(bank[:, :], 256), ACT.Tanh, d, scale=0.5)
            yield k.after(a)
            m = k.stt(zg[:, :, s], zg[:, :, s], 1.0, blocks(bank[:, :], 256), add, mul, a, d)
            psum.give(bank, m)
            for t in (0, 1):
                zm[pair, t] = k.stt(blocks(zg[:, t, s], 128), blocks(zg[:, t, s], 128), 0.5, again(cst("gain"), 2, 128),
                                    mul, mul, m)
            if len(zm) == 4:
                meet("norm0")
                meet("norm1")
        return then

    qbm, kbm, vbm = {}, {}, {}

    def swa_qk(dest, marks, pair, scale):
        def then(bank, d):
            a = k.acp(dest[:, 2 * pair:2 * pair + 2, :], blocks(bank[:, :], 256), d, scale=scale)
            psum.give(bank, a)
            marks[pair] = a
            return
            yield
        return then

    def swa_v(pair):
        def then(bank, d):
            a = k.acp(vb[:, :, pair * 256:pair * 256 + 256], blocks(bank[:, :], 256), d)
            psum.give(bank, a)
            vbm[pair] = a
            for h in range(pair * 4, pair * 4 + 4):
                k.start(head(h), qbm[pair], kbm[pair], take=[(psum, 1), (Ss, 1), (biases, 1)])
            return
            yield
        return then

    ym = {}
    outs = {}

    def head(h):
        parts = (slice(0, 128), slice(128, 384))
        ch, r = h // 2, slice(64 * (h % 2), 64 * (h % 2) + 64)
        pair = ch // 2
        bt, bfree = biases.take()
        b = k.acp(bt[:, :], cst("dist"), bfree, k.morem, scale=float(2.0 ** -(h + 1)))
        bank, free = psum.take()
        k.mm(bank[:, 0:128], qb[r, ch, 0:128], kb[r, ch, 0:128], True, True, qbm[pair], kbm[pair], free)
        d = k.mm(bank[:, 128:384], qb[r, ch, 128:256], kb[r, ch, :], True, True, signal=True)
        S, f = Ss.take()
        yield k.after(d, b)
        nm, den, inv = col(2), col(2), col(2)
        ms = [k.ttr(S[:, p], bank[:, p], bt[:, p], add, ALU.min, FAR * 4, nm[:, i:i + 1], d, b, f)
              for i, p in enumerate(parts)]
        psum.give(bank, ms[1])
        biases.give(bt, ms[1])
        yield k.after(ms)
        es = [k.fn(S[:, p], S[:, p], ACT.Exp, ms[i], bias=nm[:, i:i + 1], scale=-1.0) for i, p in enumerate(parts)]
        yield k.after(es)
        cs = [k.ttr(S[:, p], S[:, p], cst("count")[:, p], mul, add, 0.0, den[:, i:i + 1], es[i], k.morem)
              for i, p in enumerate(parts)]
        rv = k.rec(inv, den, cs)
        for i, p in enumerate(parts):
            m = k.ts(S[:, p], S[:, p], inv[:, i:i + 1], mul, rv)
        yield k.after(m, take=[(psum, 1)])
        bank, free = psum.take()
        for j in range(3):
            d = k.tr(bank[:, j * 128:j * 128 + 128], S[:, j * 128:j * 128 + 128], m, free, signal=j == 2)
        Ss.give(S, d)
        yield k.after(d, take=[(PTs, 1)])
        PT, f = PTs.take()
        a = k.acp(PT[:, :], bank[:, 0:384], d, f)
        psum.give(bank, a)
        both = outs.setdefault(ch, [])
        both.append((r, slice(h * 64, h * 64 + 64), PT, a))
        if len(both) == 2:
            yield k.after(a, vbm[pair], take=[(psum, 1)])
            bank, free = psum.take()
            for r, v, PT, a in both:
                k.mm(bank[r, 0:256], vb[:, 0, v], PT[:, 0:256], True, False, a, vbm[pair], free)
            for r, v, PT, a in both:
                d = k.mm(bank[r, 128:256], vb[:, 1, v], PT[:, 256:384], False, True, signal=True)
                PTs.give(PT, d)
            yield k.after(d)
            a = k.acp(k.yh[:, 4 + ch, :], bank[:, 0:256], d)
            m = k.tt(k.yl[:, 4 + ch, :], bank[:, 0:256], k.yh[:, 4 + ch, :].bitcast(F32), sub, a)
            psum.give(bank, m)
            ym[4 + ch] = m


    arrivals = {}

    def meet(name):
        arrivals[name] = arrivals.get(name, 0) + 1
        if name == "delta" and arrivals[name] == 2:
            k.start(delta(), ssm[-1], first=True)
        if name == "value" and arrivals[name] == 3:
            for c in (0, 1):
                k.start(value(c), [vm[h] for h in range(4)], g["beta"], take=[(psum, 1)])
        if name == "first" and arrivals[name] == 2:
            k.start(first_chunk(), tm[0], ttm[0], bvm[0], g["ekd"], take=[(psum, 2)], first=True)
        if name == "second" and arrivals[name] == 3:
            k.start(second_chunk(), state[0][2], ttm, bvm[1], first=True)
        for c in (0, 1):
            if name == f"norm{c}" and arrivals[name] == 2:
                k.start(norm(c), om[c])
            if name == f"write{c}" and arrivals[name] == 2:
                k.start(write(c), normed[c], g["free"], take=[(psum, 1)], first=True)

    cum, tot, av, rv, sv, er, es, ekd, beta, gl = (col(8) for _ in range(10))
    y2, sp, ss, lnr = col(16), col(16), col(16), col(16)
    g = {}

    def logits():
        bank, free = psum.take()
        wba = cst("wba")
        for kt in range(8):
            for i, part in enumerate((k.hh, k.hl)):
                d = k.mm(bank[32 * i:32 * i + 8, 0:256], wba[:, kt * 8:kt * 8 + 8], part[:, kt, :].bitcast(F32), kt == 0,
                         kt == 7, free, hm, k.cmark, signal=kt == 7)
        yield k.after(d)
        k.cp(bs[0:8, 0:256], bank[0:8, 0:256], d)
        m = k.cp(bs[0:8, 256:512], bank[32:40, 0:256], d)
        psum.give(bank, m)
        yield k.after(m, take=[(psum, 1)])
        bank, free = psum.take()
        for t in (0, 1):
            for i in (0, 1):
                q = slice(i * 256 + t * 128, i * 256 + t * 128 + 128)
                d = k.mm(bank[:, t * 8:t * 8 + 8], bs[0:8, q], ident[0:8, 0:8], i == 0, i == 1, m, free, signal=True)
        yield k.after(d)
        b3 = blocks(bank[:, 0:16], 8)
        k.ts(blocks(y2[:, 0:8], 4), b3[:, :, 0:4], -1.0, mul, d)
        m = k.tt(blocks(y2[:, 8:16], 4), b3[:, :, 4:8], again(cst("dtb"), 2, 4), add, d)
        psum.give(bank, m)
        ab, u, w, lw, den, ea = (col(16) for _ in range(6))
        m = k.stt(ab, y2, -1.0, y2, mul, ALU.max, m)
        yield k.after(m)
        uu = k.fn(u, ab, ACT.Exp, m, scale=-1.0)
        em = k.fn(ea[:, 0:4], cst("alog"), ACT.Exp, k.cmark)
        yield k.after(uu)
        wm = k.ts(w, u, 1.0, add, uu)
        dm = k.ts(den, w, -1.0, add, wm, s2=1e-30, op1=add)
        dm = k.rec(den, den, dm)
        yield k.after(wm)
        lm = k.fn(lw, w, ACT.Ln, wm)
        k.start(k.setup(vBat), k.morem)
        yield k.after(lm)
        m = k.stt(lw, lw, 1e-30, u, add, mul, lm)
        m = k.tt(lw, lw, den, mul, m, dm)
        g["sp"] = m = k.stt(sp, y2, 0.0, lw, ALU.max, add, m)
        m = k.stt(blocks(gl, 4), blocks(sp[:, 8:16], 4), -1.0, again(ea[:, 0:4], 2, 4), mul, mul, m, em)
        yield k.after(m, take=[(psum, 1)])
        bank, free = psum.take()
        k.mm(bank[:, 0:8], cst("tri"), gl, True, True, m, free)
        d = k.mm(bank[:, 8:16], ones, gl, True, True, signal=True)
        yield k.after(d)
        k.cp(cum, bank[:, 0:8], d)
        m = k.cp(tot, bank[:, 8:16], d)
        psum.give(bank, m)
        g["cum"] = m
        meet("delta")

    def delta():
        m = k.cp(bs[0:8, 512:768], sbank[0:8, 0:256], ssm)
        psum.give(sbank, m)
        yield k.after(m, take=[(psum, 1)])
        bank, free = psum.take()
        for t in (0, 1):
            q = slice(512 + t * 128, 512 + t * 128 + 128)
            d = k.mm(bank[:, 16 + t * 8:24 + t * 8], bs[0:8, q], ident[0:8, 0:8], True, True, m, free, signal=t == 1)
        yield k.after(d)
        s3 = blocks(bank[:, 16:32], 8)
        k.cp(blocks(ss[:, 0:8], 4), s3[:, :, 0:4], d)
        m = k.cp(blocks(ss[:, 8:16], 4), s3[:, :, 4:8], d)
        psum.give(bank, m)
        yield k.after(m)
        lm = k.fn(lnr, ss, ACT.Ln, m, k.lastm, bias=cst("eps"))
        yield k.after(lm)
        lm = k.ts(lnr, lnr, -0.5, mul, lm)
        lnk, lnq = lnr[:, 0:8], lnr[:, 8:16]
        m1 = k.tt(rv, cum, sp[:, 0:8], sub, g["cum"], g["sp"])
        g["av"] = k.tt(av, lnk, cum, sub, lm)
        g["sv"] = k.stt(sv, cum, -0.5 * float(np.log(128.0)), lnq, add, add, lm)
        g["rv"] = k.tt(rv, rv, lnk, add, m1)
        m = k.tt(ekd, tot, av, add, g["av"])
        for i in range(4):
            k.start(decay(i), g["rv"], g["sv"], take=[(psum, 1)])
        yield k.after(m)
        g["er"] = k.fn(er, rv, ACT.Exp, g["rv"])
        g["es"] = k.fn(es, sv, ACT.Exp, g["sv"])
        g["ekd"] = k.fn(ekd, ekd, ACT.Exp, m)
        m = k.fn(beta, sp[:, 0:8], ACT.Exp, g["sp"], scale=-1.0)
        yield k.after(m)
        g["beta"] = k.ts(beta, beta, 0.5, mul, m)
        k.start(k.lambdas())
        meet("value")

    rows = (slice(0, 64), slice(64, 128))
    aqm = [[], []]

    def decay(i):
        us = (2 * i, 2 * i + 1)
        bank, free = psum.take()
        for u in us:
            o = (u % 2) * 256
            own = rv[:, u:u + 1].to_broadcast([128, 64])
            k.mm(bank[0:64, o:o + 128], own, ident, True, True, g["rv"], free)
            for j in (0, 1):
                k.mm(bank[64:128, o + j * 64:o + j * 64 + 64], own, ident[:, rows[1 - j]], True, True)
            d = k.row(bank[:, o + 128:o + 256], sv[:, u:u + 1], g["sv"], signal=True)
        yield k.after(d)
        m = k.tt(AQ[:, 2 * i:2 * i + 2, :], blocks(bank[:, :], 256), again(cst("gmask"), 2, 256), add, d, k.morem)
        psum.give(bank, m)
        yield k.after(m, take=[(psum, 1)])
        bank, free = psum.take()
        for u in us:
            a = k.fn(AQ[:, u, :], AQ[:, u, :], ACT.Exp, m, g["av"], bias=av[:, u:u + 1])
        for u in us:
            c, h = u // 4, u % 4
            s = slice(c * 128, c * 128 + 128)
            o = (u % 2) * 256
            keys = kq[:, h, 0, s]
            d = k.mm(blocks(bank[0:64, o:o + 256], 128), keys[:, rows[0]], kq[:, h, :, s], True, True, kqm["k", h],
                     kqm["q", h], free)
            for j in (0, 1):
                k.mm(bank[64:128, o + j * 64:o + j * 64 + 64], keys[:, rows[1]], keys[:, rows[1 - j]], True, True)
            d = k.mm(bank[64:128, o + 128:o + 256], keys[:, rows[1]], kq[:, h, 1, s], True, True, signal=True)
        yield k.after(a, d)
        m = k.tt(AQ[:, 2 * i:2 * i + 2, :], AQ[:, 2 * i:2 * i + 2, :], blocks(bank[:, :], 256), mul, a, d)
        psum.give(bank, m)
        c = i // 2
        aqm[c].append(m)
        if len(aqm[c]) == 2:
            k.start(solve(c), aqm[c], first=True)

    def bank4(f, *marks):
        bank, free = psum.take()
        for h in range(4):
            l, r = f(h)
            d = k.mm(bank[:, h * 128:h * 128 + 128], l, r, True, True, free, *marks, signal=h == 3)
        return bank, blocks(bank[:, :], 128), d

    def turned4(f, *marks):
        bank, free = psum.take()
        for h in range(4):
            d = k.tr(bank[:, h * 128:h * 128 + 128], f(h), free, *marks, signal=h == 3)
        return bank, blocks(bank[:, :], 128), d

    def tiles(f, *marks):
        bank, free = psum.take()
        for h in range(4):
            for r in rows:
                l, right = f(h, r)
                d = k.mm(bank[r, h * 64:h * 64 + 64], l, right, True, True, free, *marks, signal=h == 3)
        return bank, blocks(bank[:, 0:256], 64), d

    lvl, twice = cst("level"), cst("twice")
    tm, ttm, amread, xread = [None, None], [None, None], [None, None], [None, None]

    def solve(c):
        us = slice(c * 4, c * 4 + 4)

        def masked(l):
            return k.tt(AM[c][:, :, :], AQ[:, us, 0:64], again(lvl[:, l * 64:l * 64 + 64], 4, 64), mul, aqm[c], k.morem,
                        amread[c])

        t, tt, x, am = T[c], Tt[c], X[c], AM[c]
        m = masked(0)
        ttm[c] = amread[c] = k.tt(tt[:, :, :], again(twice, 4, 64), am[:, :, :], sub, m, squared)
        yield k.after(ttm[c], take=[(psum, 1)])
        bank, b, d = tiles(lambda h, r: (tt[r, h, :], twice[r, :]), ttm[c])
        m = masked(1)
        yield k.after(d)
        tm[c] = k.acp(t[:, :, :], b, d, squared)
        psum.give(bank, tm[c])
        for l in range(1, 6):
            yield k.after(m, tm[c], take=[(psum, 1)])
            bank, b, d = tiles(lambda h, r: (am[r, h, :], t[r, h, :]), m, tm[c])
            amread[c] = d
            yield k.after(d)
            xm = k.acp(x[:, :, :], b, d, xread[c])
            psum.give(bank, xm)
            if l < 5:
                m = masked(l + 1)
            yield k.after(xm, ttm[c], take=[(psum, 2)])
            bank, b, d = tiles(lambda h, r: (tt[r, h, :], x[r, h, :]), xm, ttm[c])
            bank2, b2, d2 = tiles(lambda h, r: (x[r, h, :], tt[r, h, :]), xm, ttm[c])
            xread[c] = d2
            yield k.after(d)
            tm[c] = k.tt(t[:, :, :], t[:, :, :], b, sub, d, tm[c])
            psum.give(bank, tm[c])
            yield k.after(d2)
            if l < 5:
                ttm[c] = k.tt(tt[:, :, :], tt[:, :, :], b2, sub, d2)
                psum.give(bank2, ttm[c])
        for r in rows:
            ttm[c] = k.tt(TT[r, us, r], tt[r, :, :], b2[r], sub, d2, xm)
        psum.give(bank2, ttm[c])
        yield k.after(tm[c], take=[(psum, 1)])
        bank, free = psum.take()
        for h in range(4):
            d = k.mm(bank[64:128, h * 64:h * 64 + 64], AQ[0:64, c * 4 + h, 64:128], t[0:64, h, :], True, True, tm[c], free,
                     signal=h == 3)
        yield k.after(d)
        xm = k.acp(x[64:128, :, :], blocks(bank[64:128, 0:256], 64), d, xread[c])
        yield k.after(xm, ttm[c])
        for h in range(4):
            d = k.mm(bank[0:64, h * 64:h * 64 + 64], x[64:128, h, :], TT[64:128, c * 4 + h, 64:128], True, True, xm, ttm[c],
                     signal=h == 3)
        xread[c] = d
        yield k.after(d)
        ttm[c] = k.ts(TT[0:64, us, 64:128], blocks(bank[0:64, 0:256], 64), -1.0, mul, d, ttm[c], zeroed)
        psum.give(bank, ttm[c])
        if c == 0:
            meet("first")
        meet("second")

    bvm, vread = {}, {}

    def value(c):
        bank, b, d = turned4(lambda h: vT[:, h, c * 128:c * 128 + 128], *[vm[h] for h in range(4)])
        yield k.after(d)
        bvm[c] = k.tt(vB[:, c * 4:c * 4 + 4, :], b, spread(beta[:, c * 4:c * 4 + 4], 4, 128), mul, d, g["beta"],
                      k.t5m)
        psum.give(bank, bvm[c])
        vread[c] = d
        if c == 0:
            meet("first")

    om, state, kdread = [None, None], [], []

    def first_chunk():
        bank, b, d = turned4(lambda h: kq[:, h, 0, 0:128])
        bank2, b2, d2 = bank4(lambda h: (TT[:, h, :], vB[:, h, :]), ttm[0], bvm[0])
        yield k.after(d)
        kdm = k.tt(kd[:, :, :], b, spread(ekd[:, 0:4], 4, 128), mul, d, g["ekd"], ttm[0])
        psum.give(bank, kdm)
        yield k.after(d2, list(vread.values()))
        vnm = k.acp(vn[0][:, :, :], b2, d2, list(vread.values()))
        psum.give(bank2, vnm)
        yield k.after(vnm, kdm, take=[(psum, 2)])
        bank, b, d = bank4(lambda h: (kd[:, h, :], vn[0][:, h, :]), vnm, kdm)
        bank2, b2, d2 = bank4(lambda h: (AQ[:, h, 128:256], vn[0][:, h, :]), vnm, aqm[0])
        kdread.append(d)
        yield k.after(d2)
        om[0] = k.cp(o[:, 0:4, :], b2, d2, kdread)
        psum.give(bank2, om[0])
        state.append((bank, b, d))
        meet("norm0")
        meet("second")

    def second_chunk():
        bank, b, d = state[0]
        s1m = k.acp(S1[:, :, :], b, d, ttm[1])
        psum.give(bank, s1m)
        yield k.after(s1m, take=[(psum, 2)])
        bank, b, d = bank4(lambda h: (kq[:, h, 0, 128:256], S1[:, h, :]), s1m)
        bank2, b2, d2 = bank4(lambda h: (kq[:, h, 1, 128:256], S1[:, h, :]), s1m)
        yield k.after(d)
        m = k.tt(r1[:, :, :], b, spread(er[:, 4:8], 4, 128), mul, d, g["er"], amread)
        psum.give(bank, m)
        rm = k.tt(r1[:, :, :], vB[:, 4:8, :], r1[:, :, :], sub, m, bvm[1])
        yield k.after(rm, d2, take=[(psum, 1)])
        qsm = k.tt(qs[:, :, :], b2, spread(es[:, 4:8], 4, 128), mul, d2, g["es"], amread)
        psum.give(bank2, qsm)
        sread = d2
        bank, b, d = bank4(lambda h: (TT[:, 4 + h, :], r1[:, h, :]), rm, ttm[1])
        yield k.after(d)
        vnm = k.acp(vn[1][:, :, :], b, d, list(vread.values()))
        psum.give(bank, vnm)
        yield k.after(vnm, take=[(psum, 1)])
        bank, b, d = bank4(lambda h: (AQ[:, 4 + h, 128:256], vn[1][:, h, :]), vnm, aqm[1])
        g["free"] = [qsm, d]
        yield k.after(d, qsm)
        om[1] = k.tt(o[:, 4:8, :], b, qs[:, :, :], add, d, qsm, sread)
        g["free"].append(om[1])
        psum.give(bank, om[1])
        meet("norm1")
        meet("write0")
        meet("write1")

    normed = [None, None]

    def norm(c):
        us = slice(c * 4, c * 4 + 4)
        sq = k.sb([128, 4, 128], base + 12288 + 4096 * c)
        ss = col(4)
        for h in range(4):
            a = k.fn(sq[:, h, :], o[:, c * 4 + h, :], ACT.Square, om[c], accum=ss[:, h:h + 1])
        zs = [zm[pair, c] for pair in (0, 1)]
        m = k.tt(o[:, us, :], o[:, us, :], blocks(zg[:, c, :], 128), mul, a, zs)
        r, rm = yield from k.rstd_steps(ss, 4, 1.0 / 128, a)
        normed[c] = k.tt(o[:, us, :], o[:, us, :], spread(r, 4, 128), mul, rm, m)
        meet(f"write{c}")

    def write(c):
        bank, b, d = turned4(lambda h: o[:, c * 4 + h, :], normed[c])
        yield k.after(d)
        q = slice(c * 128, c * 128 + 128)
        a = k.acp(k.yh[:, 0:4, q], b, d, xread)
        m = k.tt(k.yl[:, 0:4, q], b, k.yh[:, 0:4, q].bitcast(F32), sub, a, d, g["free"])
        psum.give(bank, m)
        g["ym", c] = m

    k.start(logits(), hm, k.cmark, take=[(psum, 1)])
    for pair in (0, 1):
        for kind in "kq":
            k.run(k.feature_major((kind, pair), conv_piece(kind, pair), hm))
            if (kind, pair) == ("k", 0):
                k.more_constants()
    for pair in (0, 1):
        k.run(k.feature_major(("v", pair), conv_piece("v", pair), hm))
    for pair in (0, 1):
        k.run(k.feature_major(("qb", pair), swa_qk(qb, qbm, pair, -0.125), hm))
        k.run(k.feature_major(("kb", pair), swa_qk(kb, kbm, pair, None), hm))
        k.run(k.token_major(("vb", pair), swa_v(pair), hm))
    for p in (0, 1):
        k.run(k.token_major(("z", p), z_piece(p), hm))
    k.project_open()
    for j in (2, 3):
        for half in (0, 1):
            kt = 2 * j + half
            k.until(lambda: kt in ym)
            k.project([(("wo", j), half, (k.yh[:, kt, :], k.yl[:, kt, :]), ym[kt])], first=kt == 4)
            k.turn()
    k.grow(1)
    k.drain()
    k.grow(2)
    marks = [g["ym", 0], g["ym", 1]]
    for j in (0, 1):
        d = k.project([(("wo", j), half, (k.yh[:, 2 * j + half, :], k.yl[:, 2 * j + half, :]), marks)
                       for half in (0, 1)], last=j == 1)
    k.yread = d
    k.junk = Turns([k.sb([128, 512], tat), k.sb([128, 512], tat + 2048)], marks)
    k.open_squares()
    k.add_sums(each=k.square)


def first_ffn(k, base):
    at = base

    def room(*shape, dt=F32):
        nonlocal at
        t = k.sb([128, *shape], at, dt)
        at += int(np.prod(shape)) * 4
        return t

    ys = Turns([room(256) for _ in range(2)], k.fence)
    squares = [room(512) for _ in range(4)]
    gs = Turns([room(256) for _ in range(2)], k.fence)
    ams = Turns([room(256) for _ in range(2)], k.fence)
    aps = Turns([(room(256, dt=F32R), room(256, dt=F32R)) for _ in range(3)], k.fence)
    lnf = room(1024)
    assert at <= base + k.f2size
    count, src = Count(k.nc, "lnf"), k.lnf
    k.diagonals(*k.scales())
    k.top(2, force=True)
    hm = k.front((k.cst("ln2"), k.lastm), None, None, [k.hread])
    taps = k.cst("fconv")
    k.project_open()
    acts = {}

    def gate_up(c):
        bank, free = k.bank()
        for half in (0, 1):
            hi, lo, m, st = k.staged(("gu", c), half)
            for kt in range(8):
                s = slice(kt * 128, kt * 128 + 128)
                d = k.mm3(bank[:, half * 256:half * 256 + 256], (hi[:, s], lo[:, s]), (k.hh[:, kt, :], k.hl[:, kt, :]),
                          kt == 0, kt == 7, m, free, hm[kt // 2], signal=kt == 7)
                if kt == 3:
                    yield
            k.stages.give(st, d)
            if half == 0:
                gated = d
            else:
                k.hread = d
                k.start(activate(c, bank, d), d, take=[(ys, 1), (gs, 1), (ams, 1), (aps, 1)])
            yield

    def activate(c, bank, d):
        y, yf = ys.take()
        g, gf = gs.take()
        f, ff = ams.take()
        part, af = aps.take()
        w = taps[:, c * 3:c * 3 + 3]
        m = k.acp(y[:, :], bank[:, 0:256], d, yf, scale=w[:, 2:3])
        for j in (1, 2):
            m = k.stt(y[:, j:256], bank[:, 0:256 - j], w[:, 2 - j:3 - j], y[:, j:256], ALU.mult, ALU.add, m, d)
        yield k.after(m)
        a = k.fn(g[:, :], y[:, :], ACT.Silu, m, gf)
        ys.give(y, a)
        yield k.after(a)
        m = k.tt(f[:, :], g[:, :], bank[:, 256:512], ALU.mult, a, d, ff)
        k.psum.give(bank, m)
        gs.give(g, m)
        yield k.after(m)
        a = k.acp(part[0][:, :], f[:, :], m, af)
        yield k.after(a)
        m = k.tt(part[1][:, :], f[:, :], part[0][:, :].bitcast(F32), ALU.subtract, a, m, af)
        ams.give(f, m)
        acts[c] = (part, m)

    def down(*cs):
        k.until(lambda: all(c in acts for c in cs))
        got = [acts.pop(c) for c in cs]
        d = k.project([(("wd", c // 2), c % 2, part, am) for c, (part, am) in zip(cs, got)], cs[0] == 0, cs[-1] == 21)
        for part, _ in got:
            aps.give(part, d)
        if len(cs) == 1:
            k.turn()

    lm = k.act.dma(lambda e: e.dma_start(lnf[:, :], src), count, k.fence, size=1 << 19)
    lnf2m = None
    for c in range(22):
        if c == 21:
            k.backing, k.holding = False, True
            lnf2m = k.fn(k.gbuf[:, :], lnf[:, :], ACT.Square, lm, k.gread)
        k.run(gate_up(c))
        if 2 <= c:
            down(c - 2)
    down(20)
    down(21)
    k.holding = False
    k.open_squares()
    a, am, b, bm = k.ss, [], k.col(4), []

    def scaled(i):
        sq, s = squares[i], slice(i % 2 * 512, i % 2 * 512 + 512)
        bm.append(k.ttr(sq[:, :], sq[:, :], k.gbuf[:, s], ALU.mult, ALU.add, 0.0, b[:, i:i + 1], am[i], lnf2m))

    def each(t, nh, xs, m):
        i = 2 * t + nh
        am.append(k.fn(squares[i][:, :], xs, ACT.Square, m, k.fence, scale=1 / 32, accum=a[:, i:i + 1]))
        if i > 0:
            scaled(i - 1)

    k.add_sums(each=each)
    v, w, u = k.col(2), k.col(2), k.col(8)
    m = k.tt(v, a[:, 0:4:2], a[:, 1:4:2], ALU.add, am, lane=k.pool)
    vm = k.ts(v, v, EPS, ALU.add, m, lane=k.pool)
    m = k.ts(w, v, EPS, ALU.mult, vm, lane=k.pool)
    m = k.tt(w, w, b[:, 0:4:2], ALU.add, m, bm, lane=k.pool)
    scaled(3)
    r, rm = k.rstd(w, 2, None, m, bm, rest=b[:, 1:4:2], eps=0.0)
    k.diagonals(r, rm)
    c, m = k.mod[0, 1]
    k.mod[0, 1] = (u, k.tt(u, c, k.cst("lnf"), ALU.mult, m))
    k.gread = bm
    k.later = (lnf, lm, v, vm)


def rescale(k):
    lnf, lm, v, vm = k.later
    r, m = k.rstd(v, 2, 1.0, vm, eps=0.0)
    for t in (0, 1):
        s = k.stt(k.x[:, t, :], k.x[:, t, :], r[:, t:t + 1], lnf[:, :], ALU.mult, ALU.mult, m, lm, k.dread)
        k.xmarks[t] = [s, s]
    k.lnfread = s


def first_halves():
    keys = ([(s, p) for p in (0, 1) for s in "kq"] + [("v", 0), ("v", 1), ("qb", 0), ("kb", 0), ("vb", 0), ("qb", 1),
            ("kb", 1), ("vb", 1), ("z", 0), ("z", 1)] + [("wo", j) for j in (2, 3, 0, 1)])
    seq = [(key, half) for key in keys for half in (0, 1)]
    for c in range(22):
        seq += [(("gu", c), 0), (("gu", c), 1)]
        if c >= 2:
            seq.append((("wd", (c - 2) // 2), c % 2))
    return seq + [(("wd", 10), 0), (("wd", 10), 1)]


def modulation(k):
    for layer in (0, 1):
        for v in range(6):
            c = k.keep(8)
            for s in range(4):
                k.halfway = True
                w, load, slot = k.piece(("ada", layer, v, s))
                yield k.after(load, k.csrm)
                for kk in (0, 1):
                    j = 2 * s + kk
                    part = w[:, kk * 1024:kk * 1024 + 1024]
                    m = k.ttr(part, part, k.csr[:, :], ALU.mult, ALU.add, 0.0, c[:, j:j + 1], load, k.csrm)
                    if kk == 0:
                        yield k.after()
                k.piece_done(slot, m)
                if s == 3:
                    a = (layer * 6 + v) * 8
                    m = k.tt(c, c, k.cst("adab")[:, a:a + 8], ALU.add, m)
                    if v in (1, 4):
                        gain = k.cst("nmix" if v == 1 else "nffn")[:, layer * 8:layer * 8 + 8]
                        m = k.stt(c, c, 1.0, gain, ALU.add, ALU.mult, m)
                    k.mod[layer, v] = (c, m)
                k.halfway = False
                yield k.after()


def need(k, layer, v):
    while (layer, v) not in k.mod:
        k.push()
    return k.mod[layer, v]


def gate_rows(k, layer, v):
    c, m = need(k, layer, v)
    for half in (0, 1):
        yield k.after(m, take=[(k.psum, 1)])
        bank, free = k.psum.take()
        for j in range(4):
            i = half * 4 + j
            d = k.row(bank[:, j * 128:j * 128 + 128], c[:, i:i + 1], m, free, signal=j == 3)
        yield k.after(d)
        a = k.acp(k.gbuf[:, half * 512:half * 512 + 512], bank[:, :], d, k.gread)
        k.psum.give(bank, a)
    k.gate = (k.gbuf, a)


def load_bias(k, lane, bias, windows, src, step, first, mark, marks):
    corner = again(k.cst("corner"), 4, 256)
    k.biasm = []

    def flip(g, w, m):
        yield k.after(m)
        m = k.tt(bias[:, g * 4:g * 4 + 4, :], corner, w[0][:, :, 255::-1], ALU.subtract, m, marks)
        windows.give(w, m)
        k.biasm.append(m)

    for g in range(bias.shape[1] // 4):
        yield k.after(mark, marks, take=[(windows, 1)])
        w, free = windows.take()
        at = bass.AP(tensor=src.tensor, offset=g * 4 * step + first, ap=[[1, 128], [step, 4], [1, 256]])
        m = lane.dma(lambda e, w=w, at=at: e.dma_start(w[0][:, :, :], at), w[1], mark, marks, free, size=1 << 19)
        k.start(flip(g, w, m), m)


def second_mixer(k, layer, base, windows):
    at = base

    def room(*shape):
        nonlocal at
        t = k.sb([128, *shape], at)
        at += int(np.prod(shape)) * 4
        return t

    mul, add, sub = ALU.mult, ALU.add, ALU.subtract
    fence = k.fence
    bias = k.bias[layer]
    qTs, kTs, vs = (Turns([room(2, 256) for _ in range(2)], fence) for _ in range(3))
    tmp = Turns([room(512) for _ in range(2)], fence)
    sqs = Turns([room(512) for _ in range(2)], fence)
    ns = Turns([room(512) for _ in range(2)], fence)
    Ss = Turns([room(384) for _ in range((6, 5)[layer])], fence, k.biasm)
    PTs = Turns([room(384) for _ in range((3, 4)[layer])], fence, k.biasm)
    assert at <= base + k.asize, at - base - k.asize
    gain, shift = need(k, layer, 1), need(k, layer, 0)
    for _ in gate_rows(k, layer, 2):
        pass
    if layer == 1:
        k.diagonals(*k.scales())
        k.top(2, force=True)
        hm = k.front(gain, shift, tmp, [k.hread])
    else:
        k.top(2, force=True)
        hm = k.front(gain, shift, tmp, [k.hread])
        rescale(k)
        ns = Turns([n for n, _ in ns.free], fence, k.lnfread)
    gcol = k.col(2)
    gains = k.cst("qk")[:, layer * 2:layer * 2 + 2]
    k.ts(gcol[:, 0:1], gains[:, 0:1], -0.125, mul)
    gm = k.cp(gcol[:, 1:2], gains[:, 1:2])
    parts = (slice(0, 128), slice(128, 384))
    psum = k.psum

    def qk_piece(g, store, which):
        def then(bank, d):
            yield k.after(d, take=[(sqs, 1)])
            sq, f = sqs.take()
            a = k.fn(sq[:, :], bank[:, :], ACT.Square, d, f)
            ss = k.col(8)
            yield k.after(a)
            m = k.red(ss, blocks(sq[:, :], 64), add, a)
            sqs.give(sq, m)
            r, m = yield from k.rstd_steps(ss, 8, 1.0 / 64, m)
            yield k.after(m, take=[(ns, 1)])
            n, f = ns.take()
            m = k.tt(blocks(n[:, :], 64), blocks(bank[:, :], 64), spread(r, 8, 64), mul, m, d, f)
            psum.give(bank, m)
            yield k.after(m, take=[(psum, 1)])
            bank, free = psum.take()
            for j in (0, 1):
                for t in (0, 1):
                    o = (j * 2 + t) * 128
                    d = k.tr(bank[:, o:o + 128], n[:, t * 256 + j * 128:t * 256 + j * 128 + 128], m, free,
                             signal=j == 1 and t == 1)
            ns.give(n, d)
            turns = (qTs, kTs)[which]
            yield k.after(d, take=[(turns, 1)])
            dest, f = turns.take()
            a = k.acp(dest[:, :, :], blocks(bank[:, :], 256), d, f, gm, scale=gcol[:, which:which + 1])
            psum.give(bank, a)
            arrive(g, store, which, dest, a)
        return then

    def v_piece(g, store):
        def then(bank, d):
            yield k.after(d, take=[(vs, 1)])
            v, f = vs.take()
            a = k.acp(v[:, :, :], blocks(bank[:, :], 256), d, f)
            psum.give(bank, a)
            arrive(g, store, 2, v, a)
        return then

    ym, outs = {}, {}

    def arrive(g, store, which, thing, m):
        store[which] = (thing, m)
        if which == 1:
            store["left"] = 2
            for i in range((2, 4)[layer]):
                k.start((double, single)[layer](g, store, i), store[0][1], store[1][1], take=[(psum, 1), (Ss, 1)])
        if which == 2:
            for steps in store.pop("ready", []):
                k.start(steps, m)

    def valued(store, steps):
        if 2 in store:
            yield from steps
        else:
            store.setdefault("ready", []).append(steps)

    def leave(store, d):
        store["left"] -= 1
        if store["left"] == 0:
            for turns, i in ((qTs, 0), (kTs, 1), (vs, 2)):
                turns.give(store[i][0], d)

    def scores(store, j, r):
        (q, qm), (kk, km) = store[0], store[1]
        rows = slice(64 * r, 64 * r + 64)
        bank, free = psum.take()
        k.mm(bank[:, 0:128], q[rows, j, 0:128], kk[rows, j, 0:128], True, True, qm, km, free)
        return bank, k.mm(bank[:, 128:384], q[rows, j, 128:256], kk[rows, j, :], True, True, signal=True)

    def weights(bank, d, head):
        S, f = Ss.take()
        nm, den = k.col(2), k.col(2)
        windows = (bias[:, head, 128:256], bias[:, head, :])
        ms = [k.ttr(S[:, p], bank[:, p], windows[i], add, ALU.min, FAR * 4, nm[:, i:i + 1], d, f, k.biasm)
              for i, p in enumerate(parts)]
        psum.give(bank, ms[1])
        yield k.after(ms)
        es = [k.fn(S[:, p], S[:, p], ACT.Exp, ms[i], bias=nm[:, i:i + 1], scale=-1.0, accum=den[:, i:i + 1])
              for i, p in enumerate(parts)]
        return S, den, es

    def turned(S, m):
        yield k.after(m, take=[(psum, 1)])
        bank, free = psum.take()
        for j in range(3):
            d = k.tr(bank[:, j * 128:j * 128 + 128], S[:, j * 128:j * 128 + 128], m, free, signal=j == 2)
        Ss.give(S, d)
        yield k.after(d, take=[(PTs, 1)])
        PT, f = PTs.take()
        a = k.acp(PT[:, :], bank[:, 0:384], d, f)
        psum.give(bank, a)
        return PT, a

    def single(g, store, i):
        bank, d = scores(store, i // 2, i % 2)
        yield k.after(d)
        S, den, es = yield from weights(bank, d, g * 4 + i)
        yield k.after(es)
        inv = k.col(2)
        rv = k.rec(inv, den, es)
        for j, p in enumerate(parts):
            m = k.ts(S[:, p], S[:, p], inv[:, j:j + 1], mul, rv)
        PT, a = yield from turned(S, m)
        yield from valued(store, single_out(g, store, i, PT, a))

    def single_out(g, store, i, PT, a):
        v, vm = store[2]
        r = slice(64 * (i % 2), 64 * (i % 2) + 64)
        kt = 2 * g + i // 2
        both = outs.setdefault(kt, [])
        both.append((r, slice(i * 64, i * 64 + 64), PT, a))
        if len(both) == 2:
            yield k.after(a, vm, take=[(psum, 1)])
            bank, free = psum.take()
            for r, c, PT, a in both:
                k.mm(bank[r, 0:256], v[:, 0, c], PT[:, 0:256], True, False, a, vm, free)
            for r, c, PT, a in both:
                d = k.mm(bank[r, 128:256], v[:, 1, c], PT[:, 256:384], False, True, signal=True)
                PTs.give(PT, d)
            leave(store, d)
            yield k.after(d)
            a = k.acp(k.yh[:, kt, :], bank[:, 0:256], d, k.yread)
            m = k.tt(k.yl[:, kt, :], bank[:, 0:256], k.yh[:, kt, :].bitcast(F32), sub, a, k.yread)
            psum.give(bank, m)
            ym[kt] = m

    def double(g, store, i):
        bank, d = scores(store, i, 0)
        yield k.after(d)
        S0, den0, e0 = yield from weights(bank, d, 2 * g + i)
        yield k.after(take=[(psum, 1), (Ss, 1)])
        bank, d = scores(store, i, 1)
        yield k.after(d)
        S1, den1, e1 = yield from weights(bank, d, 2 * g + i)
        yield k.after(e0, e1)
        inv0, inv1 = k.col(2), k.col(2)
        r0 = k.rec(inv0, den0, e0)
        r1 = k.rec(inv1, den1, e1)
        cm = k.ts(inv1, inv1, k.neglam, mul, r1, k.neglamm)
        for j, p in enumerate(parts):
            m = k.ts(S1[:, p], S1[:, p], inv1[:, j:j + 1], mul, cm)
            m = k.stt(S0[:, p], S0[:, p], inv0[:, j:j + 1], S1[:, p], mul, add, m, r0)
        Ss.give(S1, m)
        PT, a = yield from turned(S0, m)
        yield from valued(store, double_out(g, store, i, PT, a))

    def double_out(g, store, i, PT, a):
        v, vm = store[2]
        yield k.after(a, vm, take=[(psum, 1)])
        c = slice(i * 128, i * 128 + 128)
        bank, free = psum.take()
        k.mm(bank[:, 0:128], PT[:, 0:128], v[:, 0, c], True, True, a, vm, free)
        k.mm(bank[:, 128:256], PT[:, 128:256], v[:, 0, c], True, False)
        d = k.mm(bank[:, 128:256], PT[:, 256:384], v[:, 1, c], False, True, signal=True)
        PTs.give(PT, d)
        leave(store, d)
        yield k.after(d, take=[(sqs, 1)])
        sq, f = sqs.take()
        ss = k.col(2)
        for t in (0, 1):
            a = k.fn(sq[:, t * 128:t * 128 + 128], bank[:, t * 128:t * 128 + 128], ACT.Square, d, f, accum=ss[:, t:t + 1])
        yield k.after(a)
        r, m = yield from k.rstd_steps(ss, 2, 1.0 / 128, a)
        m = k.tt(blocks(sq[:, 0:256], 128), blocks(bank[:, 0:256], 128), spread(r, 2, 128), mul, m)
        psum.give(bank, m)
        yield k.after(m, take=[(psum, 1)])
        bank, free = psum.take()
        for t in (0, 1):
            d = k.tr(bank[:, t * 128:t * 128 + 128], sq[:, t * 128:t * 128 + 128], m, free, signal=t == 1)
        sqs.give(sq, d)
        yield k.after(d)
        kt = 2 * g + i
        a = k.acp(k.yh[:, kt, :], bank[:, 0:256], d, k.sublnm, k.yread, scale=k.subln)
        yield k.after(a)
        m = k.stt(k.yl[:, kt, :], bank[:, 0:256], k.subln, k.yh[:, kt, :].bitcast(F32), mul, sub, a, d, k.yread)
        psum.give(bank, m)
        ym[kt] = m

    for g in range(4):
        store = {}
        k.run(k.token_major(("aq", layer, g), qk_piece(g, store, 0), hm))
        k.run(k.token_major(("ak", layer, g), qk_piece(g, store, 1), hm))
        if g == 0:
            k.until(lambda: len(k.biasm) == bias.shape[1] // 4)
        k.run(k.token_major(("av", layer, g), v_piece(g, store), hm))
    for t in k.hslots:
        k.lend(t, k.hread)
    k.start(routing(k, layer))
    k.project_open()
    k.halt()
    for kt in range(6):
        k.until(lambda: kt in ym)
        k.project([(("ao", layer, kt // 2), kt % 2, (k.yh[:, kt, :], k.yl[:, kt, :]), ym[kt])], first=kt == 0)
        k.turn()
    k.halt()
    k.drain()
    k.extend()
    k.yread = k.project([(("ao", layer, 3), kt % 2, (k.yh[:, kt, :], k.yl[:, kt, :]), ym[kt]) for kt in (6, 7)], last=True)
    stage, free = k.stages.free[0]
    spare = [stage[2][:, 512 * i:512 * i + 512] for i in range(4)]
    tmp, k.junk = Turns(spare[0:2], free), Turns(spare[2:4], free)
    k.open_squares()
    k.turned = {}
    xT = k.xT

    def each(t, nh, xs, m):
        k.square(t, nh, xs, m)
        bank, free = psum.take()
        for j in range(4):
            d = k.tr(bank[:, j * 128:j * 128 + 128], xs[:, j * 128:j * 128 + 128], m, free, signal=j == 3)
        copy = k.cp if t == 1 and nh == 1 else k.acp
        k.turned[t, nh] = copy(xT[:, nh * 4:nh * 4 + 4, t * 128:t * 128 + 128], blocks(bank[:, :], 128), d)
        psum.give(bank, k.turned[t, nh])

    k.add_sums(k.gate, tmp, each)
    k.stages.free[0] = (stage, [tmp.marks(), k.junk.marks()])
    k.gread = k.xmarks


def routing(k, layer):
    (gain, gm), (shift, sm) = need(k, layer, 4), need(k, layer, 3)
    need(k, layer, 5)
    rw = k.cst("rw")
    yield k.after(gm, sm, take=[(k.psum, 1)])
    bank, free = k.psum.take()
    for kt in range(8):
        d = k.mm(bank[:, 0:16], shift[:, kt:kt + 1].to_broadcast([128, 128]), rw[:, kt * 16:kt * 16 + 16], kt == 0,
                 kt == 7, sm, free, signal=kt == 7)
    m = k.tt(blocks(k.rwg[:, 0:128], 16), blocks(rw, 16), spread(gain, 8, 16), ALU.mult, gm, k.rread)
    yield k.after(d)
    k.routed = [m, k.cp(k.rshift, bank[:, 0:16], d, k.rread)]
    k.psum.give(bank, k.routed[1])


def mixer_halves(layer):
    keys = [(n, layer, g) for g in range(4) for n in ("aq", "ak", "av")] + [("ao", layer, j) for j in range(4)]
    return [(key, half) for key in keys for half in (0, 1)]


def experts(k, layer, base, out=None):
    at = base

    def room(*shape, dt=F32):
        nonlocal at
        t = k.sb([128, *shape], at, dt)
        at += (int(np.prod(shape)) * 4 + 31) // 32 * 32
        return t

    mul, add, sub, eq = ALU.mult, ALU.add, ALU.subtract, ALU.is_equal
    cst, ones, ident = k.cst, k.cst("ones"), k.ident
    fence = k.fence
    gain, shift = need(k, layer, 4), need(k, layer, 3)
    sg, ac, ac2, aT = (room(512) for _ in range(4))
    rt = room(20, 32)
    pair = room(96)
    GS = room(8)
    M3 = room(2, 48)
    ov = room(16)
    number = k.numbers[layer]
    Pr, lg = room(2, 256), k.sb([128, 256], at - 2048)
    assert at <= base + k.msize, (at - base, k.msize)
    P = [k.sb([128, 2, 256], k.yhat + 2048 * i, F32R) for i in (0, 1)]
    PT = [k.sb([128, 2, 256], k.yhat + 4096 + 2048 * i, F32R) for i in (0, 1)]
    (stage, hgfree), (ystage, yfree), *others = [k.stages.take() for _ in range(4)]
    hg, ylast = stage[2], ystage[2][:, 512:1024]
    for st, free in others:
        k.lend(st[2], free)
    k.lend(k.ylslot, k.yread)
    k.slots.insert(10, ((ystage[2], Count(k.nc, f"ystage{layer}"), "once"), yfree))
    yfree = []
    for lane in (k.dve, k.act, k.pool):
        lane.wait(fence)
    scales = k.scale_steps()
    next(scales)
    lbank, lfree = k.psum.take()
    for nh in (0, 1):
        for t in (0, 1):
            for g in range(4):
                kt = 4 * nh + g
                d = k.mm(lbank[32 * g:32 * g + 32, t * 128:t * 128 + 128], k.rwg[:, kt * 16:kt * 16 + 32],
                         k.xT[:, kt, t * 128:t * 128 + 128], nh == 0 and t == 0, nh == 1, k.routed, k.turned[t, nh], lfree,
                         signal=g == 3)
    hTread = k.rread = d
    m = k.cp(lg[:, :], lbank[:, 0:256], d)
    k.psum.give(lbank, m)
    bank, free = k.psum.take()
    for t in (0, 1):
        d = k.mm(bank[:, t * 16:t * 16 + 16], lg[:, t * 128:t * 128 + 128], cst("fold"), True, True, m, free, signal=t == 1)
    r, rm = finish(scales)
    n = iter(range(20))
    take = lambda w=32: rt[:, next(n), 0:w]
    sc, sel, gates, M, posm = take(), take(), take(), take(), take()
    z, rank, best, gs, first = take(), take(), take(), take(8), take(8)

    def before(out, v, n, m):
        s4, pairs = blocks(v, 4), blocks(pair[:, 0:n * 12], 12)
        for i in (1, 2, 3):
            k.tt(pairs[:, :, 4 * i - 1:12:3], s4[:, :, 0:4 - i], s4[:, :, i:4], ALU.is_ge, m)
            d = k.tt(pairs[:, :, 3 - i:13 - 4 * i:3], s4[:, :, i:4], s4[:, :, 0:4 - i], ALU.is_gt, m)
        return k.red(out, blocks(pair[:, 0:n * 12], 3), add, d)

    for t in (0, 1):
        m = k.stt(z[:, t * 16:t * 16 + 16], bank[:, t * 16:t * 16 + 16], r[:, t:t + 1], k.rshift, mul, add, d, rm)
    k.rread = [hTread, m]
    k.psum.give(bank, m)
    m = k.fn(z, z, ACT.Exp, m, scale=-1.0)
    for _ in gate_rows(k, layer, 5):
        pass
    m = k.ts(z, z, 1.0, add, m)
    m = k.rec(sc, z, m)
    m = k.tt(blocks(sel, 16), blocks(sc, 16), again(cst("rbias"), 2, 16), add, m)
    m = before(rank, sel, 8, m)
    m1 = k.stt(z, rank, 2.0, sel, ALU.is_lt, mul, m)
    bm = k.ts(best, rank, 2.0, ALU.is_lt, m)
    m = k.red(gs, blocks(z, 4), add, m1)
    m = before(first, gs, 2, m)
    Mm = k.stt(blocks(M, 4), spread(first, 8, 4), 1.0, blocks(best, 4), ALU.is_lt, mul, m, bm)
    bank, free = k.psum.take()
    k.mm(bank[:, 0:16], cst("stri"), M[:, 0:16], True, True, Mm, free)
    k.mm(bank[:, 16:32], cst("stri"), M[:, 16:32], True, False)
    d = k.mm(bank[:, 16:32], ones, M[:, 0:16], False, True, signal=True)
    pm, rpm, rpfree = {}, {}, []
    posmm = k.stt(posm, bank[:, 0:32], 1.0, M, add, mul, d)
    k.psum.give(bank, posmm)
    pfree = [k.yread, k.yread]

    def places(q):
        pm[q] = [k.tt(blocks(P[q % 2][:, t, :], 64), again(cst("iota"), 4, 64),
                      spread(posm[:, t * 16 + q * 4:t * 16 + q * 4 + 4], 4, 64), eq, posmm, pfree[q % 2]) for t in (0, 1)]
        src = [P[q % 2][:, t, :].bitcast(F32) for t in (0, 1)]
        rpm[0] = k.acp(Pr[:, 0, :], src[0], pm[q][0], rm, rpfree, scale=r[:, 0:1])
        rpm[1] = k.ts(Pr[:, 1, :], src[1], r[:, 1:2], mul, pm[q][1], rm, rpfree)

    places(0)
    w, ws, wi = take(), take(2), take(2)
    m = k.tt(w, sc, M, mul, Mm)
    m = k.red(ws, blocks(w, 16), add, m)
    m = k.rec(wi, ws, m)
    gm = k.tt(blocks(gates, 16), blocks(w, 16), spread(wi, 2, 16), mul, m)

    hgm = []

    def gather(q, work=()):
        hgm.clear()
        work = iter(work)
        for j in range(4):
            if j > 0:
                next(work, None)
            bank, free = k.psum.take()
            for kk in (0, 1):
                c = slice((2 * j + kk) * 128, (2 * j + kk) * 128 + 128)
                for t in (0, 1):
                    d = k.mm(bank[:, kk * 256:kk * 256 + 256], k.x[:, t, c], Pr[:, t, :], t == 0, t == 1, rpm[t], free,
                             k.xmarks[t], signal=kk == 1 and t == 1)
            for kk in (0, 1):
                kt = 2 * j + kk
                src, g, s = bank[:, kk * 256:kk * 256 + 256], gain[0][:, kt:kt + 1], shift[0][:, kt:kt + 1]
                to = hg[:, kt * 256:kt * 256 + 256]
                if j % 2:
                    m = k.fn(to, src, ACT.Identity, d, hgfree, scale=g, bias=s)
                else:
                    m = k.ts(to, src, g, mul, d, hgfree, s2=s, op1=add)
            k.psum.give(bank, m)
            hgm.append(m)
        rpfree[:] = [d]

    ptm, gsm, nm, ptfree = {}, {}, [], [k.yread, k.yread]
    ind, rank, T8 = ov[0:48, 0:1], ov[0:48, 1:2], ov[0:48, 2:10]

    def slot_rows(q):
        bank, free = k.psum.take()
        bank2, free2 = k.psum.take()
        for i in (0, 1):
            for t in (0, 1):
                o = (i * 2 + t) * 128
                d = k.tr(bank[:, o:o + 128], P[q % 2][:, t, i * 128:i * 128 + 128].bitcast(F32), free, pm[q],
                         signal=i == 1 and t == 1)
        for i in (0, 1):
            for t in (0, 1):
                d2 = k.mm(bank2[:, i * 16:i * 16 + 16], P[q % 2][:, t, i * 128:i * 128 + 128].bitcast(F32),
                          gates[:, t * 16:t * 16 + 16], t == 0, t == 1, gm, free2, signal=i == 1 and t == 1)
        pfree[q % 2] = [d2]
        ptm[q] = k.acp(PT[q % 2][:, :, :], blocks(bank[:, :], 256), d, ptfree[q % 2])
        k.psum.give(bank, ptm[q])
        e = 4 * q
        k.cp(GS[0:64, 2 * q:2 * q + 2], bank2[0:64, e:e + 19:18], d2)
        gsm[q] = k.cp(GS[64:128, 2 * q:2 * q + 2], bank2[64:128, e + 1:e + 20:18], d2)
        k.psum.give(bank2, gsm[q])

    def overflow():
        m = [k.cp(blocks(M3[:, t, :], 16), again(M[:, t * 16:t * 16 + 16], 3, 16), Mm) for t in (0, 1)]
        bank, free = k.psum.take()
        for t in (0, 1):
            d = k.mm(bank[0:48, 0:1], M3[:, t, :], ones[:, 0:1], t == 0, t == 1, m, free, signal=t == 1)
        m = k.tt(ind, bank[0:48, 0:1], cst("cut")[0:48, :], ALU.is_gt, d)
        yield
        d = k.mm(bank[0:48, 1:2], cst("stri")[0:48, 0:48], ind, True, True, m, signal=True)
        m = k.ts(rank, bank[0:48, 1:2], 1.0, add, d)
        m = k.ts(T8, cst("iota")[0:48, 0:8], rank, eq, m, s2=ind, op1=mul)
        yield
        k.mm(bank[0:1, 2:3], ind, ones[0:48, 0:1], True, True, m)
        d = k.mm(bank[0:1, 8:16], cst("where")[0:48, :], T8, True, True, m, signal=True)
        k.cp(number[0:1, 0:1], bank[0:1, 2:3], d)
        nm.append(k.cp(number[0:1, 1:9], bank[0:1, 8:16], d))
        k.psum.give(bank, nm[0])
        yield

    first_piece = len(k.order)
    for p in range(8):
        k.reserve([("mu", layer, 2 * p + j, s) for s in range(4) for j in (0, 1)])
        k.reserve([("md", layer, 2 * p + j, nh) for nh in (0, 1) for j in (0, 1)])
    sgs = Turns([sg], hTread)
    acs = Turns([ac, ac2], hTread)
    aTs = Turns([aT], hTread)
    ys = {}

    def gate_up(p):
        (G, gf), (U, uf) = k.psum.take(), k.psum.take()
        for s in range(4):
            yield
            ws = [k.piece(("mu", layer, 2 * p + j, s)) for j in (0, 1)]
            for kk in (0, 1):
                kt = 2 * s + kk
                for o, free, c in ((G, gf, 0), (U, uf, 512)):
                    for j in (0, 1):
                        w, load, _ = ws[j]
                        a = kt * 256 + ((2 * p + j) % 4) * 64
                        d = k.mm(o[64 * j:64 * j + 64, :], hg[:, a:a + 64], w[:, kk * 1024 + c:kk * 1024 + c + 512],
                                 kt == 0, kt == 7, load, free, hgm[kt // 2], signal=kk == 1 and c == 512 and j == 1)
            for j in (0, 1):
                k.piece_done(ws[j][2], d)
        hgfree[:] = [d]
        t1, f = sgs.take()
        a = k.fn(t1[:, :], G[:, :], ACT.Silu, d, f)
        k.psum.give(G, a)
        t2, f = acs.take()
        m = k.tt(t2[:, :], t1[:, :], U[:, :], mul, a, f, d)
        k.psum.give(U, m)
        sgs.give(t1, m)
        ys[p] = (t2, m)

    def turn(p):
        t2, m = ys[p]
        bank, free = k.psum.take()
        for c in range(4):
            d = k.tr(bank[:, c * 128:c * 128 + 128], t2[:, c * 128:c * 128 + 128], m, free, signal=c == 3)
        acs.give(t2, d)
        t3, f = (aTs if p < 7 else sgs).take()
        am = k.acp(t3[:, :], bank[:, :], d, f)
        k.psum.give(bank, am)
        ys[p] = (t3, am)

    def down(p):
        t3, am = ys[p]
        made = ys[p] = {}
        ds = [k.psum.take() for _ in (0, 1)]
        done = [None, None]

        def rows(nh, ws, cs):
            for c in cs:
                for j in (0, 1):
                    w, load, _ = ws[j]
                    load = load[c // 2] if p == 7 else load
                    d = k.mm(ds[nh][0][64 * j:64 * j + 64, :], t3[:, c * 128 + 64 * j:c * 128 + 64 * j + 64],
                             w[:, c * 512:c * 512 + 512], c == 0, c == 3, load, am, ds[nh][1], signal=c == 3 and j == 1)
            if c == 3:
                done[nh] = d
                for j in (0, 1):
                    k.piece_done(ws[j][2], d)

        def row(nh):
            s = slice(nh * 512, nh * 512 + 512)
            f, free = acs.take()
            m = k.tt(f[:, :], ds[nh][0][:, :], k.gate[0][:, s], mul, done[nh], k.gate[1], free)
            k.psum.give(ds[nh][0], m)
            a = k.acp(ystage[0][:, s], f[:, :], m, yfree, gsm[p // 2], scale=GS[:, p:p + 1])
            made[nh] = k.stt(ystage[1][:, s], f[:, :], GS[:, p:p + 1], ystage[0][:, s].bitcast(F32), mul, sub, a, yfree)
            acs.give(f, made[nh])

        pieces = [[("md", layer, 2 * p + j, nh) for j in (0, 1)] for nh in (0, 1)]
        if p < 7:
            for nh in (0, 1):
                rows(nh, [k.piece(key) for key in pieces[nh]], range(4))
            if p == 0:
                yfree[:] = k.once
            for nh in (0, 1):
                row(nh)
        else:
            ws = [k.split_pieces(keys) for keys in pieces]
            rows(0, ws[0], (0, 1))
            scatter(6, (0,))
            rows(0, ws[0], (2, 3))
            scatter(6, (1,))
            row(0)
            rows(1, ws[1], (0, 1))
            scatter(7, (0,), (0,))
            rows(1, ws[1], (2, 3))
            made[1] = k.stt(ylast[:, :], ds[1][0][:, :], GS[:, p:p + 1], k.gate[0][:, 512:1024], mul, mul, done[1],
                            k.gate[1], yfree, gsm[3])
            k.psum.give(ds[1][0], made[1])
            scatter(7, (0,), (1,))
            scatter(7, (1,))
        (aTs if p < 7 else sgs).give(t3, done[1])

    def scatter(p, halves=(0, 1), tiles=(0, 1)):
        made = ys[p]
        for nh in halves:
            for t in tiles:
                bank, free = k.sums[t * 2 + nh]
                rows = PT[p // 2 % 2][:, p % 2, t * 128:t * 128 + 128]
                s = slice(nh * 512, nh * 512 + 512)
                if p == 7 and nh == 1:
                    d = k.mm(bank[:, :], rows.bitcast(F32), ylast[:, :], False, True, made[nh], signal=True)
                    k.sumsm[t * 2 + nh] = d
                    continue
                for i, part in enumerate(ystage[0:2]):
                    d = k.mm(bank[:, :], rows, part[:, s], p == 0 and i == 0, p == 7 and i == 1, made[nh], ptm[p // 2], free,
                             signal=i == 1 and (t == 1 or p == 7))
                if p == 7:
                    k.sumsm[t * 2 + nh] = d
        yfree[:] = [d]
        ptfree[p // 2 % 2] = [d]

    more = overflow()
    steps = gate_up(0)
    gather(0, steps)
    next(more)
    next(steps)
    next(more)
    next(more)
    next(steps, None)
    slot_rows(0)
    for p in range(8):
        if p == 1:
            k.project_open()
        if p % 2 == 1 and p < 7:
            gather(p // 2 + 1)
            scatter(p - 1)
            slot_rows(p // 2 + 1)
        if p == 6:
            k.retiring = True
        if p < 7:
            steps = gate_up(p + 1)
            for _ in range(3):
                next(steps)
            turn(p)
            next(steps)
            if p % 2 == 0 and p < 6:
                places(p // 2 + 1)
            next(steps, None)
        if p in (2, 4, 6):
            scatter(p - 1)
        if p == 6:
            turn(7)
        down(p)
    d = k.sumsm[3]
    k.retire()
    k.hread = k.yread = [d, k.retired]

    assert len(k.order) == first_piece + 96
    lanes = (k.pe, k.act, k.dve, k.sp)
    counts = [Count(k.nc, f"more{layer}{i}") for i in range(4)]
    loads = [Count(k.nc, f"moreload{layer}{i}") for i in range(2)]
    wfree, space = [[d], [d]], [hg, ystage[2]]
    at = base + k.msize
    Pu, PTu, tab, pu, gu, gsu, hu, yu = (room(n) for n in (128, 256, 32, 32, 32, 32, 512, 1024))
    Pu = Pu[:, :].rearrange("p (t s) -> p t s", t=2)
    tail = [d, nm, k.retired, list(gsm.values()), [t.marks() for t in (acs, aTs, sgs, k.psum)]]
    b0, b1, b2, b3 = [b for b, _ in k.psum.free][0:4]
    lists = [[] for _ in lanes]
    for u in range(EXTRA):
        for lane, count in zip(lanes, counts):
            lane.open(count)
        d = k.mm(b0[:, 0:17], T8[:, u:u + 1].to_broadcast([48, 128]), cst("unit")[0:48, :], True, True, tail, signal=True)
        m = k.cp(tab[:, 0:17], b0[:, 0:17], d, tail)
        for src, res in ((posm, pu), (gates, gu)):
            q = k.tt(blocks(yu[:, 0:32], 16), blocks(src, 16), again(tab[:, 0:16], 2, 16), mul, m, gm, posmm)
            m = k.red(res[:, 0:2], blocks(yu[:, 0:32], 16), add, q)
        m = k.ts(pu[:, 0:2], pu[:, 0:2], tab[:, 16:17], sub, m)
        pum = k.tt(Pu[:, :, :], again(cst("iota"), 2, 64), spread(pu[:, 0:2], 2, 64), eq, m)
        prum = [k.ts(Pr[:, t, 0:64], Pu[:, t, :], r[:, t:t + 1], mul, pum, tail) for t in (0, 1)]
        for kt in range(8):
            for t in (0, 1):
                d = k.mm(b1[:, kt * 64:kt * 64 + 64], k.x[:, t, kt * 128:kt * 128 + 128], Pr[:, t, 0:64], t == 0, t == 1,
                         prum[t], signal=kt == 7 and t == 1)
        for t in (0, 1):
            k.tr(b2[0:64, t * 128:t * 128 + 128], Pu[:, t, :])
        for t in (0, 1):
            d = k.mm(b2[0:64, 256:257], Pu[:, t, :], gu[:, t:t + 1], t == 0, t == 1, signal=t == 1)
        m = k.tt(blocks(hu[:, :], 64), blocks(b1[:, :], 64), spread(gain[0], 8, 64), mul, d)
        hum = k.tt(blocks(hu[:, :], 64), blocks(hu[:, :], 64), spread(shift[0], 8, 64), add, m)
        k.cp(PTu[0:64, :], b2[0:64, 0:256], d)
        ptum = k.cp(gsu[0:64, 0:1], b2[0:64, 256:257], d)
        for s in range(6):
            slot = s % 2

            def fetch(e, s=s, u=u, slot=slot):
                i = e.value_load(number[0:1, 1 + u:2 + u], min_val=0, max_val=85)
                src = k.weights[bass.ds(i + (first_piece + 2 * s), 1), :, :].rearrange("a p n -> p (a n)")
                return e.dma_start(space[slot][:, :], src)

            lm = k.sp.dma(fetch, loads[slot], tail, wfree[slot], size=1 << 20)
            if s < 4:
                for kk in (0, 1):
                    kt = 2 * s + kk
                    for o, c in ((b0, 0), (b3, 512)):
                        d = k.mm(o[0:64, :], hu[:, kt * 64:kt * 64 + 64], space[slot][:, kk * 1024 + c:kk * 1024 + c + 512],
                                 kt == 0, kt == 7, lm, hum, signal=kk == 1 and c == 512)
                if s == 3:
                    a = k.fn(sg[0:64, :], b0[0:64, :], ACT.Silu, d)
                    m = k.tt(ac[0:64, :], sg[0:64, :], b3[0:64, :], mul, a)
                    for c in range(4):
                        t4 = k.tr(b1[:, c * 64:c * 64 + 64], ac[0:64, c * 128:c * 128 + 128], m, signal=c == 3, rows=64)
                    atm = k.cp(aT[:, 0:256], b1[:, 0:256], t4)
            else:
                o = (b0, b3)[s - 4]
                for c in range(4):
                    d = k.mm(o[0:64, :], aT[:, c * 64:c * 64 + 64], space[slot][:, c * 512:c * 512 + 512], c == 0, c == 3,
                             lm, atm, signal=c == 3)
            wfree[slot] = [d]
        for nh, o in ((0, b0), (1, b3)):
            m = k.stt(yu[0:64, nh * 512:nh * 512 + 512], o[0:64, :], gsu[0:64, 0:1],
                      k.gate[0][0:64, nh * 512:nh * 512 + 512], mul, mul, d, ptum, k.gate[1])
        for t in (0, 1):
            for nh in (0, 1):
                bank, _ = k.sums[t * 2 + nh]
                d = k.mm(bank[:, :], PTu[0:64, t * 128:t * 128 + 128], yu[0:64, nh * 512:nh * 512 + 512], False, True, m,
                         signal=t == 1 and nh == 1)
        tail = [d]
        for lane in lanes:
            lane.wait(d)
        for i, lane in enumerate(lanes):
            lists[i].append(lane.close())
    for lane, inner in zip(lanes, lists):
        lane.wait(nm)
        lane.branch(number[0:1, 0:1], inner)
    k.stages.give(stage, k.marks())
    k.stages.give(ystage, k.marks())
    for st, _ in others:
        k.stages.give(st, k.retired)
    k.gread = k.marks()
    k.open_squares()
    k.junk = acs
    k.add_sums(None, None, out or k.square, ((0, 0), (1, 0), (0, 1), (1, 1)))


def setup(k, io, at):
    nc = k.nc
    yield k.after(k.cm)
    k.csrm = k.fn(k.csr[:, :], k.csr[:, :], ACT.Silu, k.cm)
    k.back, k.backing = [modulation(k), 0.0], True
    yield k.after(take=[(k.psum, 1)])
    bank, free = k.psum.take()
    d = k.mm(bank[0:8, :], k.cst("t5")[0:32, :], k.cst("hot")[0:32, :], True, True, k.morem, free, signal=True)
    t5 = k.sb([8, 512], at)
    yield k.after(d)
    a = k.acp(t5[:, :], bank[0:8, :], d)
    k.psum.give(bank, a)
    count = Count(nc, "t5")
    dst = io["scratch"]
    k.t5m = k.act.dma(lambda e: e.dma_start(dst, t5[:, :]), count, a, size=1 << 14)


def lambdas(k):
    mul, add = ALU.mult, ALU.add
    k.subln, k.neglam = k.keep(1), k.keep(1)
    k.sublnm = k.ts(k.subln, k.cst("subln"), 1.0 - LAMBDA_INIT, mul, k.lastm)
    lam = k.cst("lam")
    junk, s, e, l = k.sb([128, 64], k.gbufat + 3072)[:, :], k.col(2), k.col(2), k.col(1)
    m = k.ttr(junk, lam[:, 0:64], lam[:, 64:128], mul, add, 0.0, s[:, 0:1], k.morem)
    m = k.ttr(junk, lam[:, 128:192], lam[:, 192:256], mul, add, 0.0, s[:, 1:2], m)
    yield k.after(m)
    m = k.fn(e, s, ACT.Exp, m)
    yield k.after(m)
    m = k.tt(l, e[:, 1:2], e[:, 0:1], ALU.subtract, m)
    k.neglamm = k.ts(k.neglam, l, -LAMBDA_INIT, add, m)


def build(nc, io):
    k = Core(nc)
    k.weights, k.lnf = io["weights"], io["lnf"]
    at = BASE

    def place(size):
        nonlocal at
        a, at = at, at + (size + 31) // 32 * 32
        return a

    k.x = k.sb([128, 2, 1024], place(8192))
    k.cstt = k.sb([128, NLAST], place(NLAST * 4))
    k.cols = k.sb([128, ZONES], place(ZONES * 4))
    k.zone(KEPT, ZONE_A)
    k.rwg, k.rread = k.sb([128, 144], place(576)), []
    k.rshift = k.rwg[:, 128:144]
    k.numbers = [k.sb([1, 16], place(64), I32) for _ in (0, 1)]
    k.newton = Turns([k.sb([128, 32], place(128)) for _ in range(8)])
    k.diag, k.dread = k.sb([128, 2, 128], place(1024)), []
    k.hhat, k.hlat, k.yhat, k.ylat = (place(8192) for _ in range(4))
    k.hh, k.hl, k.yh, k.yl = (k.sb([128, 8, 256], a, F32R) for a in (k.hhat, k.hlat, k.yhat, k.ylat))
    stages = []
    for _ in range(4):
        a = place(8192)
        stages.append((k.sb([128, 1024], a, F32R), k.sb([128, 1024], a + 4096, F32R), k.sb([128, 2048], a)))
    k.stages = Turns(stages)
    k.csr = k.sb([128, 1024], place(4096))
    k.gbufat = place(4096)
    k.gbuf, k.gread = k.sb([128, 1024], k.gbufat), []
    local = at
    ring = LIMIT - 8 * PIECE
    more = ring - 5 * PIECE
    k.f2size, k.asize, k.msize = 24576, ring - 16384 - local, more - local
    bias = [k.sb([128, 8, 256], ring - 8192), k.sb([128, 16, 256], ring - 16384)]
    k.bias = bias
    windows = Turns([(k.sb([128, 4, 256], local + 24576 + 4096 * i), Count(nc, f"window{i}")) for i in range(3)])
    k.xT = k.sb([128, 8, 256], local)
    for i in range(3, 8):
        k.add_slot(ring + i * PIECE)
    grown = iter(range(3))

    def grow(n):
        marks = k.marks()
        for _ in range(n):
            k.add_slot(ring + next(grown) * PIECE, marks)

    k.grow = grow

    def first_constants(a):
        start = ring + 3 * PIECE - (NCST - NLAST) * 4 // 32 * 32 - 32
        assert a <= start
        a = start
        k.cstf = k.sb([128, NCST - NLAST], a)
        k.cmark = constant(k.cstf, NLAST, NLAST, NSOON)

    def more_constants():
        k.morem = constant(k.cstf, NLAST, NSOON, NCST)
        count, src = Count(nc, "c"), io["c"]
        k.cm = k.sp.dma(lambda e: e.dma_start(k.csr[:, :], src), count, size=1 << 19)

    k.first_constants, k.more_constants = first_constants, more_constants

    k.ident = k.cst("ident")
    counts = [Count(nc, n) for n in ("x0", "x1")]
    xin, cin = io["x"], io["cst"]

    def constant(t, start, a, b):
        count = Count(nc, f"cst{a}")
        return k.sp.dma(lambda e: e.dma_start(t[:, a - start:b - start], cin[:, a:b]), count, size=(b - a) * 512)

    k.xmarks = []
    k.oncem = constant(k.cstt, 0, 0, NONCE)
    for t in (0, 1):
        m = k.sp.dma(lambda e, t=t: e.dma_start(k.x[:, t, :], xin[:, t, :]), counts[t], size=1 << 19)
        k.xmarks.append([m, m])
    k.mod = {}
    k.feed(first_halves())
    k.opened["k", 0] = k.piece(("k", 0))
    k.lastm = constant(k.cstt, 0, NONCE, NLAST)
    k.opened["q", 0] = k.piece(("q", 0))
    k.setup, k.lambdas = lambda at: setup(k, io, at), lambda: lambdas(k)

    k.hslots = [k.sb([128, 2048], a) for a in (k.hhat, k.hlat)]
    k.ylslot = k.sb([128, 2048], k.ylat)
    regions = [k.sb([128, 2048], more + i * PIECE) for i in range(5)]

    def extend():
        for t in regions:
            k.lend(t, k.marks())

    k.extend = extend
    first_mixer(k, local)
    k.pace("first ffn")
    k.fence = k.gread = k.marks()
    k.feed(mixer_halves(0))
    k.start(load_bias(k, k.act, bias[0], windows, io["scratch"], 512, 128, k.t5m, k.fence))
    first_ffn(k, local)
    for layer in (0, 1):
        k.fence = k.marks()
        if layer == 0:
            ffn = k.fence
            k.zone(ZONE_A, ZONES)
        k.backing = True
        k.pace(f"mixer {layer}")
        second_mixer(k, layer, local, windows)
        k.halt()
        k.fence = k.marks()
        if layer == 0:
            mixed = k.fence
            k.zone(KEPT, ZONE_A, ffn)
        else:
            k.zone(ZONE_A, ZONES, mixed)
        experts(k, layer, local, None if layer == 0 else writer(k, io))
        if layer == 0:
            k.feed(mixer_halves(1))
            for key in ("aq", "ak", "av"):
                k.opened[key, 1, 0] = k.piece((key, 1, 0))
            marks = [k.retired, k.marks()]
            windows = Turns([w for w, _ in windows.free], marks)
            load = load_bias(k, k.sp, bias[1], windows, io["rel"], 513, 129, None, marks)
            for _ in range(4):
                step = next(load)
            k.live.append([load, *step])
    return end(k, io)


def writer(k, io):
    count = Count(k.nc, "out")

    def write(t, nh, xs, m):
        dst = io["out"][:, t, nh * 512:nh * 512 + 512]
        k.written = k.sp.dma(lambda e: e.dma_start(dst, xs), count, m, size=1 << 18)

    return write


def end(k, io):
    if k.written is None:
        write = writer(k, io)
        for t in (0, 1):
            for nh in (0, 1):
                write(t, nh, k.x[:, t, nh * 512:nh * 512 + 512], k.xmarks[t][nh])
    k.sp.wait(k.t5m, k.written)
    assert not k.live
    with k.nc.Block() as block:
        @block.sync
        def _(e):
            k.sp.emit(e)

        @block.gpsimd
        def _(e):
            k.pool.emit(e)

        @block.scalar
        def _(e):
            k.act.emit(e)

        @block.vector
        def _(e):
            k.dve.emit(e)

        @block.tensor
        def _(e):
            k.pe.emit(e)
    return k.order




def _columns(w, a):
    return w[:, a:a + 256].reshape(8, 128, 2, 128).transpose(1, 2, 0, 3).reshape(128, 2048)


def _block(w, a):
    return w[:, a:a + 256].reshape(8, 128, 256).transpose(1, 0, 2).reshape(128, 2048)


def _chunk(w, c):
    return w[:, c * 128:c * 128 + 128].reshape(8, 128, 128).transpose(1, 0, 2).reshape(128, 1024)


def _rows(w, j):
    return w[j * 256:j * 256 + 256].reshape(2, 128, 1024).transpose(1, 0, 2).reshape(128, 2048)


def _piece(key, inp):
    name, n = key[0], key[1]
    w_in = inp["w_in"][0]
    if name in ("q", "k", "v"):
        return _columns(w_in, "qkv".index(name) * 512 + 256 * n)
    if name == "z":
        return _block(w_in, 1536 + 256 * n)
    if name == "qb":
        return _columns(w_in, 2056 + 256 * n)
    if name == "kb":
        return _columns(w_in, 2568 + 256 * n)
    if name == "vb":
        return _block(w_in, 3080 + 256 * n)
    if name == "wo":
        return _rows(inp["w_out"][0], n)
    if name == "gu":
        return np.concatenate([_chunk(inp["w_gate"][0], n), _chunk(inp["w_up"][0], n)], 1)
    if name == "wd":
        return _rows(inp["w_down"][0], n)
    if name in ("aq", "ak", "av"):
        w = inp["a_w_qkv_2"][0] if n == 0 else inp["b_w_qkv_2"][0]
        return _block(w, ("aq", "ak", "av").index(name) * 1024 + 256 * key[2])
    if name == "ao":
        return _rows(inp["a_w_o_2"][0] if n == 0 else inp["b_w_o_2"][0], key[2])
    if name == "ada":
        w = inp["ada_w_2"][n][:, key[2] * 1024 + key[3] * 256:key[2] * 1024 + key[3] * 256 + 256]
        return w.T.reshape(2, 128, 1024).transpose(1, 0, 2).reshape(128, 2048)
    if name == "mu":
        g, u = (inp[f"moe_w_{s}_2"][n, key[2]][key[3] * 256:key[3] * 256 + 256].reshape(2, 128, 512) for s in ("gate", "up"))
        return np.concatenate([g, u], 2).transpose(1, 0, 2).reshape(128, 2048)
    assert name == "md"
    w = inp["moe_w_down_2"][n, key[2]][:, key[3] * 512:key[3] * 512 + 512]
    return w.reshape(4, 128, 512).transpose(1, 0, 2).reshape(128, 2048)


def _params(inp):
    def cols(v, n):
        return v.reshape(n, 128).T

    def wide(v):
        return np.broadcast_to(v.reshape(1, -1), (128, v.size))

    def twice(v):
        return np.tile(v.reshape(64), 2)[:, None]

    out = dict(constants())
    out["ln1"], out["ln2"] = cols(inp["ln1"], 8), cols(inp["ln2"], 8)
    out["lnf"] = cols(inp["ln_f"], 8)
    out["conv"] = inp["conv_qkv"][0].reshape(4, 12, 128).transpose(2, 1, 0).reshape(128, 48)
    out["fconv"] = inp["ffn_conv"][0].reshape(3, 22, 128).transpose(2, 1, 0).reshape(128, 66)
    out["alog"], out["dtb"], out["gain"] = wide(inp["a_log"]), wide(inp["dt_bias"]), wide(inp["gdn_norm"])
    out["wba"] = inp["w_in"][0][:, 2048:2056].reshape(8, 128, 8).transpose(1, 0, 2).reshape(128, 64)
    out["nmix"], out["nffn"] = cols(inp["norm_mix_g_2"], 16), cols(inp["norm_ffn_g_2"], 16)
    out["qk"] = np.concatenate([twice(inp[n]) for n in ("a_q_gain_2", "a_k_gain_2", "b_q_gain_2", "b_k_gain_2")], 1)
    out["subln"] = inp["a_subln_g_2"].reshape(128, 1)
    out["lam"] = wide(inp["a_lambda_2"])
    out["rw"] = inp["router_w_2"].reshape(8, 128, 16).transpose(1, 0, 2).reshape(128, 128)
    out["rbias"] = wide(inp["router_bias_2"])
    out["adab"] = cols(inp["ada_b_2"], 96)
    out["t5"] = np.concatenate([inp["t5_bias_2"], np.zeros((96, 8), np.float32)], 0)
    return np.concatenate([out[name] for name in PLACE], 1)


def kernel(**inputs):
    import numpy as _np
    import concourse.bacc as _bacc
    from concourse import mybir as _mybir
    from concourse.bass_utils import run_bass_kernel_spmd as _run

    inp = {k: _np.asarray(v) for k, v in inputs.items()}
    arrays = {
        "x": inp["x"][0],
        "cst": _params(inp),
        "lnf": _np.broadcast_to(inp["ln_f"], (128, 1024)),
        "rel": inp["b_rel_bias_2"][0][:, ::-1],
        "c": _np.broadcast_to(inp["c_2"], (128, 1024)),
    }
    nc = _bacc.Bacc("TRN2", target_bir_lowering=False, num_devices=1)
    io = {}
    shapes = {name: list(a.shape) for name, a in arrays.items()}
    shapes["weights"] = [PIECES, 128, 2048]
    for name, shape in shapes.items():
        io[name] = nc.dram_tensor(f"in_{name}_dram", shape, _mybir.dt.float32, kind="ExternalInput").ap()
    io["scratch"] = nc.dram_tensor("scratch", [8, 512], _mybir.dt.float32, kind="Internal").ap()
    out = nc.dram_tensor("out_0_dram", [256, 1024], _mybir.dt.float32, kind="ExternalOutput").ap()
    io["x"] = io["x"].rearrange("(t p) d -> p t d", p=128)
    io["out"] = out.rearrange("(t p) d -> p t d", p=128)
    order = build(nc, io)
    arrays["weights"] = _np.stack([_piece(key, inp) for key in order])
    arrays = {f"in_{name}_dram": _np.ascontiguousarray(a) for name, a in arrays.items()}
    r = _run(nc, [arrays], core_ids=[0])
    return r.results[0]["out_0_dram"].reshape(1, 256, 1024)
```
